# Optimizing a Trainium2 kernel written in Bass

```python
import math
import jax, jax.numpy as jnp
from jax import lax
import numpy as np

D_MODEL = 1024
BATCH = 1
SEQ = 1024
DEPTH = 1
DEC_BATCH = 8
DEC_SEQ = 8
PAST_LEN = 4096
PAGE_SIZE = 128

D_MIX = D_MODEL
D_A = D_MIX // 2
H_A = 4
DK_A = D_A // H_A
DV_A = D_A // H_A
D_B = D_MIX - D_A
H_B = 4
DH_B = D_B // (2 * H_B)
DV_B = 2 * DH_B
N_BUCKETS = 32
MAX_EXACT = N_BUCKETS // 2
MAX_DIST = 1024
CHUNK = 64
Q_BLOCK = 128
EPS = 1e-6

kernel_name = 'hymba_hgrn2_diffattn_adaln_step'

def rms_norm(x, w):
    xf = x.astype(jnp.float32)
    return xf * lax.rsqrt(jnp.mean(xf * xf, axis=-1, keepdims=True) + EPS) * w.astype(jnp.float32)

def t5_bucket(dist):
    d = jnp.maximum(dist, 0)
    large = MAX_EXACT + (jnp.log(jnp.maximum(d, 1).astype(jnp.float32) / MAX_EXACT)
                         / math.log(MAX_DIST / MAX_EXACT) * (N_BUCKETS - MAX_EXACT)).astype(jnp.int32)
    large = jnp.minimum(large, N_BUCKETS - 1)
    return jnp.where(d < MAX_EXACT, d, large)

def hgrn2_chunked(q, k, v, logf, S0):
    B, L, H, K = q.shape
    V = v.shape[-1]
    C = CHUNK if L % CHUNK == 0 else L
    n = L // C

    def blocks(a):
        return jnp.moveaxis(a.reshape(B, n, C, H, a.shape[-1]), 1, 0)

    tril = jnp.tril(jnp.ones((C, C), dtype=bool))[None, :, :, None, None]

    def step(S, inp):
        qc, kc, vc, lfc = inp
        b = jnp.cumsum(lfc, axis=1)
        o_inter = jnp.einsum('bthk,bhkv->bthv', qc * jnp.exp(b), S)
        diff = b[:, :, None] - b[:, None]
        decay = jnp.where(tril, jnp.exp(jnp.where(tril, diff, 0.0)), 0.0)
        att = jnp.einsum('btjhk,bjhk->bhtj', qc[:, :, None] * decay, kc)
        o_intra = jnp.einsum('bhtj,bjhv->bthv', att, vc)
        b_last = b[:, -1]
        S_new = jnp.exp(b_last)[..., None] * S + jnp.einsum(
            'bjhk,bjhv->bhkv', kc * jnp.exp(b_last[:, None] - b), vc)
        return S_new, o_inter + o_intra

    S_fin, o = lax.scan(step, S0, (blocks(q), blocks(k), blocks(v), blocks(logf)))
    o = jnp.moveaxis(o, 0, 1).reshape(B, L, H, V)
    return o, S_fin

def diff_attention(q, k, v, q_pos, k_pos, rel_table, lam):
    B, Lq = q.shape[:2]
    scale = DH_B ** -0.5

    def block(args):
        qb, qp = args
        s = jnp.einsum('bqhcd,bkhcd->bchqk', qb, k) * scale
        bias = jnp.moveaxis(rel_table.astype(jnp.float32)[t5_bucket(qp[:, None] - k_pos[None, :])], -1, 0)
        causal = qp[:, None] >= k_pos[None, :]
        s = jnp.where(causal, s.astype(jnp.float32) + bias, -jnp.inf)
        p = jax.nn.softmax(s, axis=-1)
        a = p[:, 0] - lam * p[:, 1]
        return jnp.einsum('bhqk,bkhe->bqhe', a, v)

    if Lq > Q_BLOCK and Lq % Q_BLOCK == 0:
        nb = Lq // Q_BLOCK
        qs = jnp.moveaxis(q.reshape(B, nb, Q_BLOCK, *q.shape[2:]), 1, 0)
        ps = q_pos.reshape(nb, Q_BLOCK)
        o = lax.map(block, (qs, ps))
        return jnp.moveaxis(o, 0, 1).reshape(B, Lq, *o.shape[3:])
    return block((q, q_pos))

def mixer_layer(x, c, S0, past_k, past_v, norm_w, w_ada, b_ada, w_in, w_out, lb,
                hg_norm_w, q_norm_w, k_norm_w, lam_q1, lam_k1, lam_q2, lam_k2,
                sub_norm_w, rel_table, lambda_init):
    f32 = jnp.float32
    B, L, _ = x.shape
    mod = jax.nn.silu(c.astype(f32)) @ w_ada.astype(f32) + b_ada.astype(f32)
    shift, scale, gate = jnp.split(mod, 3, axis=-1)
    h = rms_norm(x, norm_w) * (1.0 + scale[:, None]) + shift[:, None]
    proj = (h.astype(x.dtype) @ w_in).astype(f32)
    splits = [int(s) for s in np.cumsum([D_A] * 5 + [D_B] * 4)[:-1]]
    qa, fa, ia, ga, za, qb, kb, vb, zb = jnp.split(proj, splits, axis=-1)

    lb = lb.astype(f32).reshape(H_A, DK_A)
    fa = fa.reshape(B, L, H_A, DK_A)
    logf = jnp.log(lb + (1.0 - lb) * jax.nn.sigmoid(fa))
    k_in = (1.0 - lb) * jax.nn.sigmoid(-fa)
    o_a, S_fin = hgrn2_chunked(qa.reshape(B, L, H_A, DK_A) * DK_A ** -0.5, k_in,
                               ia.reshape(B, L, H_A, DV_A), logf, S0.astype(f32))
    o_a = rms_norm(o_a * jax.nn.sigmoid(ga.reshape(B, L, H_A, DV_A)), hg_norm_w)
    y_a = o_a.reshape(B, L, D_A) * jax.nn.silu(za)

    q = rms_norm(qb.reshape(B, L, H_B, 2, DH_B), q_norm_w)
    k = rms_norm(kb.reshape(B, L, H_B, 2, DH_B), k_norm_w)
    v = vb.reshape(B, L, H_B, DV_B)
    if past_k is None:
        k_all, v_all, pos0 = k, v, 0
    else:
        pos0 = past_k.shape[1]
        k_all = jnp.concatenate([past_k.astype(f32).reshape(B, pos0, H_B, 2, DH_B), k], axis=1)
        v_all = jnp.concatenate([past_v.astype(f32), v], axis=1)
    q_pos = pos0 + jnp.arange(L, dtype=jnp.int32)
    k_pos = jnp.arange(k_all.shape[1], dtype=jnp.int32)
    lam = (jnp.exp(jnp.sum(lam_q1.astype(f32) * lam_k1.astype(f32)))
           - jnp.exp(jnp.sum(lam_q2.astype(f32) * lam_k2.astype(f32))) + lambda_init)
    o_b = diff_attention(q, k_all, v_all, q_pos, k_pos, rel_table, lam)
    o_b = rms_norm(o_b, sub_norm_w) * (1.0 - lambda_init)
    y_b = o_b.reshape(B, L, D_B) * jax.nn.silu(zb)

    out = (jnp.concatenate([y_a, y_b], axis=-1).astype(x.dtype) @ w_out).astype(f32)
    x_new = (x.astype(f32) + gate[:, None] * out).astype(x.dtype)
    return (x_new, k.reshape(B, L, H_B, DV_B).astype(x.dtype), v.astype(x.dtype),
            S_fin.astype(x.dtype))

def setup_inputs(seed: int = 0) -> dict:
    key = jax.random.key(seed)
    ks = jax.random.split(key, 24)
    n_pages = PAST_LEN // PAGE_SIZE
    n_used = DEC_BATCH * n_pages
    n_pool = -(-5 * n_used // 4)
    d_in = 5 * D_A + 4 * D_B
    nrm = jax.random.normal
    page_table = jax.random.permutation(ks[0], n_pool)[:n_used].reshape(DEC_BATCH, n_pages).astype(jnp.int32)
    return {
        'x_prompt': nrm(ks[1], (BATCH, SEQ, D_MODEL), jnp.float32),
        'x_sample': nrm(ks[2], (DEC_BATCH, DEC_SEQ, D_MODEL), jnp.float32),
        'c_prompt': nrm(ks[3], (BATCH, D_MODEL), jnp.float32),
        'c_sample': nrm(ks[4], (DEC_BATCH, D_MODEL), jnp.float32),
        'cache_k': nrm(ks[5], (DEPTH, n_pool, PAGE_SIZE, H_B, DV_B), jnp.float32),
        'cache_v': nrm(ks[6], (DEPTH, n_pool, PAGE_SIZE, H_B, DV_B), jnp.float32),
        'state_hgrn': 0.3 * nrm(ks[7], (DEPTH, DEC_BATCH, H_A, DK_A, DV_A), jnp.float32),
        'page_table': page_table,
        'norm_w': 1.0 + 0.02 * nrm(ks[8], (DEPTH, D_MODEL), jnp.float32),
        'w_ada': 0.5 * D_MODEL ** -0.5 * nrm(ks[9], (DEPTH, D_MODEL, 3 * D_MODEL), jnp.float32),
        'b_ada': 0.1 * nrm(ks[10], (DEPTH, 3 * D_MODEL), jnp.float32),
        'w_in': D_MODEL ** -0.5 * nrm(ks[11], (DEPTH, D_MODEL, d_in), jnp.float32),
        'w_out': D_MIX ** -0.5 * nrm(ks[12], (DEPTH, D_MIX, D_MODEL), jnp.float32),
        'lb_param': 0.5 * nrm(ks[13], (DEPTH + 1, D_A), jnp.float32),
        'hg_norm_w': 1.0 + 0.02 * nrm(ks[14], (DEPTH, DV_A), jnp.float32),
        'q_norm_w': 1.0 + 0.02 * nrm(ks[15], (DEPTH, DH_B), jnp.float32),
        'k_norm_w': 1.0 + 0.02 * nrm(ks[16], (DEPTH, DH_B), jnp.float32),
        'lam_q1': 0.1 * nrm(ks[17], (DEPTH, DH_B), jnp.float32),
        'lam_k1': 0.1 * nrm(ks[18], (DEPTH, DH_B), jnp.float32),
        'lam_q2': 0.1 * nrm(ks[19], (DEPTH, DH_B), jnp.float32),
        'lam_k2': 0.1 * nrm(ks[20], (DEPTH, DH_B), jnp.float32),
        'sub_norm_w': 1.0 + 0.02 * nrm(ks[21], (DEPTH, DV_B), jnp.float32),
        'rel_table': 0.5 * nrm(ks[22], (N_BUCKETS, H_B), jnp.float32),
    }

def reference(x_prompt, x_sample, c_prompt, c_sample, cache_k, cache_v, state_hgrn, page_table,
              norm_w, w_ada, b_ada, w_in, w_out, lb_param, hg_norm_w, q_norm_w, k_norm_w,
              lam_q1, lam_k1, lam_q2, lam_k2, sub_norm_w, rel_table):
    lb_all = jnp.cumsum(jax.nn.softmax(lb_param.astype(jnp.float32), axis=0), axis=0)
    dec_b = x_sample.shape[0]
    yp, ys = x_prompt, x_sample
    kp_l, vp_l, sp_l, ksm_l, vsm_l, ssm_l = [], [], [], [], [], []
    for l in range(DEPTH):
        lambda_init = 0.8 - 0.6 * math.exp(-0.3 * l)
        wl = (norm_w[l], w_ada[l], b_ada[l], w_in[l], w_out[l], lb_all[l], hg_norm_w[l],
              q_norm_w[l], k_norm_w[l], lam_q1[l], lam_k1[l], lam_q2[l], lam_k2[l],
              sub_norm_w[l], rel_table, lambda_init)
        S0p = jnp.zeros((yp.shape[0], H_A, DK_A, DV_A), jnp.float32)
        yp, kp, vp, sp = mixer_layer(yp, c_prompt, S0p, None, None, *wl)
        past_k = cache_k[l][page_table].reshape(dec_b, -1, H_B, DV_B)
        past_v = cache_v[l][page_table].reshape(dec_b, -1, H_B, DV_B)
        ys, ksm, vsm, ssm = mixer_layer(ys, c_sample, state_hgrn[l], past_k, past_v, *wl)
        kp_l.append(kp); vp_l.append(vp); sp_l.append(sp)
        ksm_l.append(ksm); vsm_l.append(vsm); ssm_l.append(ssm)
    k_prompt = jnp.stack(kp_l)
    v_prompt = jnp.stack(vp_l)
    state_prompt = jnp.stack(sp_l)
    k_sample = jnp.stack(ksm_l)
    v_sample = jnp.stack(vsm_l)
    state_sample = jnp.stack(ssm_l)
    return (yp, ys, k_prompt, v_prompt, state_prompt, k_sample, v_sample, state_sample)


_drawn_inputs = setup_inputs


def setup_inputs(seed=0):
    import zlib

    import numpy as np

    out = dict(_drawn_inputs(seed))
    spreads = {}
    factors = {'norm_w': 3.089,
     'hg_norm_w': 8.0,
     'q_norm_w': 8.0,
     'lam_q1': 8.0,
     'lam_k1': 8.0,
     'lam_q2': 8.0,
     'lam_k2': 8.0,
     'sub_norm_w': 8.0,
     'rel_table': 2.689}
    for name, (base, spread) in spreads.items():
        noise = np.random.default_rng([zlib.crc32(name.encode()), seed]).standard_normal(out[name].shape)
        drawn = base * np.exp(spread * noise) if base else spread * noise
        out[name] = __import__('jax').numpy.asarray(drawn.astype(out[name].dtype))
    for name, factor in factors.items():
        out[name] = (out[name] * factor).astype(out[name].dtype)
    return out
```

```python
import concourse.bass as bass
from concourse import mybir
from contextlib import ExitStack
import numpy as np

F32 = mybir.dt.float32
I32 = mybir.dt.int32
U32 = mybir.dt.uint32
ALU = mybir.AluOpType
ACT = mybir.ActivationFunctionType
AX = mybir.AxisListType

P = 128
DM = 1024
KT_N = DM // P
SEQ = 1024
NT = SEQ // P
NB, QS = 8, 8
ST = NB * QS
H, DH = 4, 64
SEC = 512
D_IN = 9 * SEC
QA, FA, IA, GA, ZA, QB, KB, VB, ZB = range(9)
PAGES, PAGE = 32, 128
PAST = PAGES * PAGE
CH = 4
NCH = PAGES // CH
SROW = (PAGES + CH) * 32
SUSE = (PAGES + 1) * 32
EPS = 1e-6
LAMBDA_INIT = 0.2
NEG = -1e30
DMAX = PAST + QS - 1
DTAB = DMAX + P
TCH = (DTAB + 511) // 512
PTAB = SEQ + P - 1
LEVELS = (16, 8, 4, 2, 1)

C_ID, C_SL, C_SZ, C_WM, C_GP, C_GS, C_BM, C_ONE, C_LC = 0, 128, 384, 864, 1056, 1312, 1440, 1448, 1480
C_N = 1482


def spread(view, axis, n):
    pattern = list(view.ap)
    pattern.insert(axis, (0, n))
    return bass.AP(view.tensor, view.offset, pattern)


class Shared:
    pass


class Own:

    def __init__(self, sem, base=0):
        self.sem, self.base, self.n = sem, base, 0

    def done(self, eng, ins):
        ins.then_inc(self.sem, 1)
        self.n += 1
        eng.wait_ge(self.sem, self.base + self.n)


def tensors(nc, stack):
    def sb(name, shape, dt=F32):
        return stack.enter_context(nc.sbuf_tensor(name, shape, dt))

    def pb(name, shape):
        return stack.enter_context(nc.psum_tensor(name, shape, F32))
    return sb, pb


def semaphores(nc, stack):
    made = []

    def clear():
        nc.clear_and_free_semaphores(made)
        nc.all_engine_barrier()

    def sem(name):
        made.append(nc.alloc_semaphore(name=name))
        return made[-1]
    stack.callback(clear)
    return sem


def layer(nc, a, outs):
    with ExitStack() as whole:
        g = Shared()
        g.a = a
        g.y_prompt, g.y_sample, g.k_prompt, g.v_prompt, g.s_prompt, g.k_sample, g.v_sample, g.s_sample = outs
        g.w_sec = a["w_in"].rearrange("l (k p) n -> (l p) k n", p=P)
        g.ks_rows = g.k_sample.rearrange("l b q h d -> (l b q) (h d)")
        g.vs_rows = g.v_sample.rearrange("l b q h d -> (l b q) (h d)")
        g.proj_d = nc.dram_tensor("proj_scratch", [SEQ + ST, D_IN], F32, kind="Internal").ap()
        g.tab_d = nc.dram_tensor("bias_scratch", [H, TCH * 512], F32, kind="Internal").ap()
        g.tabs_d = nc.dram_tensor("sample_bias_scratch", [QS, H, DTAB], F32, kind="Internal").ap()
        g.tabp_d = nc.dram_tensor("prompt_bias_scratch", [P, H, PTAB], F32, kind="Internal").ap()
        g.q_d = nc.dram_tensor("query_scratch", [NB, P, 512], F32, kind="Internal").ap()
        sb, _ = tensors(nc, whole)
        g.cst = sb("cst", [P, C_N])
        g.ident = g.cst[:, C_ID:C_ID + P]
        g.mod = sb("mod", [P, 2, 512])
        g.rT = sb("rT", [P, P])
        g.wqk = sb("wqk", [P, 2, DH])
        g.subw = sb("subw", [P, P])
        g.hgw = sb("hgw", [P, P])
        g.nlam = sb("nlam", [P, 1])
        g.lamc = sb("lamc", [P, 1])
        g.epsc = sb("epsc", [P, 1])
        g.Oall = sb("Oall", [P, NB, P])
        g.dve = Own(whole.enter_context(nc.semaphore("own_dve")))
        g.act = Own(whole.enter_context(nc.semaphore("own_act")))
        with ExitStack() as inputs:
            sb, _ = tensors(nc, inputs)
            g.hT = sb("hT", [P, KT_N, SEQ])
            g.hS = sb("hS", [P, KT_N, ST])
            g.W = sb("W", [P, 2, KT_N, SEC])
            g.w_early = [inputs.enter_context(nc.semaphore(f"w_early{i}")) for i in range(2)]
            g.w_in = [inputs.enter_context(nc.semaphore(f"w_in{i}")) for i in range(2)]
            g.tab_rows = inputs.enter_context(nc.semaphore("tab_rows"))
            setup(nc, g)
            with ExitStack() as both:
                sb, _ = tensors(nc, both)
                g.stage = sb("stage", [P, 4, SEC])
                g.bias = sb("bias", [P, 2, SUSE])
                sample_projection(nc, g)
                main_loop(nc, g)
        with ExitStack() as ys:
            sb, _ = tensors(nc, ys)
            g.yT = sb("yT", [P, KT_N, SEQ + ST])
            g.ot = sb("ot", [P, NT + 1, SEC])
            prompt_attention(nc, g)
            recurrence(nc, g)
            output(nc, g)


def setup(nc, g):
    a = g.a
    x_p = a["x_prompt"].rearrange("a (t p) d -> (a t) p d", p=P)
    x_s = a["x_sample"].rearrange("b q d -> (b q) d")
    w_ada = a["w_ada"].rearrange("l (k p) n -> (l k) p n", p=P)
    with ExitStack() as here:
        sb, pb = tensors(nc, here)
        sem = semaphores(nc, here)
        wa = sb("wa", [P, 4, 3 * DM])
        xin = sb("xin", [P, NT + 1, DM])
        rows = sb("rows", [P, P])
        silu_c = sb("silu_c", [P, KT_N, 32])
        sig_c = sb("sig_c", [P, 72])
        hot = sb("hot", [P, DTAB])
        rel = sb("rel", [P, H])
        tab = hot[64:64 + H, :]
        junk = g.hT[:, 0, :]
        bada = g.hT[:, 1:4, :].rearrange("p k n -> p (k n)")
        modT = sb("modT", [P, 2, 4, P])
        amp = sb("amp", [P, KT_N, 9])
        shf = sb("shf", [P, KT_N, 9])
        lamv = sb("lamv", [P, 4, DH])
        lamp = sb("lamp", [P, 2, DH])
        lamd = sb("lamd", [P, 2])
        lame = sb("lame", [P, 2])
        ssq = sb("ssq", [P, NT + 1])
        lnx = sb("lnx", [P, NT + 1])
        rsx = sb("rsx", [P, NT + 1])
        tmpS = sb("tmpS", [P, KT_N, ST])
        ada_ps = pb("ada_ps", [P, 2, 512])
        x_ps = pb("x_ps", [P, 2, DM])
        m_ps = pb("m_ps", [P, 2, 512])

        zeroed, bada_in = sem("zeroed"), sem("bada_in")
        cst_in, small_in, lam_in, hot_in = sem("cst_in"), sem("small_in"), sem("lam_in"), sem("hot_in")
        wa_in = [sem(f"wa_in{i}") for i in range(4)]
        x_in = [sem(f"x_in{t}") for t in range(NT + 1)]
        rows_t, rT_ok, silu_ok, wa_used = sem("rows_t"), sem("rT_ok"), sem("silu_ok"), sem("wa_used")
        tab_t, tab_ok, tab_out = sem("tab_t"), sem("tab_ok"), sem("tab_out")
        ada_t, mod_ok, modT_t, modT_ok, amp_ok = sem("ada_t"), sem("mod_ok"), sem("modT_t"), sem("modT_ok"), sem("amp_ok")
        sq_ok, xn_ok, x_t, hT_dve, hT_act, lamd_ok, lame_ok = (sem(n) for n in (
            "sq_ok", "xn_ok", "x_t", "hT_dve", "hT_act", "lamd_ok", "lame_ok"))

        block = here.enter_context(nc.Block())

        @block.sync
        def _(sp):
            sp.dma_start(g.cst[:, :], a["constants"]).then_inc(cst_in, 16)
            sp.wait_ge(zeroed, 1)
            sp.dma_start(rows[0:8, :], a["c_prompt"].rearrange("b (k p) -> (b k) p", p=P)).then_inc(small_in, 16)
            sp.dma_start(rows[8:72, :], a["c_sample"].rearrange("b (k p) -> (b k) p", p=P)).then_inc(small_in, 16)
            sp.dma_start(rows[72:80, :], a["norm_w"].rearrange("b (k p) -> (b k) p", p=P)).then_inc(small_in, 16)
            sp.dma_start(rows[80:88, :], a["lb_param"].rearrange("b (k p) -> (b k) p", p=P)).then_inc(small_in, 16)
            sp.wait_ge(zeroed, 3)
            sp.dma_start(bada[0:1, :], a["b_ada"]).then_inc(bada_in, 16)
            for k in range(KT_N):
                if k >= 4:
                    sp.wait_ge(wa_used, k - 3)
                sp.dma_start(wa[:, k % 4, :], w_ada[k]).then_inc(wa_in[k % 4], 16)
                if k < 4:
                    for t in (2 * k, 2 * k + 1):
                        sp.dma_start(xin[:, t, :], x_p[t]).then_inc(x_in[t], 16)
                if k == 3:
                    sp.dma_start(xin[0:ST, NT, :], x_s).then_inc(x_in[NT], 16)
            for i, s in enumerate((QB, KB)):
                sp.dma_start(g.W[:, i, :, :], g.w_sec[:, :, s * SEC:(s + 1) * SEC]).then_inc(g.w_early[i], 16)
            sp.wait_ge(tab_out, 16)
            sp.dma_start(g.tabs_d, spread(g.tab_d[:, 0:DTAB], 0, QS)).then_inc(g.tab_rows, 16)
            sp.dma_start(g.tabp_d, spread(g.tab_d[:, DTAB - PTAB:DTAB], 0, P)).then_inc(g.tab_rows, 16)

        @block.gpsimd
        def _(pool):
            nc.gpsimd.memset(rows[:, :], 0.0).then_inc(zeroed, 1)
            nc.gpsimd.memset(rel[:, :], 0.0).then_inc(zeroed, 1)
            nc.gpsimd.memset(bada, 0.0).then_inc(zeroed, 1)
            nc.gpsimd.memset(hot[0:64, :], 0.0).then_inc(zeroed, 1)
            nc.gpsimd.memset(silu_c[:, :, :], 0.0).then_inc(zeroed, 1)

        @block.scalar
        def _(act):
            act.wait_ge(zeroed, 2)
            act.dma_start(rel[0:32, :], a["rel_table"]).then_inc(hot_in, 16)
            act.dma_start(rel[32:33, :], a["masked"]).then_inc(hot_in, 16)
            act.wait_ge(zeroed, 4)
            act.dma_start(hot[0:33, :], a["buckets"]).then_inc(hot_in, 16)
            for j, name in enumerate(("lam_q1", "lam_k1", "lam_q2", "lam_k2")):
                act.dma_start(lamv[:, j, :], a[name].partition_broadcast(P)).then_inc(lam_in, 16)
            act.dma_start(g.wqk[:, 0, :], a["q_norm_w"].partition_broadcast(P)).then_inc(lam_in, 16)
            act.dma_start(g.wqk[:, 1, :], a["k_norm_w"].partition_broadcast(P)).then_inc(lam_in, 16)
            act.dma_start(g.subw[:, :], a["sub_norm_w"].partition_broadcast(P)).then_inc(lam_in, 16)
            act.dma_start(g.hgw[:, :], a["hg_norm_w"].partition_broadcast(P)).then_inc(lam_in, 16)
            act.wait_ge(rT_ok, 1)
            nc.scalar.activation(sig_c[:, :], g.rT[:, 0:72], ACT.Sigmoid).then_inc(silu_ok, 1)

            for t in range(NT + 1):
                n = P if t < NT else ST
                act.wait_ge(x_in[t], 16)
                g.act.done(act, nc.scalar.activation(junk[0:n, :], xin[0:n, t, :], ACT.Square,
                                                     accum_out=ssq[0:n, t:t + 1]))
            act.wait_ge(sq_ok, 1)
            g.act.done(act, nc.scalar.activation(lnx[:, :], ssq[:, :], ACT.Ln, bias=g.epsc[:, :], scale=1.0 / DM))
            g.act.done(act, nc.scalar.activation(rsx[:, :], lnx[:, :], ACT.Exp, scale=-0.5))
            for t in range(NT + 1):
                n = P if t < NT else ST
                nc.scalar.activation(xin[0:n, t, :], xin[0:n, t, :], ACT.Copy,
                                     scale=rsx[0:n, t:t + 1]).then_inc(xn_ok, 1)
            act.wait_ge(tab_ok, TCH)
            act.dma_start(g.tab_d[:, 0:DTAB], tab).then_inc(tab_out, 16)
            act.wait_ge(lamd_ok, 1)
            nc.scalar.activation(lame[:, :], lamd[:, :], ACT.Exp).then_inc(lame_ok, 1)
            act.wait_ge(amp_ok, 1)
            for t in range(NT):
                act.wait_ge(x_t, t + 1)
                for k in range(4, KT_N):
                    ins = nc.scalar.activation(g.hT[:, k, t * P:(t + 1) * P], x_ps[:, t % 2, k * P:(k + 1) * P],
                                               ACT.Identity, bias=shf[:, k, 0:1], scale=amp[:, k, 0:1])
                ins.then_inc(hT_act, 1)

        @block.vector
        def _(dve):
            own = g.dve
            nc.vector.memset(ssq[:, NT:NT + 1], 1.0)
            nc.vector.memset(g.epsc[:, :], EPS)
            nc.vector.memset(ada_ps[:, 1, :], 0.0).then_inc(sq_ok, 1)
            dve.wait_ge(rows_t, 1)
            nc.vector.tensor_copy(g.rT[:, :], m_ps[:, 0, 0:P]).then_inc(rT_ok, 1)
            dve.wait_ge(silu_ok, 1)
            dve.wait_ge(rT_ok, 1)
            dve.wait_ge(zeroed, 5)
            nc.vector.tensor_tensor(silu_c[:, :, 0:9], sig_c[:, :].rearrange("p (r k) -> p k r", k=KT_N),
                                    g.rT[:, 0:72].rearrange("p (r k) -> p k r", k=KT_N),
                                    ALU.mult).then_inc(silu_ok, 1)
            dve.wait_ge(lam_in, 16 * 8)
            dve.wait_ge(cst_in, 16)
            for j in range(2):
                own.done(dve, nc.vector.tensor_tensor_reduce(
                    out=lamp[:, j, :], in0=lamv[:, 2 * j, :], in1=lamv[:, 2 * j + 1, :], scale=1.0, scalar=0.0,
                    op0=ALU.mult, op1=ALU.add, accum_out=lamd[:, j:j + 1]))
            nc.vector.tensor_scalar(g.subw[:, :], g.subw[:, :], 1.0 - LAMBDA_INIT, None, ALU.mult).then_inc(lamd_ok, 1)
            for c in range(TCH):
                if c == KT_N:
                    dve.wait_ge(ada_t, 1)
                    nc.vector.tensor_copy(g.mod[:, :, :], ada_ps[:, :, :]).then_inc(mod_ok, 1)
                dve.wait_ge(tab_t, c + 1)
                n = min(512, DTAB - 512 * c)
                nc.vector.tensor_copy(tab[:, 512 * c:512 * c + n], m_ps[0:H, c % 2, 0:n]).then_inc(tab_ok, 1)
            for b in range(2):
                dve.wait_ge(modT_t, b + 1)
                own.done(dve, nc.vector.tensor_copy(modT[:, b, :, :], m_ps[:, b, :].rearrange("p (k c) -> p k c", c=P)))
            nw = g.rT[:, 72:80]
            for j in range(2):
                ks = slice(4 * j, 4 * j + 4)
                own.done(dve, nc.vector.tensor_scalar(amp[:, ks, :], modT[:, 0, :, 64 + 32 * j:73 + 32 * j],
                                                      1.0, None, ALU.add))
                own.done(dve, nc.vector.tensor_tensor(amp[:, ks, :], amp[:, ks, :], spread(nw[:, ks], 2, 9), ALU.mult))
                ins = nc.vector.tensor_copy(shf[:, ks, :], modT[:, 0, :, 32 * j:9 + 32 * j])
                if j == 0:
                    own.done(dve, ins)
            ins.then_inc(amp_ok, 1)
            dve.wait_ge(amp_ok, 1)
            for t in range(NT):
                dve.wait_ge(x_t, t + 1)
                for k in range(4):
                    ins = nc.vector.tensor_scalar(g.hT[:, k, t * P:(t + 1) * P], x_ps[:, t % 2, k * P:(k + 1) * P],
                                                  amp[:, k, 0:1], shf[:, k, 0:1], ALU.mult, ALU.add)
                ins.then_inc(hT_dve, 1)
            dve.wait_ge(x_t, NT + 1)
            own.done(dve, nc.vector.tensor_tensor(
                tmpS[:, :, :].rearrange("p k (b q) -> p k b q", q=QS),
                x_ps[:, 0, 0:512].rearrange("p (k b q) -> p k b q", k=KT_N, q=QS),
                spread(amp[:, :, 1:9], 3, QS), ALU.mult))
            own.done(dve, nc.vector.tensor_tensor(
                g.hS[:, :, :].rearrange("p k (b q) -> p k b q", q=QS),
                tmpS[:, :, :].rearrange("p k (b q) -> p k b q", q=QS),
                spread(shf[:, :, 1:9], 3, QS), ALU.add))
            dve.wait_ge(lame_ok, 1)
            own.done(dve, nc.vector.tensor_tensor(lamd[:, 0:1], lame[:, 1:2], lame[:, 0:1], ALU.subtract))
            own.done(dve, nc.vector.tensor_scalar(g.nlam[:, :], lamd[:, 0:1], LAMBDA_INIT, None, ALU.subtract))
            own.done(dve, nc.vector.tensor_tensor(g.lamc[:, :], g.nlam[:, :], g.cst[:, C_LC + 1:C_LC + 2], ALU.mult))
            own.done(dve, nc.vector.tensor_tensor(g.lamc[:, :], g.lamc[:, :], g.cst[:, C_LC:C_LC + 1], ALU.add))

        @block.tensor
        def _(pe):
            pe.wait_ge(cst_in, 16)
            pe.wait_ge(small_in, 64)
            nc.tensor.transpose(m_ps[:, 0, 0:P], rows[:, :], g.ident).then_inc(rows_t, 1)

            def table(c):
                if c >= 2:
                    pe.wait_ge(tab_ok, c - 1)
                n = min(512, DTAB - 512 * c)
                nc.tensor.matmul(m_ps[0:H, c % 2, 0:n], rel[0:64, :], hot[0:64, 512 * c:512 * c + n],
                                 start=True, stop=True).then_inc(tab_t, 1)

            pe.wait_ge(rT_ok, 1)
            pe.wait_ge(silu_ok, 2)
            pe.wait_ge(sq_ok, 1)
            for k in range(KT_N):
                pe.wait_ge(wa_in[k % 4], 16 * (k // 4 + 1))
                for c in range(6):
                    ins = nc.tensor.matmul(ada_ps[32 * (c % 4):32 * (c % 4) + 32, c // 4, :], silu_c[:, k, :],
                                           wa[:, k % 4, 512 * c:512 * c + 512], start=(k == 0), stop=False)
                ins.then_inc(wa_used, 1)
                if k == 0:
                    pe.wait_ge(hot_in, 48)
                table(k)
            pe.wait_ge(bada_in, 16)
            for c in range(6):
                ins = nc.tensor.matmul(ada_ps[32 * (c % 4):32 * (c % 4) + 32, c // 4, :],
                                       g.cst[:, C_ONE:C_ONE + 32], bada[:, 512 * c:512 * c + 512],
                                       start=False, stop=True)
            ins.then_inc(ada_t, 1)
            for c in range(KT_N, TCH):
                table(c)
            pe.wait_ge(mod_ok, 1)
            pe.wait_ge(tab_ok, TCH)
            for b in range(2):
                for k in range(4):
                    ins = nc.tensor.transpose(m_ps[:, b, k * P:(k + 1) * P], g.mod[:, b, k * P:(k + 1) * P], g.ident)
                ins.then_inc(modT_t, 1)
            pe.wait_ge(xn_ok, NT + 1)
            for t in range(NT):
                if t >= 2:
                    pe.wait_ge(hT_dve, t - 1)
                    pe.wait_ge(hT_act, t - 1)
                for k in range(KT_N):
                    ins = nc.tensor.transpose(x_ps[:, t % 2, k * P:(k + 1) * P], xin[:, t, k * P:(k + 1) * P], g.ident)
                ins.then_inc(x_t, 1)
            pe.wait_ge(hT_dve, NT - 1)
            pe.wait_ge(hT_act, NT - 1)
            for k in range(KT_N):
                ins = nc.tensor.transpose(x_ps[:, 0, k * ST:(k + 1) * ST], xin[0:ST, NT, k * P:(k + 1) * P],
                                          g.ident[0:ST, 0:ST])
            ins.then_inc(x_t, 1)


def sample_projection(nc, g):
    with ExitStack() as here:
        sb, pb = tensors(nc, here)
        sem = semaphores(nc, here)
        proj = sb("s_proj", [ST, 3 * SEC])
        sq = sb("s_sq", [ST, 2 * SEC])
        qkn = sb("s_qkn", [ST, 2 * SEC])
        zs = sb("s_z", [P, SEC // 2])
        ssum, lns, rs = sb("s_ssum", [ST, 16]), sb("s_ln", [ST, 16]), sb("s_rs", [ST, 16])
        qT = sb("s_qT", [ST, SEC])
        qst = sb("s_qst", [P, NB, 16, 32])
        s_ps = pb("s_ps", [P, 2, SEC])
        p_ps = pb("p_ps", [P, 2, SEC])
        vb_in, zb_in, bias_in = sem("vb_in"), sem("zb_in"), sem("bias_in")
        s_done, s_copied = sem("s_done"), sem("s_copied")
        z_done, z_copied, z_out = sem("z_done"), sem("z_copied"), [sem(f"z_out{i}") for i in range(4)]
        sum_ok, rs_ok, qkn_ok, qst0, qst_ok, stored = (sem(n) for n in (
            "sum_ok", "rs_ok", "qkn_ok", "qst0", "qst_ok", "s_stored"))
        block = here.enter_context(nc.Block())

        @block.sync
        def _(sp):
            sp.wait_ge(s_done, 1)
            sp.dma_start(g.W[:, 0, :, :], g.w_sec[:, :, VB * SEC:(VB + 1) * SEC]).then_inc(vb_in, 16)
            sp.wait_ge(s_done, 2)
            sp.dma_start(g.W[:, 1, :, :], g.w_sec[:, :, ZB * SEC:(ZB + 1) * SEC]).then_inc(zb_in, 16)
            sp.wait_ge(qkn_ok, 1)
            sp.dma_start(g.ks_rows, qkn[:, SEC:2 * SEC]).then_inc(stored, 16)
            sp.wait_ge(s_done, 3)
            sp.dma_start(g.W[:, 0, :, :], g.w_sec[:, :, 0:SEC]).then_inc(g.w_in[0], 16)
            sp.wait_ge(s_copied, 3)
            sp.dma_start(g.vs_rows, proj[:, 2 * SEC:3 * SEC]).then_inc(stored, 16)
            sp.wait_ge(qst_ok, 8)
            sp.dma_start(g.q_d.rearrange("b p n -> p b n"), qst[:, :, :, :].rearrange("p b j q -> p b (j q)")).then_inc(stored, 16)
            sp.wait_ge(s_copied, 4)
            for half in range(2):
                c0 = ZB * SEC + half * (SEC // 2)
                sp.dma_start(g.proj_d[SEQ:SEQ + ST, c0:c0 + SEC // 2], zs[half * ST:(half + 1) * ST, :]).then_inc(stored, 16)
            sp.wait_ge(stored, 80)
            for i in range(4):
                sp.wait_ge(z_out[i], 32)

        @block.gpsimd
        def _(pool):
            nc.gpsimd.memset(qst[:, :, :, :], 0.0).then_inc(qst0, 1)

        @block.scalar
        def _(act):
            for s in range(3):
                act.wait_ge(s_done, s + 1)
                for half in range(2):
                    ins = nc.scalar.activation(proj[:, s * SEC + half * (SEC // 2):s * SEC + (half + 1) * (SEC // 2)],
                                               s_ps[half * ST:(half + 1) * ST, s % 2, 0:SEC // 2], ACT.Copy)
                ins.then_inc(s_copied, 1)
                if s == 1:
                    act.wait_ge(sum_ok, 1)
                    g.act.done(act, nc.scalar.activation(lns[:, :], ssum[:, :], ACT.Ln, bias=g.epsc[0:ST, :], scale=1.0 / DH))
                    nc.scalar.activation(rs[:, :], lns[:, :], ACT.Exp, scale=-0.5).then_inc(rs_ok, 1)
            act.wait_ge(g.tab_rows, 32)
            loads = [(j, i, gr) for j in range(4) for i in range(4) for gr in range(2)]
            for t in range(NT):
                act.wait_ge(z_done, t + 1)
                if t >= 4:
                    act.wait_ge(z_out[t % 4], 16 * (t // 4))
                nc.scalar.activation(g.stage[:, t % 4, :], p_ps[:, t % 2, :], ACT.Copy).then_inc(z_copied, 1)
                act.wait_ge(z_copied, t + 1)
                act.dma_start(g.proj_d[t * P:(t + 1) * P, ZB * SEC:(ZB + 1) * SEC],
                              g.stage[:, t % 4, :]).then_inc(z_out[t % 4], 16)
                for j, i, gr in loads[t * 4:t * 4 + 4]:
                    first = g.tabs_d.offset + (2 * gr + j // 2) * DTAB + DMAX - PAST + 32 * i
                    row = 32 * j + QS * i
                    act.dma_start(g.bias[row:row + QS, gr, :].rearrange("p (n k) -> p n k", k=32),
                                  bass.AP(g.tabs_d.tensor, first, [[H * DTAB - 1, QS], [PAGE, PAGES + 1], [1, 32]])
                                  ).then_inc(bias_in, 16)
            act.wait_ge(s_done, 4)
            nc.scalar.activation(zs[:, :], s_ps[:, 1, 0:SEC // 2], ACT.Copy).then_inc(s_copied, 1)
            act.wait_ge(bias_in, 16 * 32)

        @block.vector
        def _(dve):
            own = g.dve
            own.done(dve, nc.vector.tensor_scalar(g.wqk[:, 0, :], g.wqk[:, 0, :], DH ** -0.5, None, ALU.mult))
            dve.wait_ge(s_copied, 2)
            qk = proj[:, 0:2 * SEC]
            own.done(dve, nc.vector.tensor_tensor(sq[:, :], qk, qk, ALU.mult))
            nc.vector.tensor_reduce(ssum[:, :], sq[:, :].rearrange("p (n d) -> p n d", d=DH), AX.X,
                                    ALU.add).then_inc(sum_ok, 1)
            dve.wait_ge(rs_ok, 1)
            own.done(dve, nc.vector.tensor_tensor(
                sq[:, :].rearrange("p (n d) -> p n d", d=DH), qk.rearrange("p (n d) -> p n d", d=DH),
                spread(rs[:, :], 2, DH), ALU.mult))
            ins = nc.vector.tensor_tensor(
                qkn[:, :].rearrange("p (w n d) -> p w n d", w=2, d=DH),
                sq[:, :].rearrange("p (w n d) -> p w n d", w=2, d=DH), spread(g.wqk[0:ST, :, :], 2, 8), ALU.mult)
            ins.then_inc(qkn_ok, 1)
            dve.wait_ge(qkn_ok, 1)
            own.done(dve, nc.vector.transpose(qT[:, :].bitcast(U32), qkn[:, 0:SEC].bitcast(U32)))
            dve.wait_ge(qst0, 1)
            for i in range(4):
                for hi in range(2):
                    nc.vector.tensor_copy(
                        qst[32 * i:32 * i + 32, 4 * hi:4 * hi + 4, :, QS * i:QS * i + QS],
                        qT[32 * hi:32 * hi + 32, :].rearrange("p (j b q) -> p b j q", j=16, q=QS)).then_inc(qst_ok, 1)

        @block.tensor
        def _(pe):
            def samples(s, half_W):
                for k in range(KT_N):
                    for half in range(2):
                        c0 = half * (SEC // 2)
                        ins = nc.tensor.matmul(s_ps[half * ST:(half + 1) * ST, s % 2, 0:SEC // 2], g.hS[:, k, :],
                                               g.W[:, half_W, k, c0:c0 + SEC // 2], start=(k == 0), stop=(k == KT_N - 1))
                ins.then_inc(s_done, 1)

            pe.wait_ge(g.w_early[0], 16)
            samples(0, 0)
            pe.wait_ge(g.w_early[1], 16)
            samples(1, 1)
            pe.wait_ge(vb_in, 16)
            pe.wait_ge(s_copied, 1)
            samples(2, 0)
            pe.wait_ge(zb_in, 16)
            for t in range(NT):
                if t >= 2:
                    pe.wait_ge(z_copied, t - 1)
                for k in range(KT_N):
                    ins = nc.tensor.matmul(p_ps[:, t % 2, :], g.hT[:, k, t * P:(t + 1) * P], g.W[:, 1, k, :],
                                           start=(k == 0), stop=(k == KT_N - 1))
                ins.then_inc(z_done, 1)
            pe.wait_ge(s_copied, 2)
            samples(3, 1)


KT0, SC0, SE0, KX0, VX0, PT0, PTV0, PV0, PJ0, PE0, OE0, SP0, EX0 = 4, 12, 2, 1, 1, 1, 2, 5, 16, 2, 1, 16, 1
PJR = NT + 1


def main_loop(nc, g):
    a = g.a
    ck = a["cache_k"].rearrange("l n t h d -> (l n) t (h d)")
    cv = a["cache_v"].rearrange("l n (i k) h d -> (l n) k i (h d)", i=4)
    n_pool = ck.shape[0]
    ks_b = g.k_sample.rearrange("l b q h d -> (l b) q (h d)")
    vs_b = g.v_sample.rearrange("l b q h d -> (l b) q (h d)")
    with ExitStack() as here:
        sb, pb = tensors(nc, here)
        sem = semaphores(nc, here)
        pages = sb("pages", [1, NB * PAGES], I32)
        K = sb("K", [P, 4, CH, SEC])
        V = sb("V", [P, 4, 4, SEC])
        KT = sb("KT", [P, 2, CH * SEC])
        kx = sb("kx", [32, SEC])
        kxT = sb("kxT", [P, SEC])
        vx = sb("vx", [P, SEC])
        Q = sb("Q", [P, 2, 512])
        S = sb("S", [P, 2, SROW])
        bias = g.bias
        ring_s = sb("ring_s", [P, SEC // 2])
        mx = sb("mx", [P, 2, NCH + 1])
        m32, mT, mr, mE, mB = (sb(n, [P, 32]) for n in ("m32", "mT", "mr", "mE", "mB"))
        den = sb("den", [P, 2])
        PTs = sb("PTs", [P, 2, 2 * P])
        coef = sb("coef", [P, 2])
        pj_ps = pb("pj_ps", [P, 2, SEC])
        sc_ps = pb("sc_ps", [P, 2, 512])
        pt_ps = pb("pt_ps", [P, 2, 512])
        o_ps = pb("o_ps", [P, 512])
        l_ps = pb("l_ps", [P, 512])

        pages_in, cleared = sem("pages_in"), sem("cleared")
        k_in = [sem(f"k_in{i}") for i in range(4)]
        v_in = [sem(f"v_in{i}") for i in range(4)]
        w_in, q_in = g.w_in, [sem("q_in0"), sem("q_in1")]
        kx_in, vx_in = sem("kx_in"), sem("vx_in")
        transposed, kx_done = sem("transposed"), sem("kx_done")
        scored, biased, max_ok, exp_ok = sem("scored"), sem("biased"), sem("max_ok"), sem("exp_ok")
        p_turned, p_copied, pv_done, den_done, o_copied = (sem(n) for n in (
            "p_turned", "p_copied", "pv_done", "den_done", "o_copied"))
        projected, proj_copied = sem("projected"), sem("proj_copied")
        spilled, spilled_s = [sem(f"spilled{i}") for i in range(4)], sem("spilled_s")
        own_loop, passed = sem("own_loop"), sem("passed")
        OWN = 2 * 6

        block = here.enter_context(nc.Block())

        @block.sync
        def _(sp):
            for s, v in ((transposed, KT0), (scored, SC0), (biased, SE0), (kx_done, KX0), (p_turned, PT0),
                         (p_copied, PTV0), (pv_done, PV0), (projected, PJ0), (proj_copied, PE0), (o_copied, OE0)):
                sp.sem_inc(s, v)
            for s in spilled + [spilled_s]:
                sp.sem_inc(s, SP0)
            sp.dma_start(pages[:, :], a["page_table"].rearrange("b n -> (b n)").rearrange("(o n) -> o n", o=1)).then_inc(pages_in, 16)
            sp.wait_ge(pages_in, 16)
            sp.wait_ge(cleared, 6)
            with sp.Fori(0, NB // 2) as it:
                for par in range(2):
                    n = it * 2 + par
                    sp.wait_ge(scored, n * (NCH + 1) + (SC0 - NCH - 1))
                    sp.dma_start(Q[:, par, :], g.q_d[bass.ds(n, 1), :, :].rearrange("b p n -> (b p) n")).then_inc(q_in[par], 16)
                    for c in range(NCH):
                        if c == 3:
                            sp.wait_ge(projected, n * PJR + PJ0)
                            sp.dma_start(g.W[:, 1 - par, :, :], g.w_sec[:, :, bass.ds(n * SEC + SEC, SEC)]
                                         ).then_inc(w_in[1 - par], 16)
                        sp.wait_ge(transposed, n * NCH + (c + 1 + KT0 - 4))
                        for i in range(CH):
                            page = sp.value_load(pages[0:1, bass.ds(n * PAGES + (c * CH + i), 1)],
                                                 min_val=0, max_val=n_pool - 1)
                            sp.dma_start(K[:, c % 4, i, :], ck[bass.ds(page, 1), :, :].rearrange("n t d -> (n t) d")
                                         ).then_inc(k_in[c % 4], 16)
                    sp.wait_ge(kx_done, n + KX0)
                    sp.dma_start(kx[0:QS, :], ks_b[bass.ds(n, 1), :, :].rearrange("b q d -> (b q) d")).then_inc(kx_in, 16)
            for i in range(4):
                sp.wait_ge(spilled[i], SP0 + 16 * NT * NB // 4)
            sp.wait_ge(spilled_s, SP0 + 32 * NB)
            sp.wait_ge(w_in[0], 16 * (NB // 2 + 1))

        @block.gpsimd
        def _(pool):
            nc.gpsimd.memset(kx[:, :], 0.0).then_inc(cleared, 1)
            nc.gpsimd.memset(vx[:, :], 0.0).then_inc(cleared, 1)
            nc.gpsimd.memset(kxT[:, :], 0.0).then_inc(cleared, 1)
            nc.gpsimd.memset(S[:, :, SUSE:SROW], 0.0).then_inc(cleared, 1)
            pool.wait_ge(pages_in, 16)
            pool.wait_ge(cleared, 6)
            with pool.Fori(0, NB // 2) as it:
                for par in range(2):
                    n = it * 2 + par
                    for c in range(NCH):
                        if c >= 4:
                            pool.wait_ge(pv_done, n * (NCH + 1) + (c - 4 + 1 + PV0))
                        else:
                            pool.wait_ge(pv_done, n * (NCH + 1) + (c + 4 - NCH + PV0))
                        for i in range(CH):
                            page = pool.value_load(pages[0:1, bass.ds(n * PAGES + (c * CH + i), 1)],
                                                   min_val=0, max_val=n_pool - 1)
                            pool.dma_start(V[32 * i:32 * i + 32, c % 4, :, :],
                                           cv[bass.ds(page, 1), :, :, :].rearrange("n k i d -> (n k) i d")
                                           ).then_inc(v_in[c % 4], 16)
                    pool.wait_ge(pv_done, n * (NCH + 1) + PV0)
                    pool.dma_start(vx[0:QS, :], vs_b[bass.ds(n, 1), :, :].rearrange("b q d -> (b q) d")).then_inc(vx_in, 16)

        @block.scalar
        def _(act):
            with act.Fori(0, NB // 2) as it:
                for par in range(2):
                    n = it * 2 + par
                    for t in range(NT):
                        if t == 4:
                            act.wait_ge(max_ok, n + 1)
                            for gr in range(2):
                                nc.scalar.activation(S[:, gr, 0:SUSE], S[:, gr, 0:SUSE], ACT.Exp, bias=mB[:, gr:gr + 1],
                                                     accum_out=den[:, gr:gr + 1]).then_inc(exp_ok, 1)
                        act.wait_ge(projected, n * PJR + (t + 1 + PJ0))
                        act.wait_ge(spilled[t % 4], n * 32 + (t // 4 + 1) * 16)
                        nc.scalar.activation(g.stage[:, t % 4, :], pj_ps[:, (par + t) % 2, :], ACT.Copy).then_inc(proj_copied, 1)
                        act.wait_ge(proj_copied, n * PJR + (t + 1 + PE0))
                        act.dma_start(g.proj_d[t * P:(t + 1) * P, bass.ds(n * SEC, SEC)],
                                      g.stage[:, t % 4, :]).then_inc(spilled[t % 4], 16)
                    act.wait_ge(projected, n * PJR + (PJR + PJ0))
                    act.wait_ge(spilled_s, n * 32 + SP0)
                    nc.scalar.activation(ring_s[:, :], pj_ps[:, (par + NT) % 2, 0:SEC // 2], ACT.Copy).then_inc(proj_copied, 1)
                    act.wait_ge(proj_copied, n * PJR + (PJR + PE0))
                    for half in range(2):
                        act.dma_start(g.proj_d[SEQ:SEQ + ST, bass.ds(n * SEC + half * (SEC // 2), SEC // 2)],
                                      ring_s[half * ST:(half + 1) * ST, :]).then_inc(spilled_s, 16)

        @block.vector
        def _(dve):
            nc.vector.memset(m32[:, :], 0.0).then_inc(cleared, 1)
            nc.vector.memset(o_ps[:, :], 0.0).then_inc(cleared, 1)
            dve.wait_ge(cleared, 6)

            with dve.Fori(0, NB // 2) as it:
                own = Own(own_loop, it * OWN)

                def turn(n, par, c):
                    e = n * (NCH + 1)
                    if c < NCH:
                        dve.wait_ge(k_in[c % 4], (n * 2 + (c // 4 + 1)) * 64)
                        dve.wait_ge(scored, e + (c - 1 + SC0 if c >= 2 else c - 2 + SC0))
                        nc.vector.transpose(KT[:, c % 2, :].bitcast(U32),
                                            K[:, c % 4, :, :].rearrange("p i d -> p (i d)").bitcast(U32)
                                            ).then_inc(transposed, 1)
                    else:
                        dve.wait_ge(kx_in, (n + 1) * 16)
                        dve.wait_ge(scored, e + (SC0 + c - (NCH + 1) + 1))
                        nc.vector.transpose(kxT[0:32, :].bitcast(U32), kx[:, :].bitcast(U32)).then_inc(kx_done, 1)

                def add_bias(n, par, c):
                    bank, w = (par * (NCH + 1) + c) % 2, P if c < NCH else 32
                    dve.wait_ge(scored, n * (NCH + 1) + (c + 1 + SC0))
                    if c == 0:
                        dve.wait_ge(p_turned, n * (NCH + 1) + PT0)
                    dve.sem_inc(passed, 1)
                    for gr in range(2):
                        ins = nc.vector.tensor_tensor_reduce(
                            out=S[:, gr, c * P:c * P + w], in0=sc_ps[:, bank, gr * P:gr * P + w],
                            in1=bias[:, gr, c * P:c * P + w], scale=1.0, scalar=-3e38, op0=ALU.add, op1=ALU.max,
                            accum_out=mx[:, gr, c:c + 1])
                    ins.then_inc(biased, 1)

                for par in range(2):
                    n = it * 2 + par
                    turn(n, par, 0)
                    for c in range(1, NCH + 1):
                        turn(n, par, c)
                        add_bias(n, par, c - 1)
                    add_bias(n, par, NCH)
                    dve.wait_ge(biased, n * (NCH + 1) + (NCH + 1 + SE0))
                    own.done(dve, nc.vector.tensor_reduce(m32[:, 0:2], mx[:, :, :], AX.X, ALU.max))
                    own.done(dve, nc.vector.transpose(mT[:, :].bitcast(U32), m32[:, :].bitcast(U32)))
                    own.done(dve, nc.vector.tensor_reduce(mr[:, 0:QS], mT[:, :].rearrange("p (i q) -> p q i", i=4),
                                                          AX.X, ALU.max, negate=True))
                    own.done(dve, nc.vector.tensor_copy(mE[:, :].rearrange("p (i q) -> p i q", i=4),
                                                        spread(mr[:, 0:QS], 1, 4)))
                    nc.vector.transpose(mB[:, :].bitcast(U32), mE[:, :].bitcast(U32)).then_inc(max_ok, 1)
                    for c in range(NCH + 1):
                        f = n * (NCH + 1)
                        bank = (par * (NCH + 1) + c) % 2
                        dve.wait_ge(p_turned, f + (c + 1 + PT0))
                        dve.wait_ge(pv_done, f + (c - 1 + PV0))
                        nc.vector.tensor_copy(
                            PTs[:, bank, :].rearrange("p (h i c q) -> p h c i q", h=H, i=4, q=QS),
                            pt_ps[:, bank, 0:2 * P].rearrange("p (h c i q) -> p h c i q", h=H, c=2, q=QS)
                        ).then_inc(p_copied, 1)
                    dve.wait_ge(den_done, n + 1)
                    own.done(dve, nc.vector.reciprocal(coef[:, 0:1], l_ps[:, 0:1]))
                    own.done(dve, nc.vector.tensor_tensor(coef[:, 1:2], coef[:, 0:1], g.lamc[:, :], ALU.mult))
                    dve.wait_ge(pv_done, (n + 1) * (NCH + 1) + PV0)
                    nc.vector.tensor_scalar(g.Oall[:, bass.ds(n, 1), :].rearrange("p b v -> p (b v)"),
                                            o_ps[:, 0:P], coef[:, 1:2], None, ALU.mult).then_inc(o_copied, 1)
                assert own.n == OWN

        @block.tensor
        def _(pe):
            pe.wait_ge(cleared, 6)
            with pe.Fori(0, NB // 2) as it:

                def project(n, par, t):
                    if t == 0:
                        pe.wait_ge(w_in[par], (it + 1) * 16)
                    pe.wait_ge(proj_copied, n * PJR + (t + 1 - 2 + PE0))
                    bank = (par + t) % 2
                    for k in range(KT_N):
                        if t < NT:
                            ins = nc.tensor.matmul(pj_ps[:, bank, :], g.hT[:, k, t * P:(t + 1) * P], g.W[:, par, k, :],
                                                   start=(k == 0), stop=(k == KT_N - 1))
                            continue
                        for half in range(2):
                            c0 = half * (SEC // 2)
                            ins = nc.tensor.matmul(pj_ps[half * ST:(half + 1) * ST, bank, 0:SEC // 2], g.hS[:, k, :],
                                                   g.W[:, par, k, c0:c0 + SEC // 2], start=(k == 0), stop=(k == KT_N - 1))
                    ins.then_inc(projected, 1)

                def score(n, par, c):
                    bank, e = (par * (NCH + 1) + c) % 2, n * (NCH + 1)
                    if c == 0:
                        pe.wait_ge(q_in[par], (it + 1) * 16)
                    if c < NCH:
                        pe.wait_ge(transposed, n * NCH + (c + 1 + KT0))
                        keys, w = KT[:, c % 2, :].rearrange("p (n j k) -> p n j k", n=CH, k=32), P
                    else:
                        pe.wait_ge(kx_done, n + (1 + KX0))
                        keys, w = kxT[:, :].rearrange("p (n j k) -> p n j k", n=1, k=32), 32
                    pe.wait_ge(biased, e + (c + 1 - 2 + SE0))
                    for gr in range(2):
                        for db in range(2):
                            for m in range(4):
                                j = (4 * gr + m) * 2 + db
                                ins = nc.tensor.matmul(sc_ps[32 * m:32 * m + 32, bank, gr * P:gr * P + w],
                                                       Q[:, par, j * 32:j * 32 + 32], keys[:, :, j, :],
                                                       start=(db == 0), stop=(db == 1))
                    ins.then_inc(scored, 1)

                def turn(n, par, c):
                    bank = (par * (NCH + 1) + c) % 2
                    if c == 0:
                        pe.wait_ge(exp_ok, n * 2 + 2)
                    pe.wait_ge(p_copied, n * (NCH + 1) + (c + 1 - 2 + PTV0))
                    for gr in range(2):
                        ins = nc.tensor.transpose(pt_ps[:, bank, gr * P:(gr + 1) * P], S[:, gr, c * P:(c + 1) * P], g.ident)
                    ins.then_inc(p_turned, 1)

                def values(n, par, c):
                    bank, f = (par * (NCH + 1) + c) % 2, n * (NCH + 1)
                    pe.wait_ge(p_copied, f + (c + 1 + PTV0))
                    if c < NCH:
                        pe.wait_ge(v_in[c % 4], (n * 2 + (c // 4 + 1)) * 64)
                    else:
                        pe.wait_ge(vx_in, (n + 1) * 16)
                    for i in range(4 if c < NCH else 1):
                        for h in range(H):
                            part = PTs[:, bank, h * DH + 16 * i:h * DH + 16 * i + 16]
                            v = V[:, c % 4, i, h * P:(h + 1) * P] if c < NCH else vx[:, h * P:(h + 1) * P]
                            ins = nc.tensor.matmul(o_ps[32 * h:32 * h + 16, 0:P], part, v,
                                                   start=(c == 0 and i == 0), stop=(c == NCH))
                    ins.then_inc(pv_done, 1)

                for par in range(2):
                    n = it * 2 + par
                    for t in range(4):
                        project(n, par, t)
                        score(n, par, 2 * t)
                        score(n, par, 2 * t + 1)
                    score(n, par, NCH)
                    project(n, par, 4)
                    turn(n, par, 0)
                    pe.wait_ge(o_copied, n + OE0)
                    for gr in range(2):
                        ins = nc.tensor.matmul(l_ps[:, 0:1], g.cst[:, C_SL + gr * P:C_SL + (gr + 1) * P],
                                               den[:, gr:gr + 1], start=(gr == 0), stop=(gr == 1))
                    ins.then_inc(den_done, 1)
                    for c in range(NCH + 1):
                        if c < NCH:
                            turn(n, par, c + 1)
                        values(n, par, c)
                        if c in (1, 3, 5, 7):
                            project(n, par, {1: 5, 3: 6, 5: 7, 7: 8}[c])


def prompt_attention(nc, g):
    a = g.a
    kp_rows = g.k_prompt.rearrange("l b (t p) h d -> (l b t) p (h d)", p=P)
    vp_rows = g.v_prompt.rearrange("l b (t p) h d -> (l b t) p (h d)", p=P)
    STEPS = NT * H
    groups = [[(k, min(k + 4, v // H + 1)) for k in range(0, v // H + 1, 4)] for v in range(STEPS)]
    first_group = [sum(len(x) for x in groups[:v]) for v in range(STEPS + 1)]
    with ExitStack() as here:
        sb, pb = tensors(nc, here)
        sem = semaphores(nc, here)
        KTh = sb("a_KT", [P, H, SEQ])
        Vp = sb("a_V", [P, NT, SEC])
        Z = sb("a_Z", [P, NT + 1, SEC])
        sig = sb("a_sig", [P, NT + 1, SEC])
        bias = sb("a_bias", [P, H, SEQ])
        E = sb("a_E", [P, 2, 2, SEQ])
        AT = sb("a_AT", [P, 2, SEQ])
        qk = sb("a_qk", [P, 2, 2 * SEC])
        sq = sb("a_sq", [P, 2 * SEC])
        junk = sb("a_junk", [P, H, P])
        QZ = sb("a_QZ", [P, 2, 2, H, P])
        o = sb("a_o", [P, 2, SEC])
        os_sq = sb("a_ossq", [ST, SEC])
        ssum, lns, rs = sb("a_ssum", [P, 16]), sb("a_lns", [P, 16]), sb("a_rs", [P, 16])
        mx, nm, den, rec = sb("a_mx", [P, 4]), sb("a_nm", [P, 4]), sb("a_den", [P, 4]), sb("a_rec", [P, 8])
        coef = sb("a_coef", [P, 1])
        oss, oln, ors = sb("a_oss", [P, 8]), sb("a_oln", [P, 4]), sb("a_ors", [P, 8])
        qk_ps = pb("a_qk_ps", [P, 512])
        s_ps = pb("a_s_ps", [P, 2, SEQ])
        at_ps = pb("a_at_ps", [P, 2, 512])
        o_ps = pb("a_o_ps", [P, 512])

        z_in, v_in, bias_in = sem("az_in"), sem("av_in"), sem("abias_in")
        qk_in, k_out = [sem("aqk_in0"), sem("aqk_in1")], [sem("ak_out0"), sem("ak_out1")]
        v_out, qz0 = sem("av_out"), sem("aqz0")
        names = ("sig_ok z_ok so_t so_ok so_sum so_rs so_y so_turned so_copied sq_ok sum_ok rs_ok qkn_ok q_turned "
                 "k_turned q_copied k_copied s_done biased max_ok exp_ok a_ok at_turned at_copied pv_group "
                 "o_ok oss_ok ors_ok y_ok y_turned y_copied")
        (sig_ok, z_ok, so_t, so_ok, so_sum, so_rs, so_y, so_turned, so_copied, sq_ok, sum_ok, rs_ok, qkn_ok,
         q_turned, k_turned, q_copied, k_copied, s_done, biased, max_ok, exp_ok, a_ok, at_turned, at_copied,
         pv_done, o_ok, oss_ok, ors_ok, y_ok, y_turned, y_copied) = (sem("a_" + n) for n in names.split())
        block = here.enter_context(nc.Block())

        @block.sync
        def _(sp):
            for t in range(NT + 1):
                n = P if t < NT else ST
                sp.dma_start(Z[0:n, t, :], g.proj_d[t * P:t * P + n, ZB * SEC:(ZB + 1) * SEC]).then_inc(z_in, 16)
            for i in range(NT):
                if i >= 2:
                    sp.wait_ge(qkn_ok, i - 1)
                    sp.dma_start(kp_rows[i - 2], qk[:, i % 2, SEC:2 * SEC]).then_inc(k_out[i % 2], 16)
                    sp.wait_ge(k_turned, i - 1)
                    sp.wait_ge(k_out[i % 2], 16 * (i // 2))
                sp.dma_start(qk[:, i % 2, :], g.proj_d[i * P:(i + 1) * P, QB * SEC:(KB + 1) * SEC]).then_inc(qk_in[i % 2], 16)
                if i == 0:
                    for j in range(NT):
                        sp.dma_start(Vp[:, j, :], g.proj_d[j * P:(j + 1) * P, VB * SEC:(VB + 1) * SEC]).then_inc(v_in, 16)
            sp.wait_ge(v_in, 16 * NT)
            sp.dma_start(vp_rows.rearrange("t p d -> p t d"), Vp[:, :, :]).then_inc(v_out, 16)
            for i in (NT - 2, NT - 1):
                sp.wait_ge(qkn_ok, i + 1)
                sp.dma_start(kp_rows[i], qk[:, i % 2, SEC:2 * SEC]).then_inc(k_out[i % 2], 16)
            sp.wait_ge(v_out, 16)
            for b in range(2):
                sp.wait_ge(k_out[b], 16 * NT // 2)

        @block.gpsimd
        def _(pool):
            nc.gpsimd.memset(QZ[:, :, :, :, :], 0.0).then_inc(qz0, 1)
            pool.dma_start(bias[:, :, :], bass.AP(g.tabp_d.tensor, g.tabp_d.offset + P - 1,
                                                  [[H * PTAB - 1, P], [PTAB, H], [1, SEQ]])).then_inc(bias_in, 16)
            pool.wait_ge(sig_ok, 1)
            nc.gpsimd.tensor_tensor(Z[:, 0:NT, :], Z[:, 0:NT, :], sig[:, 0:NT, :], ALU.mult).then_inc(z_ok, 1)
            pool.wait_ge(z_ok, 1)
            nc.gpsimd.tensor_tensor(
                Z[:, 0:NT, :].rearrange("p t (h d) -> p (t h) d", h=H), Z[:, 0:NT, :].rearrange("p t (h d) -> p (t h) d", h=H),
                spread(g.subw[:, :], 1, NT * H), ALU.mult).then_inc(z_ok, 1)

        @block.scalar
        def _(act):
            act.wait_ge(z_in, 16 * (NT + 1))
            nc.scalar.activation(sig[:, 0:NT, :], Z[:, 0:NT, :], ACT.Sigmoid).then_inc(sig_ok, 1)
            nc.scalar.activation(sig[0:ST, NT, :], Z[0:ST, NT, :], ACT.Sigmoid).then_inc(sig_ok, 1)
            act.wait_ge(so_sum, 1)
            g.act.done(act, nc.scalar.activation(oln[0:ST, 0:H], oss[0:ST, 0:H], ACT.Ln, bias=g.epsc[0:ST, :], scale=1.0 / P))
            nc.scalar.activation(ors[0:ST, 0:H], oln[0:ST, 0:H], ACT.Exp, scale=-0.5).then_inc(so_rs, 1)
            act.wait_ge(so_turned, 1)
            nc.scalar.activation(g.yT[:, 4:8, SEQ:SEQ + ST], qk_ps[:, 0:H * ST].rearrange("p (h t) -> p h t", h=H),
                                 ACT.Copy).then_inc(so_copied, 1)

            def square(i):
                act.wait_ge(qk_in[i % 2], 16 * (i // 2 + 1))
                if i:
                    act.wait_ge(sum_ok, i)
                nc.scalar.activation(sq[:, :], qk[:, i % 2, :], ACT.Square).then_inc(sq_ok, 1)

            def scale_of(i):
                act.wait_ge(sum_ok, i + 1)
                g.act.done(act, nc.scalar.activation(lns[:, :], ssum[:, :], ACT.Ln, bias=g.epsc[:, :], scale=1.0 / DH))
                nc.scalar.activation(rs[:, :], lns[:, :], ACT.Exp, scale=-0.5).then_inc(rs_ok, 1)

            def queries(i):
                act.wait_ge(q_turned, i + 1)
                if i == 0:
                    act.wait_ge(qz0, 1)
                if i >= 2:
                    act.wait_ge(s_done, 2 * H * (i - 1))
                for c in range(2):
                    rows = slice(DH * c, DH * c + DH)
                    ins = nc.scalar.activation(QZ[rows, i % 2, c, :, :],
                                               qk_ps[rows, :].rearrange("p (h t) -> p h t", h=H), ACT.Copy)
                ins.then_inc(q_copied, 1)

            def numerators(v):
                for c in range(2):
                    act.wait_ge(max_ok, 2 * v + c + 1)
                    w = (v // H + 1) * P
                    nc.scalar.activation(E[:, v % 2, c, 0:w], E[:, v % 2, c, 0:w], ACT.Exp,
                                         bias=nm[:, 2 * (v % 2) + c:2 * (v % 2) + c + 1],
                                         accum_out=den[:, 2 * (v % 2) + c:2 * (v % 2) + c + 1]).then_inc(exp_ok, 1)

            square(0)
            scale_of(0)
            queries(0)
            numerators(0)
            for v in range(STEPS + 4):
                i, h = divmod(v, H)
                if i + 1 < NT:
                    if h == 0:
                        square(i + 1)
                    if h == 1:
                        scale_of(i + 1)
                    if h == 2:
                        queries(i + 1)
                if v + 1 < STEPS:
                    numerators(v + 1)
                if v < STEPS:
                    for n, (k0, k1) in enumerate(groups[v]):
                        e = first_group[v] + n
                        act.wait_ge(at_turned, e + 1)
                        nc.scalar.activation(AT[:, v % 2, k0 * P:k1 * P], at_ps[:, e % 2, 0:(k1 - k0) * P],
                                             ACT.Copy).then_inc(at_copied, 1)
                if 1 <= v <= STEPS:
                    u = v - 1
                    act.wait_ge(o_ok, u + 1)
                    slot = (u // H % 2) * H + u % H
                    nc.scalar.activation(junk[:, u % H, :], o[:, u // H % 2, (u % H) * P:(u % H + 1) * P], ACT.Square,
                                         accum_out=oss[:, slot:slot + 1]).then_inc(oss_ok, 1)
                if h == 0 and i >= 1:
                    s0 = ((i - 1) % 2) * H
                    act.wait_ge(oss_ok, H * i)
                    g.act.done(act, nc.scalar.activation(oln[:, :], oss[:, s0:s0 + H], ACT.Ln, bias=g.epsc[:, :], scale=1.0 / P))
                    nc.scalar.activation(ors[:, s0:s0 + H], oln[:, :], ACT.Exp, scale=-0.5).then_inc(ors_ok, 1)
                if h == 3 and i >= 1:
                    act.wait_ge(y_turned, i)
                    nc.scalar.activation(g.yT[:, 4:8, (i - 1) * P:i * P],
                                         qk_ps[:, :].rearrange("p (h t) -> p h t", h=H), ACT.Copy).then_inc(y_copied, 1)

        @block.vector
        def _(dve):
            own = g.dve
            dve.wait_ge(so_t, 1)
            own.done(dve, nc.vector.tensor_copy(o[0:ST, 0, :], o_ps[0:ST, :]))
            so_h = o[0:ST, 0, :].rearrange("p (h d) -> p h d", h=H)
            own.done(dve, nc.vector.tensor_tensor(os_sq[:, :], o[0:ST, 0, :], o[0:ST, 0, :], ALU.mult))
            nc.vector.tensor_reduce(oss[0:ST, 0:H], os_sq[:, :].rearrange("p (h d) -> p h d", h=H), AX.X,
                                    ALU.add).then_inc(so_sum, 1)
            dve.wait_ge(sig_ok, 2)
            own.done(dve, nc.vector.tensor_tensor(Z[0:ST, NT, :], Z[0:ST, NT, :], sig[0:ST, NT, :], ALU.mult))
            own.done(dve, nc.vector.tensor_tensor(
                Z[0:ST, NT, :].rearrange("p (h d) -> p h d", h=H), Z[0:ST, NT, :].rearrange("p (h d) -> p h d", h=H),
                spread(g.subw[0:ST, :], 1, H), ALU.mult))
            dve.wait_ge(so_rs, 1)
            own.done(dve, nc.vector.tensor_tensor(so_h, so_h, spread(ors[0:ST, 0:H], 2, P), ALU.mult))
            nc.vector.tensor_tensor(o[0:ST, 0, :], o[0:ST, 0, :], Z[0:ST, NT, :], ALU.mult).then_inc(so_y, 1)
            dve.wait_ge(so_turned, 1)

            def sums(i):
                dve.wait_ge(sq_ok, i + 1)
                nc.vector.tensor_reduce(ssum[:, :], sq[:, :].rearrange("p (n d) -> p n d", d=DH), AX.X,
                                        ALU.add).then_inc(sum_ok, 1)

            def normalise(i):
                dve.wait_ge(rs_ok, i + 1)
                x = qk[:, i % 2, :]
                own.done(dve, nc.vector.tensor_tensor(x.rearrange("p (n d) -> p n d", d=DH), x.rearrange("p (n d) -> p n d", d=DH),
                                                      spread(rs[:, :], 2, DH), ALU.mult))
                nc.vector.tensor_tensor(x.rearrange("p (w n d) -> p w n d", w=2, d=DH),
                                        x.rearrange("p (w n d) -> p w n d", w=2, d=DH),
                                        spread(g.wqk[:, :, :], 2, 8), ALU.mult).then_inc(qkn_ok, 1)

            def keys(i):
                dve.wait_ge(k_turned, i + 1)
                nc.vector.tensor_copy(KTh[:, :, i * P:(i + 1) * P],
                                      qk_ps[:, :].rearrange("p (h t) -> p h t", h=H)).then_inc(k_copied, 1)

            def maxima(v):
                w = (v // H + 1) * P
                if v >= 2:
                    dve.wait_ge(at_turned, first_group[v - 1])
                for c in range(2):
                    slot = 2 * (v % 2) + c
                    dve.wait_ge(s_done, 2 * v + c + 1)
                    if v == 0 and c == 0:
                        dve.wait_ge(bias_in, 16)
                    nc.vector.tensor_tensor_reduce(
                        out=E[:, v % 2, c, 0:w], in0=s_ps[:, c, 0:w], in1=bias[:, v % H, SEQ - w:SEQ], scale=1.0,
                        scalar=-3e38, op0=ALU.add, op1=ALU.max, accum_out=mx[:, slot:slot + 1]).then_inc(biased, 1)
                    dve.wait_ge(biased, 2 * v + c + 1)
                    nc.vector.tensor_scalar(nm[:, slot:slot + 1], mx[:, slot:slot + 1], -1.0, None, ALU.mult).then_inc(max_ok, 1)

            sums(0)
            normalise(0)
            keys(0)
            maxima(0)
            for v in range(STEPS + 4):
                i, h = divmod(v, H)
                if v < STEPS:
                    s0, r0 = 2 * (v % 2), 2 * (v % 4)
                    w = (i + 1) * P
                    dve.wait_ge(exp_ok, 2 * v + 2)
                    own.done(dve, nc.vector.reciprocal(rec[:, r0:r0 + 2], den[:, s0:s0 + 2]))
                    own.done(dve, nc.vector.scalar_tensor_tensor(coef[:, :], rec[:, r0 + 1:r0 + 2], g.nlam[:, :],
                                                                 den[:, s0:s0 + 1], ALU.mult, ALU.mult))
                    nc.vector.scalar_tensor_tensor(E[:, v % 2, 0, 0:w], E[:, v % 2, 1, 0:w], coef[:, :],
                                                   E[:, v % 2, 0, 0:w], ALU.mult, ALU.add).then_inc(a_ok, 1)
                if h == 3 and i + 1 < NT:
                    keys(i + 1)
                if v + 1 < STEPS:
                    maxima(v + 1)
                if 1 <= v <= STEPS:
                    u = v - 1
                    dve.wait_ge(pv_done, u + 1)
                    if u % H == 0 and u // H >= 2:
                        dve.wait_ge(y_turned, u // H - 1)
                    nc.vector.tensor_scalar(o[:, u // H % 2, (u % H) * P:(u % H + 1) * P], o_ps[:, (u % H) * P:(u % H + 1) * P],
                                            rec[:, 2 * (u % 4):2 * (u % 4) + 1], None, ALU.mult).then_inc(o_ok, 1)
                if h == 0 and i + 1 < NT:
                    sums(i + 1)
                if h == 1:
                    if i + 1 < NT:
                        normalise(i + 1)
                    if i >= 1:
                        b = (i - 1) % 2
                        if i == 1:
                            dve.wait_ge(z_ok, 2)
                        dve.wait_ge(ors_ok, i)
                        dve.wait_ge(o_ok, H * i)
                        x = o[:, b, :]
                        own.done(dve, nc.vector.tensor_tensor(x.rearrange("p (h d) -> p h d", h=H), x.rearrange("p (h d) -> p h d", h=H),
                                                              spread(ors[:, b * H:b * H + H], 2, P), ALU.mult))
                        nc.vector.tensor_tensor(x, x, Z[:, i - 1, :], ALU.mult).then_inc(y_ok, 1)

        @block.tensor
        def _(pe):
            for h in range(H):
                for b in range(NB):
                    ins = nc.tensor.matmul(o_ps[0:ST, h * P:(h + 1) * P],
                                           g.cst[:, C_SZ + h * 120 + 56 - QS * b:C_SZ + h * 120 + 120 - QS * b],
                                           g.Oall[:, b, :], start=(b == 0), stop=(b == NB - 1))
            ins.then_inc(so_t, 1)
            pe.wait_ge(so_y, 1)
            for h in range(H):
                ins = nc.tensor.transpose(qk_ps[:, h * ST:(h + 1) * ST], o[0:ST, 0, h * P:(h + 1) * P], g.ident[0:ST, 0:ST])
            ins.then_inc(so_turned, 1)

            def turn_q(i):
                pe.wait_ge(qkn_ok, i + 1)
                if i == 0:
                    pe.wait_ge(so_copied, 1)
                else:
                    pe.wait_ge(k_copied, i)
                    if i >= 3:
                        pe.wait_ge(y_copied, i - 2)
                for h in range(H):
                    ins = nc.tensor.transpose(qk_ps[:, h * P:(h + 1) * P], qk[:, i % 2, h * P:(h + 1) * P], g.ident)
                ins.then_inc(q_turned, 1)

            def turn_k(i):
                pe.wait_ge(q_copied, i + 1)
                for h in range(H):
                    ins = nc.tensor.transpose(qk_ps[:, h * P:(h + 1) * P], qk[:, i % 2, SEC + h * P:SEC + (h + 1) * P], g.ident)
                ins.then_inc(k_turned, 1)

            def turn_y(i):
                pe.wait_ge(y_ok, i + 1)
                if i + 2 < NT:
                    pe.wait_ge(k_copied, i + 3)
                elif i >= 1:
                    pe.wait_ge(y_copied, i)
                for j in range(H):
                    ins = nc.tensor.transpose(qk_ps[:, j * P:(j + 1) * P], o[:, i % 2, j * P:(j + 1) * P], g.ident)
                ins.then_inc(y_turned, 1)

            def scores(v):
                i, h = divmod(v, H)
                if h == 0:
                    pe.wait_ge(k_copied, i + 1)
                    pe.wait_ge(q_copied, i + 1)
                for c in range(2):
                    if v >= 1:
                        pe.wait_ge(biased, 2 * v + c - 1)
                    w = (i + 1) * P
                    for n0 in range(0, w, 512):
                        n1 = min(n0 + 512, w)
                        ins = nc.tensor.matmul(s_ps[:, c, n0:n1], QZ[:, i % 2, c, h, :], KTh[:, h, n0:n1], start=True, stop=True)
                    ins.then_inc(s_done, 1)

            def turn(v):
                pe.wait_ge(a_ok, v + 1)
                for n, (k0, k1) in enumerate(groups[v]):
                    e = first_group[v] + n
                    if e >= 2:
                        pe.wait_ge(at_copied, e - 1)
                    for k in range(k0, k1):
                        ins = nc.tensor.transpose(at_ps[:, e % 2, (k - k0) * P:(k - k0 + 1) * P],
                                                  E[:, v % 2, 0, k * P:(k + 1) * P], g.ident)
                    ins.then_inc(at_turned, 1)

            def values(v):
                i, h = divmod(v, H)
                pe.wait_ge(at_copied, first_group[v + 1])
                if v == 0:
                    pe.wait_ge(so_turned, 1)
                else:
                    pe.wait_ge(o_ok, v)
                for k in range(i + 1):
                    ins = nc.tensor.matmul(o_ps[:, h * P:(h + 1) * P], AT[:, v % 2, k * P:(k + 1) * P],
                                           Vp[:, k, h * P:(h + 1) * P], start=(k == 0), stop=(k == i))
                ins.then_inc(pv_done, 1)

            turn_q(0)
            turn_k(0)
            scores(0)
            pe.wait_ge(v_in, 16 * NT)
            for v in range(STEPS + 4):
                i, h = divmod(v, H)
                if h == 2 and i + 1 < NT:
                    turn_q(i + 1)
                if v + 1 < STEPS:
                    scores(v + 1)
                if 1 <= v <= STEPS:
                    values(v - 1)
                if v < STEPS:
                    turn(v)
                if h == 2 and i + 1 < NT:
                    turn_k(i + 1)
                if h == 3 and i >= 1:
                    turn_y(i - 1)


def recurrence(nc, g):
    a = g.a
    NL = len(LEVELS) + 1
    PL = [64, 32] + list(LEVELS)
    SL = [4, 2, 1]
    with ExitStack() as here:
        sb, pb = tensors(nc, here)
        sem = semaphores(nc, here)
        q, kin, B = (sb("r_" + n, [P, H, SEQ]) for n in ("q", "k", "b"))
        qs, ks, Bs = (sb("r_" + n, [P, H, ST]) for n in ("qs", "ks", "bs"))
        reset = sb("r_reset", [P, SEQ + ST])
        v = sb("r_v", [P, 2, NT, P])
        x = sb("r_x", [P, 2, 2 * SEC])
        M = sb("r_M", [P, 3, SEQ])
        qe = sb("r_qe", [P, SEQ])
        kd = sb("r_kd", [P, SEQ])
        kdT = sb("r_kdT", [P, SEQ])
        At = sb("r_At", [P, SEQ])
        wm = sb("r_wm", [P, NT, NL * 32])
        ws = sb("r_ws", [P, NT, 32])
        S = sb("r_S", [P, NT + 1, P])
        eb = sb("r_eb", [P, NT])
        lb = sb("r_lb", [P, 2, H])
        lm, lsum, oml = sb("r_lm", [P, H]), sb("r_lsum", [P, H]), sb("r_oml", [P, H])
        win_ps = pb("r_win", [P, NT, 256])
        dir_ps = pb("r_dir", [P, SEQ])
        k_ps = pb("r_kps", [P, 512])
        o_ps = pb("r_ops", [P, 512])

        x_in, v_in = [sem("rx_in0"), sem("rx_in1")], [sem("rv_in0"), sem("rv_in1")]
        reset_in, st_out = sem("r_reset_in"), sem("r_st_out")
        names = ("lb_e lb_ok x_turned q_copied f_copied log_ok scan_ok zero_ok d_ok e_ok mk_ok mq_ok lev_done win_ok at_ok "
                 "dir_ok ebe_ok kd_ok qe_ok kd_turned kd_copied ds_done s_ok o_done o_copied")
        (lb_e, lb_ok, x_turned, q_copied, f_copied, log_ok, scan_ok, zero_ok, d_ok, e_ok, mk_ok, mq_ok, lev_done,
         win_ok, at_ok, dir_ok, ebe_ok, kd_ok, qe_ok, kd_turned, kd_copied, ds_done, s_ok, o_done,
         o_copied) = (sem("r_" + n) for n in names.split())
        NLEV = len(PL)
        stage = ExitStack()
        block = stage.enter_context(nc.Block())

        @block.sync
        def _(sp):
            sp.dma_start(reset[:, :], bass.AP(a["resets"].tensor, a["resets"].offset,
                                              [[0, P], [1, SEQ + ST]])).then_inc(reset_in, 16)
            for t in range(NT + 1):
                n = P if t < NT else ST
                if t >= 2:
                    sp.wait_ge(x_turned, t - 1)
                sp.dma_start(x[0:n, t % 2, :], g.proj_d[t * P:t * P + n, 0:2 * SEC]).then_inc(x_in[t % 2], 16)
            def values(h):
                sp.dma_start(v[:, h % 2, :, :], g.proj_d[0:SEQ, IA * SEC + h * P:IA * SEC + (h + 1) * P].rearrange(
                    "(t p) d -> p t d", p=P)).then_inc(v_in[h % 2], 16)

            values(0)
            values(1)
            for h in range(H):
                sp.wait_ge(s_ok, (h + 1) * NT)
                sp.dma_start(g.s_prompt[0, 0, h, :, :], S[:, NT, :]).then_inc(st_out, 16)
                if h + 2 < H:
                    sp.wait_ge(o_done, (h + 1) * NT)
                    values(h + 2)
            sp.wait_ge(st_out, 16 * H)

        @block.scalar
        def _(act):
            act.wait_ge(lb_e, 1)
            nc.scalar.activation(lb[:, :, :], lb[:, :, :], ACT.Exp).then_inc(lb_e, 1)
            for t in range(NT + 1):
                n = P if t < NT else ST
                act.wait_ge(x_turned, t + 1)
                src = (win_ps[:, 4 * (t % 2) + 2:4 * (t % 2) + 4, :].rearrange("p a c -> p (a c)")[:, 0:H * n]
                       .rearrange("p (h n) -> p h n", h=H))
                fo, ko = (B[:, :, t * P:(t + 1) * P], kin[:, :, t * P:(t + 1) * P]) if t < NT else (Bs[:, :, :], ks[:, :, :])
                nc.scalar.activation(fo, src, ACT.Sigmoid)
                nc.scalar.activation(ko, src, ACT.Sigmoid, scale=-1.0).then_inc(f_copied, 1)
            act.wait_ge(lb_ok, 1)
            act.wait_ge(f_copied, NT + 1)
            for h in range(H):
                for m in (B, Bs):
                    ins = nc.scalar.activation(m[:, h, :], m[:, h, :], ACT.Ln, bias=lb[:, 0, h:h + 1],
                                               scale=oml[:, h:h + 1])
                ins.then_inc(log_ok, 1)

            def decays(h):
                for n, s in enumerate(PL):
                    e = h * (NLEV + 1) + n
                    act.wait_ge(d_ok, e + 1)
                    m = M[:, e % 3, :].rearrange("p (b s) -> p b s", s=2 * s)
                    nc.scalar.activation(m[:, :, 0:s], m[:, :, 0:s], ACT.Exp, scale=-1.0)
                    nc.scalar.activation(m[:, :, s:2 * s], m[:, :, s:2 * s], ACT.Exp).then_inc(e_ok, 1)
                e = h * (NLEV + 1) + NLEV
                act.wait_ge(d_ok, e + 1)
                nc.scalar.activation(M[:, e % 3, :], M[:, e % 3, :], ACT.Exp).then_inc(e_ok, 1)
                if h >= 1:
                    act.wait_ge(o_done, h * NT)
                    act.wait_ge(s_ok, h * NT)
                nc.scalar.activation(qe[:, :], B[:, h, :], ACT.Exp)
                nc.scalar.activation(eb[:, :], B[:, h, :].rearrange("p (t n) -> p t n", n=P)[:, :, P - 1], ACT.Exp).then_inc(ebe_ok, 1)

            for h in range(H):
                decays(h)
                act.wait_ge(lev_done, (h + 1) * (NLEV + 1))
                nc.scalar.activation(At[:, :], dir_ps[:, :], ACT.Copy).then_inc(dir_ok, 1)
                for half in range(2):
                    act.wait_ge(kd_turned, 2 * h + half + 1)
                    nc.scalar.activation(kdT[:, half * 512:(half + 1) * 512], k_ps[:, :], ACT.Copy).then_inc(kd_copied, 1)
                for half in range(2):
                    act.wait_ge(o_done, h * NT + 4 * (half + 1))
                    nc.scalar.activation(g.ot[:, 4 * half:4 * half + 4, h * P:(h + 1) * P],
                                         o_ps[:, :].rearrange("p (t d) -> p t d", t=4), ACT.Copy).then_inc(o_copied, 1)

        @block.gpsimd
        def _(pool):
            for h in range(H):
                for n, s in enumerate(PL):
                    e = h * (NLEV + 1) + n
                    pool.wait_ge(e_ok, e + 1)
                    if e == 0:
                        pool.wait_ge(scan_ok, 2 * H + 1)
                    m = M[:, e % 3, :].rearrange("p (b s) -> p b s", s=2 * s)
                    k = kin[:, h, :].rearrange("p (b s) -> p b s", s=2 * s)
                    nc.gpsimd.tensor_tensor(m[:, :, 0:s], m[:, :, 0:s], k[:, :, 0:s], ALU.mult).then_inc(mk_ok, 1)

        @block.vector
        def _(dve):
            own = g.dve
            raw = g.rT[:, 80:88].rearrange("p (l h) -> p l h", h=H)
            own.done(dve, nc.vector.tensor_tensor(lm[:, :], raw[:, 0, :], raw[:, 1, :], ALU.max))
            nc.vector.tensor_tensor(lb[:, :, :], raw, spread(lm[:, :], 1, 2), ALU.subtract).then_inc(lb_e, 1)
            nc.vector.memset(dir_ps[:, :], 0.0).then_inc(zero_ok, 1)
            nc.vector.memset(S[:, 0, :], 0.0).then_inc(zero_ok, 1)
            dve.wait_ge(lb_e, 2)
            own.done(dve, nc.vector.tensor_tensor(lsum[:, :], lb[:, 0, :], lb[:, 1, :], ALU.add))
            own.done(dve, nc.vector.reciprocal(lsum[:, :], lsum[:, :]))
            own.done(dve, nc.vector.tensor_tensor(lb[:, 0, :], lb[:, 0, :], lsum[:, :], ALU.mult))
            nc.vector.tensor_scalar(oml[:, :], lb[:, 0, :], -1.0, 1.0, ALU.mult, ALU.add).then_inc(lb_ok, 1)
            for t in range(NT + 1):
                n = P if t < NT else ST
                dve.wait_ge(x_turned, t + 1)
                src = (win_ps[:, 4 * (t % 2):4 * (t % 2) + 2, :].rearrange("p a c -> p (a c)")[:, 0:H * n]
                       .rearrange("p (h n) -> p h n", h=H))
                dst = q[:, :, t * P:(t + 1) * P] if t < NT else qs[:, :, :]
                nc.vector.tensor_scalar(dst, src, P ** -0.5, None, ALU.mult).then_inc(q_copied, 1)
            dve.wait_ge(f_copied, NT + 1)
            dve.wait_ge(lb_ok, 1)
            dve.wait_ge(reset_in, 16)
            for h in range(H):
                for m in (kin, ks):
                    ins = nc.vector.tensor_scalar(m[:, h, :], m[:, h, :], oml[:, h:h + 1], None, ALU.mult)
                if h == H - 1:
                    ins.then_inc(scan_ok, 1)
            for h in range(H):
                dve.wait_ge(log_ok, h + 1)
                for m, r0, r1 in ((B, 0, SEQ), (Bs, SEQ, SEQ + ST)):
                    nc.vector.tensor_tensor_scan(m[:, h, :], reset[:, r0:r1], m[:, h, :], 0.0, ALU.mult, ALU.add).then_inc(scan_ok, 1)
            dve.wait_ge(scan_ok, 2 * H + 1)

            def differences(h, n):
                e = h * (NLEV + 1) + n
                if e >= 3:
                    dve.wait_ge(lev_done, (e - 3) + 1)
                if n < NLEV:
                    s = PL[n]
                    b = B[:, h, :].rearrange("p (b s) -> p b s", s=2 * s)
                    nc.vector.tensor_tensor(M[:, e % 3, :].rearrange("p (b s) -> p b s", s=2 * s), b,
                                            spread(b[:, :, s - 1], 2, 2 * s), ALU.subtract).then_inc(d_ok, 1)
                else:
                    b = B[:, h, :].rearrange("p (t n) -> p t n", n=P)
                    nc.vector.tensor_tensor(M[:, e % 3, :].rearrange("p (t n) -> p t n", n=P),
                                            spread(b[:, :, P - 1], 2, P), b, ALU.subtract).then_inc(d_ok, 1)

            def queries(h, n):
                e = h * (NLEV + 1) + n
                dve.wait_ge(e_ok, e + 1)
                if n < NLEV:
                    s = PL[n]
                    m = M[:, e % 3, :].rearrange("p (b s) -> p b s", s=2 * s)
                    qq = q[:, h, :].rearrange("p (b s) -> p b s", s=2 * s)
                    nc.vector.tensor_tensor(m[:, :, s:2 * s], m[:, :, s:2 * s], qq[:, :, s:2 * s], ALU.mult).then_inc(mq_ok, 1)
                else:
                    if h >= 1:
                        dve.wait_ge(kd_turned, 2 * h)
                    nc.vector.tensor_tensor(kd[:, :], M[:, e % 3, :], kin[:, h, :], ALU.mult).then_inc(kd_ok, 1)
                    dve.wait_ge(ebe_ok, h + 1)
                    nc.vector.tensor_tensor(qe[:, :], qe[:, :], q[:, h, :], ALU.mult).then_inc(qe_ok, 1)

            for h in range(H):
                differences(h, 0)
                for n in range(NLEV + 1):
                    if n < NLEV:
                        differences(h, n + 1)
                    queries(h, n)
                dve.wait_ge(lev_done, (h + 1) * (NLEV + 1))
                own.done(dve, nc.vector.tensor_tensor(wm[:, :, :], win_ps[:, :, 0:NL * 32],
                                                      spread(g.cst[:, C_WM:C_WM + NL * 32], 1, NT), ALU.mult))
                nc.vector.tensor_reduce(ws[:, :, :], wm[:, :, :].rearrange("p t (l c) -> p t c l", l=NL), AX.X,
                                        ALU.add).then_inc(win_ok, 1)
                dve.wait_ge(win_ok, h + 1)
                dve.wait_ge(dir_ok, h + 1)
                for w in range(4):
                    rows = slice(32 * w, 32 * w + 32)
                    ins = nc.vector.tensor_copy(At[rows, :].rearrange("p (t n) -> p t n", n=P)[:, :, 32 * w:32 * w + 32],
                                                ws[rows, :, :])
                ins.then_inc(at_ok, 1)
                for t in range(NT):
                    dve.wait_ge(ds_done, h + 1)
                    if t >= 1:
                        dve.wait_ge(s_ok, h * NT + t)
                    if h >= 1:
                        if t == 0:
                            dve.wait_ge(o_done, h * NT)
                            dve.wait_ge(st_out, 16 * h)
                    nc.vector.scalar_tensor_tensor(S[:, t + 1, :], S[:, t, :], eb[:, t:t + 1],
                                                   win_ps[:, t, 0:P], ALU.mult, ALU.add).then_inc(s_ok, 1)

        @block.tensor
        def _(pe):
            pe.wait_ge(zero_ok, 2)
            for t in range(NT + 1):
                n = P if t < NT else ST
                pe.wait_ge(x_in[t % 2], 16 * (t // 2 + 1))
                if t >= 2:
                    pe.wait_ge(q_copied, t - 1)
                    pe.wait_ge(f_copied, t - 1)
                for part in range(2):
                    bank = win_ps[:, 4 * (t % 2) + 2 * part:4 * (t % 2) + 2 * part + 2, :].rearrange("p a c -> p (a c)")
                    for h in range(H):
                        ins = nc.tensor.transpose(bank[:, h * n:(h + 1) * n], x[0:n, t % 2, part * SEC + h * P:part * SEC + (h + 1) * P],
                                                  g.ident[0:n, 0:n])
                ins.then_inc(x_turned, 1)
            pe.wait_ge(q_copied, NT + 1)
            pe.wait_ge(f_copied, NT + 1)
            pe.wait_ge(scan_ok, 2 * H + 1)
            for h in range(H):
                if h >= 1:
                    pe.wait_ge(s_ok, h * NT)
                    pe.wait_ge(dir_ok, h)
                for n, s in enumerate(PL):
                    e = h * (NLEV + 1) + n
                    pe.wait_ge(mk_ok, h * NLEV + n + 1)
                    pe.wait_ge(mq_ok, h * NLEV + n + 1)
                    for t in range(NT):
                        m = M[:, e % 3, t * P:(t + 1) * P]
                        if s >= 32:
                            for b in range(P // (2 * s)):
                                j0 = 2 * s * b
                                ins = nc.tensor.matmul(dir_ps[j0:j0 + s, t * P + j0 + s:t * P + j0 + 2 * s], m[:, j0:j0 + s],
                                                       m[:, j0 + s:j0 + 2 * s], start=True, stop=True)
                        else:
                            for w in range(4):
                                ins = nc.tensor.matmul(win_ps[32 * w:32 * w + 32, t, (n - 2) * 32:(n - 1) * 32],
                                                       m[:, 32 * w:32 * w + 32], m[:, 32 * w:32 * w + 32], start=True, stop=True)
                    ins.then_inc(lev_done, 1)
                for t in range(NT):
                    for w in range(4):
                        c0 = t * P + 32 * w
                        ins = nc.tensor.matmul(win_ps[32 * w:32 * w + 32, t, (NL - 1) * 32:NL * 32], kin[:, h, c0:c0 + 32],
                                               q[:, h, c0:c0 + 32], start=True, stop=True)
                ins.then_inc(lev_done, 1)
                pe.wait_ge(kd_ok, h + 1)
                for half in range(2):
                    if half:
                        pe.wait_ge(kd_copied, 2 * h + 1)
                    for t in range(4):
                        c0 = (4 * half + t) * P
                        last = nc.tensor.transpose(k_ps[:, t * P:(t + 1) * P], kd[:, c0:c0 + P], g.ident)
                    last.then_inc(kd_turned, 1)
                pe.wait_ge(at_ok, h + 1)
                pe.wait_ge(qe_ok, h + 1)
                pe.wait_ge(kd_copied, 2 * h + 2)
                pe.wait_ge(v_in[h % 2], 16 * (h // 2 + 1))
                for t in range(NT):
                    ins = nc.tensor.matmul(win_ps[:, t, 0:P], kdT[:, t * P:(t + 1) * P], v[:, h % 2, t, :],
                                           start=True, stop=True)
                ins.then_inc(ds_done, 1)
                for t in range(NT):
                    if t == 0 and h >= 1:
                        pe.wait_ge(o_copied, 2 * h)
                    if t == 4:
                        pe.wait_ge(o_copied, 2 * h + 1)
                    col = (t % 4) * P
                    nc.tensor.matmul(o_ps[:, col:col + P], At[:, t * P:(t + 1) * P], v[:, h % 2, t, :], start=True, stop=False)
                    if t >= 1:
                        pe.wait_ge(s_ok, h * NT + t)
                    nc.tensor.matmul(o_ps[:, col:col + P], qe[:, t * P:(t + 1) * P], S[:, t, :], start=False, stop=True).then_inc(o_done, 1)
        stage.close()

        s_in, v_s_in, st_s_out = sem("rs_st_in"), sem("rs_v_in"), sem("rs_st_out")
        names = "zero d_ok e_ok m_ok lev_done win_ok at_ok kd_turned kd_copied kdm_ok ds_done s_ok o_done o_copied"
        (zero, d_ok, e_ok, m_ok, lev_done, win_ok, at_ok, kd_turned, kd_copied, kdm_ok, ds_done, s_ok, o_done,
         o_copied) = (sem("rs_" + n) for n in names.split())
        n_sl = len(SL) + 1
        W = H * ST
        wide = q[:, 0:2, :].rearrange("p h n -> p (h n)")
        st = kin[:, :, :].rearrange("p h n -> p (h n)").rearrange("p (b h d) -> p b h d", b=NB, h=H)
        kdm = B[:, :, :].rearrange("p h n -> p (h n)").rearrange("p (b n) -> p b n", b=NB)
        vs = x[:, 0, 0:SEC]
        kdt = x[:, 1, 0:SEC]
        qflat, kflat, bflat = (m[:, :, :].rearrange("p h n -> p (h n)") for m in (qs, ks, Bs))
        kend, qdec, ends = M[:, 0, W:2 * W], M[:, 1, W:2 * W], M[:, 2, W:W + H * NB]
        masks = g.cst[0:ST, C_WM + 32 * LEVELS.index(SL[0]):C_WM + 32 * LEVELS.index(SL[0]) + 32 * n_sl]
        stage = ExitStack()
        block = stage.enter_context(nc.Block())

        @block.sync
        def _(sp):
            for b in range(NB):
                sp.dma_start(st[:, b, :, :], a["state_hgrn"].rearrange("l b h k v -> (l b) k h v")[b]).then_inc(s_in, 16)
            sp.wait_ge(zero, 3)
            sp.dma_start(vs[0:ST, :], g.proj_d[SEQ:SEQ + ST, IA * SEC:(IA + 1) * SEC]).then_inc(v_s_in, 16)
            sp.wait_ge(s_ok, NB * H)
            sp.dma_start(g.s_sample.rearrange("l b h k v -> k (l b h) v"), st.rearrange("p b h d -> p (b h) d")).then_inc(st_s_out, 16)
            sp.wait_ge(st_s_out, 16)

        @block.gpsimd
        def _(pool):
            nc.gpsimd.memset(vs, 0.0).then_inc(zero, 1)
            nc.gpsimd.memset(At[:, 0:W], 0.0).then_inc(zero, 1)
            nc.gpsimd.memset(wide, 0.0).then_inc(zero, 1)
            pool.wait_ge(zero, 3)
            nc.gpsimd.memset(kdm[ST:P, :, :], 0.0).then_inc(zero, 1)

        @block.scalar
        def _(act):
            for n, s in enumerate(SL):
                act.wait_ge(d_ok, n + 1)
                m = M[:, n, 0:W].rearrange("p (b s) -> p b s", s=2 * s)
                nc.scalar.activation(m[:, :, 0:s], m[:, :, 0:s], ACT.Exp, scale=-1.0)
                nc.scalar.activation(m[:, :, s:2 * s], m[:, :, s:2 * s], ACT.Exp).then_inc(e_ok, 1)
            act.wait_ge(d_ok, len(SL) + 1)
            nc.scalar.activation(kend, kend, ACT.Exp).then_inc(e_ok, 1)
            nc.scalar.activation(qdec, bflat, ACT.Exp).then_inc(e_ok, 1)
            nc.scalar.activation(ends, bflat.rearrange("p (b q) -> p b q", q=QS)[:, :, QS - 1], ACT.Exp).then_inc(e_ok, 1)
            act.wait_ge(kd_turned, 1)
            nc.scalar.activation(kdt[0:ST, :], k_ps[0:ST, :], ACT.Copy).then_inc(kd_copied, 1)
            act.wait_ge(o_done, 1)
            nc.scalar.activation(g.ot[0:ST, NT, :], o_ps[0:ST, :], ACT.Copy).then_inc(o_copied, 1)

        @block.vector
        def _(dve):
            own = g.dve
            for n, s in enumerate(SL):
                b = bflat.rearrange("p (b s) -> p b s", s=2 * s)
                nc.vector.tensor_tensor(M[:, n, 0:W].rearrange("p (b s) -> p b s", s=2 * s), b,
                                        spread(b[:, :, s - 1], 2, 2 * s), ALU.subtract).then_inc(d_ok, 1)
            b = bflat.rearrange("p (b q) -> p b q", q=QS)
            nc.vector.tensor_tensor(kend.rearrange("p (b q) -> p b q", q=QS), spread(b[:, :, QS - 1], 2, QS), b,
                                    ALU.subtract).then_inc(d_ok, 1)
            for n, s in enumerate(SL):
                dve.wait_ge(e_ok, n + 1)
                m, kk, qq = (z.rearrange("p (b s) -> p b s", s=2 * s) for z in (M[:, n, 0:W], kflat, qflat))
                nc.vector.tensor_tensor(m[:, :, 0:s], m[:, :, 0:s], kk[:, :, 0:s], ALU.mult)
                nc.vector.tensor_tensor(m[:, :, s:2 * s], m[:, :, s:2 * s], qq[:, :, s:2 * s], ALU.mult).then_inc(m_ok, 1)
            dve.wait_ge(e_ok, len(SL) + 3)
            nc.vector.tensor_tensor(kend, kend, kflat, ALU.mult).then_inc(m_ok, 1)
            dve.wait_ge(zero, 4)
            diagonal = bass.AP(wide.tensor, wide.offset, [list(wide.ap[0]), [NB * ST, H], [ST + QS, NB], [1, QS]])
            nc.vector.tensor_tensor(diagonal, qdec.rearrange("p (h b q) -> p h b q", h=H, q=QS),
                                    qflat.rearrange("p (h b q) -> p h b q", h=H, q=QS), ALU.mult).then_inc(m_ok, 1)
            dve.wait_ge(lev_done, 1)
            own.done(dve, nc.vector.tensor_tensor(wm[0:ST, 0:H, 0:32 * n_sl], win_ps[0:ST, 0:H, 0:32 * n_sl],
                                                  spread(masks, 1, H), ALU.mult))
            own.done(dve, nc.vector.tensor_reduce(
                ws[0:ST, 0:H, :], wm[0:ST, 0:H, 0:32 * n_sl].rearrange("p h (l c) -> p h c l", l=n_sl), AX.X, ALU.add))
            for w in range(2):
                rows = slice(32 * w, 32 * w + 32)
                ins = nc.vector.tensor_copy(At[rows, 0:W].rearrange("p (h n) -> p h n", h=H)[:, :, 32 * w:32 * w + 32],
                                            ws[rows, 0:H, :])
            ins.then_inc(at_ok, 1)
            dve.wait_ge(kd_copied, 1)
            nc.vector.tensor_tensor(kdm[0:ST, :, :], spread(kdt[0:ST, :], 1, NB),
                                    spread(g.cst[0:ST, C_BM:C_BM + NB], 2, SEC), ALU.mult).then_inc(kdm_ok, 1)
            dve.wait_ge(o_done, 1)
            for b in range(NB):
                dve.wait_ge(ds_done, b + 1)
                for h in range(H):
                    nc.vector.scalar_tensor_tensor(st[:, b, h, :], st[:, b, h, :], ends[:, h * NB + b:h * NB + b + 1],
                                                   dir_ps[:, (b % 2) * 512 + h * P:(b % 2) * 512 + (h + 1) * P],
                                                   ALU.mult, ALU.add).then_inc(s_ok, 1)

        @block.tensor
        def _(pe):
            for n in range(n_sl):
                if n < len(SL):
                    pe.wait_ge(m_ok, n + 1)
                for h in range(H):
                    for w in range(2):
                        c0 = h * ST + 32 * w
                        left, right = (M[:, n, c0:c0 + 32],) * 2 if n < len(SL) else (kflat[:, c0:c0 + 32], qflat[:, c0:c0 + 32])
                        ins = nc.tensor.matmul(win_ps[32 * w:32 * w + 32, h, 32 * n:32 * n + 32], left, right, start=True, stop=True)
            ins.then_inc(lev_done, 1)
            pe.wait_ge(m_ok, len(SL) + 1)
            for h in range(H):
                ins = nc.tensor.transpose(k_ps[0:ST, h * P:(h + 1) * P], kend[:, h * ST:(h + 1) * ST], g.ident)
            ins.then_inc(kd_turned, 1)
            pe.wait_ge(v_s_in, 16)
            pe.wait_ge(s_in, 16 * NB)
            pe.wait_ge(at_ok, 1)
            pe.wait_ge(m_ok, len(SL) + 2)
            for h in range(H):
                nc.tensor.matmul(o_ps[0:ST, h * P:(h + 1) * P], At[:, h * ST:(h + 1) * ST], vs[:, h * P:(h + 1) * P],
                                 start=True, stop=False)
                for b in range(NB):
                    c0 = (h * NB + b) * ST
                    ins = nc.tensor.matmul(o_ps[0:ST, h * P:(h + 1) * P], wide[:, c0:c0 + ST], st[:, b, h, :],
                                           start=False, stop=(b == NB - 1))
            ins.then_inc(o_done, 1)
            pe.wait_ge(kdm_ok, 1)
            for b in range(NB):
                if b >= 2:
                    pe.wait_ge(s_ok, H * (b - 1))
                for h in range(H):
                    ins = nc.tensor.matmul(dir_ps[:, (b % 2) * 512 + h * P:(b % 2) * 512 + (h + 1) * P],
                                           kdm[:, b, h * P:(h + 1) * P], vs[:, h * P:(h + 1) * P], start=True, stop=True)
                ins.then_inc(ds_done, 1)
        stage.close()


def output(nc, g):
    a = g.a
    x_p = a["x_prompt"].rearrange("a (t p) d -> (a t) p d", p=P)
    x_s = a["x_sample"].rearrange("b q d -> (b q) d")
    y_p = g.y_prompt.rearrange("a (t p) d -> (a t) p d", p=P)
    y_s = g.y_sample.rearrange("b q d -> (b q) d")
    w_out = a["w_out"].rearrange("l (k p) n -> (l p) k n", p=P)
    with ExitStack() as here:
        sb, pb = tensors(nc, here)
        sem = semaphores(nc, here)
        WO = sb("f_W", [P, KT_N, DM])
        gz = sb("f_gz", [P, NT + 1, 2, SEC])
        sg = sb("f_sg", [P, NT + 1, 2, SEC])
        xr = sb("f_x", [P, 2, DM])
        y = sb("f_y", [P, 2, DM])
        junk = sb("f_junk", [P, H, P])
        ssq, lns, rs = sb("f_ssq", [P, (NT + 1) * H]), sb("f_ln", [P, H]), sb("f_rs", [P, (NT + 1) * H])
        gate = sb("f_gate", [P, 2, DM])
        p_ps = pb("f_ps", [P, 2, DM])
        t_ps = pb("f_tps", [P, 2, SEC])
        g_ps = pb("f_gps", [P, 2, SEC])
        z_in, w_in = sem("oz_in"), sem("ow_in")
        x_in, y_out = [sem("ox_in0"), sem("ox_in1")], [sem("oy_out0"), sem("oy_out1")]
        names = "sg_ok gp_t gp_ok gated ss_ok rs_ok y_ok turned yT_ok done added"
        (sg_ok, gp_t, gp_ok, gated, ss_ok, rs_ok, y_ok, turned, yT_ok, done, added) = (sem("f_" + n) for n in names.split())
        block = here.enter_context(nc.Block())
        rows = [P] * NT + [ST]

        @block.sync
        def _(sp):
            for t, n in enumerate(rows):
                sp.dma_start(gz[0:n, t, :, :].rearrange("p a d -> p (a d)"),
                             g.proj_d[t * P:t * P + n, GA * SEC:(ZA + 1) * SEC]).then_inc(z_in, 16)
            sp.dma_start(WO[:, :, :], w_out).then_inc(w_in, 16)
            for t, n in enumerate(rows):
                if t >= 2:
                    sp.wait_ge(added, t - 1)
                sp.dma_start(xr[0:n, t % 2, :], x_p[t] if t < NT else x_s).then_inc(x_in[t % 2], 16)
            for b in range(2):
                sp.wait_ge(y_out[b], 16 * ((NT + 2 - b) // 2))

        @block.gpsimd
        def _(pool):
            for t, n in enumerate(rows):
                pool.wait_ge(added, t + 1)
                pool.dma_start(y_p[t] if t < NT else y_s, y[0:n, t % 2, :]).then_inc(y_out[t % 2], 16)

        @block.scalar
        def _(act):
            act.wait_ge(z_in, 16 * (NT + 1))
            nc.scalar.activation(sg[:, 0:NT, :, :], gz[:, 0:NT, :, :], ACT.Sigmoid).then_inc(sg_ok, 1)
            nc.scalar.activation(sg[0:ST, NT, :, :], gz[0:ST, NT, :, :], ACT.Sigmoid).then_inc(sg_ok, 1)
            for j in range(2):
                act.wait_ge(gp_t, j + 1)
                n = (P, ST)[j]
                nc.scalar.activation(gate[0:n, j, :], g_ps[0:n, :, :].rearrange("p a d -> p (a d)"), ACT.Copy).then_inc(gp_ok, 1)
            for t, n in enumerate(rows):
                act.wait_ge(gated, t + 1)
                for h in range(H):
                    ins = nc.scalar.activation(junk[0:n, h, :], g.ot[0:n, t, h * P:(h + 1) * P], ACT.Square,
                                               accum_out=ssq[0:n, t * H + h:t * H + h + 1])
                ins.then_inc(ss_ok, 1)
                act.wait_ge(ss_ok, t + 1)
                g.act.done(act, nc.scalar.activation(lns[0:n, :], ssq[0:n, t * H:(t + 1) * H], ACT.Ln,
                                                     bias=g.epsc[0:n, :], scale=1.0 / P))
                nc.scalar.activation(rs[0:n, t * H:(t + 1) * H], lns[0:n, :], ACT.Exp, scale=-0.5).then_inc(rs_ok, 1)
                act.wait_ge(turned, t + 1)
                nc.scalar.activation(g.yT[:, 0:4, t * P:t * P + n],
                                     t_ps[:, t % 2, 0:H * n].rearrange("p (h t) -> p h t", h=H), ACT.Copy).then_inc(yT_ok, 1)

        @block.vector
        def _(dve):
            own = g.dve

            def gates(t, n):
                nc.vector.tensor_tensor(g.ot[0:n, t, :], g.ot[0:n, t, :], sg[0:n, t, 0, :], ALU.mult).then_inc(gated, 1)

            def branch(t, n):
                z, s = gz[0:n, t, 1, :], sg[0:n, t, 1, :]
                o = g.ot[0:n, t, :]
                own.done(dve, nc.vector.tensor_tensor(z, z, s, ALU.mult))
                own.done(dve, nc.vector.tensor_tensor(z.rearrange("p (h d) -> p h d", h=H), z.rearrange("p (h d) -> p h d", h=H),
                                                      spread(g.hgw[0:n, :], 1, H), ALU.mult))
                dve.wait_ge(rs_ok, t + 1)
                own.done(dve, nc.vector.tensor_tensor(o.rearrange("p (h d) -> p h d", h=H), o.rearrange("p (h d) -> p h d", h=H),
                                                      spread(rs[0:n, t * H:(t + 1) * H], 2, P), ALU.mult))
                nc.vector.tensor_tensor(o, o, z, ALU.mult).then_inc(y_ok, 1)

            def residual(t, n):
                dve.wait_ge(done, t + 1)
                dve.wait_ge(x_in[t % 2], 16 * (t // 2 + 1))
                if t >= 2:
                    dve.wait_ge(y_out[t % 2], 16 * (t // 2))
                own.done(dve, nc.vector.tensor_tensor(y[0:n, t % 2, :], p_ps[0:n, t % 2, :], gate[0:n, t // NT, :], ALU.mult))
                nc.vector.tensor_tensor(y[0:n, t % 2, :], y[0:n, t % 2, :], xr[0:n, t % 2, :], ALU.add).then_inc(added, 1)

            dve.wait_ge(sg_ok, 2)
            gates(0, P)
            dve.wait_ge(gp_ok, 2)
            for t in range(NT + 2):
                if t + 1 <= NT:
                    gates(t + 1, rows[t + 1])
                if t <= NT:
                    branch(t, rows[t])
                if t >= 1:
                    residual(t - 1, rows[t - 1])

        @block.tensor
        def _(pe):
            for j, (c0, n) in enumerate(((C_GP, P), (C_GS, ST))):
                if j:
                    pe.wait_ge(gp_ok, 1)
                for half in range(2):
                    ins = nc.tensor.matmul(g_ps[0:n, half, :], g.cst[:, c0 + half * n:c0 + (half + 1) * n], g.mod[:, 1, :],
                                           start=True, stop=True)
                ins.then_inc(gp_t, 1)

            def turn(t, n):
                pe.wait_ge(y_ok, t + 1)
                if t >= 2:
                    pe.wait_ge(yT_ok, t - 1)
                for h in range(H):
                    ins = nc.tensor.transpose(t_ps[:, t % 2, h * n:(h + 1) * n], g.ot[0:n, t, h * P:(h + 1) * P], g.ident[0:n, 0:n])
                ins.then_inc(turned, 1)

            turn(0, P)
            pe.wait_ge(w_in, 16)
            for t, n in enumerate(rows):
                if t >= 2:
                    pe.wait_ge(added, t - 1)
                for n0 in range(2):
                    for k in (4, 5, 6, 7):
                        nc.tensor.matmul(p_ps[0:n, t % 2, n0 * 512:(n0 + 1) * 512], g.yT[:, k, t * P:t * P + n],
                                         WO[:, k, n0 * 512:(n0 + 1) * 512], start=(k == 4), stop=False)
                pe.wait_ge(yT_ok, t + 1)
                for n0 in range(2):
                    for k in (0, 1, 2, 3):
                        ins = nc.tensor.matmul(p_ps[0:n, t % 2, n0 * 512:(n0 + 1) * 512], g.yT[:, k, t * P:t * P + n],
                                               WO[:, k, n0 * 512:(n0 + 1) * 512], start=False, stop=(k == 3))
                ins.then_inc(done, 1)
                if t < NT:
                    turn(t + 1, rows[t + 1])


def constants():
    c = np.zeros((P, C_N), np.float32)
    p = np.arange(P)
    c[p, C_ID + p] = 1
    j, i, q = p // 32, p % 32 // QS, p % QS
    for gr in range(2):
        for z in range(2):
            c[p, C_SL + gr * P + 32 * (2 * gr + j // 2) + 16 * z + 8 * (j % 2) + q] = 1
    used = p % 32 < 16
    for h in range(H):
        rows = p[used & (p // 32 == h)]
        c[rows, C_SZ + h * 120 + 56 + rows % QS] = 1
    t = np.arange(32)
    jj = (p % 32)[:, None]
    for n, s in enumerate(LEVELS):
        c[:, C_WM + 32 * n:C_WM + 32 * n + 32] = ((jj // (2 * s) == t // (2 * s)) & (jj % (2 * s) < s)
                                                  & (t % (2 * s) >= s))
    c[:, C_WM + 160:C_WM + 192] = jj == t
    for half in range(2):
        c[32 * half, C_GP + half * P:C_GP + half * P + P] = 1
        for b in range(NB):
            c[32 * half + 1 + b, C_GS + half * ST + QS * b:C_GS + half * ST + QS * b + QS] = 1
    for b in range(NB):
        c[QS * b:QS * b + QS, C_BM + b] = 1
    c[0, C_ONE:C_ONE + 9] = 1
    c[:, C_LC] = p % 16 < 8
    c[:, C_LC + 1] = p % 16 >= 8
    return c


def buckets():
    d = DMAX - np.arange(DTAB)
    pos = np.maximum(d, 1).astype(np.float32)
    large = 16 + (np.log(pos / np.float32(16)) / np.float32(np.log(64.0)) * np.float32(16)).astype(np.int32)
    b = np.where(d < 16, d, np.minimum(large, 31))
    b = np.where(d < 0, 32, b)
    return (np.arange(33)[:, None] == b).astype(np.float32)


def resets():
    n = np.arange(SEQ + ST)
    return np.where(n < SEQ, n % P, n % QS).astype(bool).astype(np.float32)[None, :]


OUTS = [(1, SEQ, DM), (NB, QS, DM), (1, 1, SEQ, H, P), (1, 1, SEQ, H, P), (1, 1, H, P, P),
        (1, NB, QS, H, P), (1, NB, QS, H, P), (1, NB, H, P, P)]


def build(nc, arrays):
    a = {n: nc.dram_tensor(n, x.shape, mybir.dt.from_np(x.dtype), kind="ExternalInput").ap()
         for n, x in arrays.items()}
    outs = [nc.dram_tensor(f"out_{i}", s, F32, kind="ExternalOutput").ap() for i, s in enumerate(OUTS)]
    layer(nc, a, outs)


def host_arrays(inputs):
    arrays = {n: np.ascontiguousarray(x) for n, x in inputs.items()}
    arrays["constants"] = constants()
    arrays["buckets"] = buckets()
    arrays["resets"] = resets()
    arrays["masked"] = np.full((1, H), NEG, np.float32)
    return arrays


def kernel(**inputs):
    import concourse.bacc as bacc
    from concourse.bass_utils import run_bass_kernel_spmd

    nc = bacc.Bacc("TRN2", target_bir_lowering=False, num_devices=1)
    arrays = host_arrays(inputs)
    build(nc, arrays)
    r = run_bass_kernel_spmd(nc, [arrays], core_ids=[0])
    return tuple(r.results[0][f"out_{i}"] for i in range(len(OUTS)))
```

```python
import concourse.bass as bass
from concourse import mybir
from contextlib import ExitStack
import numpy as np

F32 = mybir.dt.float32
F32R = mybir.dt.float32r
I32 = mybir.dt.int32
U32 = mybir.dt.uint32
ALU = mybir.AluOpType
ACT = mybir.ActivationFunctionType
AX = mybir.AxisListType

P = 128
DM = 1024
KT_N = DM // P
SEQ = 1024
NT = SEQ // P
NB, QS = 8, 8
ST = NB * QS
H, DH = 4, 64
SEC = 512
HSEC = SEC // 2
D_IN = 9 * SEC
QA, FA, IA, GA, ZA, QB, KB, VB, ZB = range(9)
PAGES, PAGE = 32, 128
PAST = PAGES * PAGE
CH = 4
NCH = PAGES // CH
SROW = (PAGES + CH) * 32
SUSE = (PAGES + 1) * 32
EPS = 1e-6
LAMBDA_INIT = 0.2
NEG = -1e30
DMAX = PAST + QS - 1
DTAB = DMAX + P
TCH = (DTAB + 511) // 512
WA_RING = 3
HX = 3
PTAB = SEQ + P - 1
LEVELS = (16, 8, 4, 2, 1)

C_ID, C_SL, C_SZ, C_WM, C_GP, C_GS, C_BM, C_ONE, C_LC = 0, 128, 384, 864, 1056, 1312, 1440, 1448, 1480
C_N = 1482


def spread(view, axis, n):
    pattern = list(view.ap)
    pattern.insert(axis, (0, n))
    return bass.AP(view.tensor, view.offset, pattern)


class Shared:
    pass


class Own:

    def __init__(self, sem, base=0):
        self.sem, self.base, self.n = sem, base, 0

    def done(self, eng, ins):
        ins.then_inc(self.sem, 1)
        self.n += 1
        eng.wait_ge(self.sem, self.base + self.n)


def tensors(nc, stack):
    def sb(name, shape, dt=F32):
        return stack.enter_context(nc.sbuf_tensor(name, shape, dt))

    def pb(name, shape):
        return stack.enter_context(nc.psum_tensor(name, shape, F32))
    return sb, pb


def semaphores(nc, stack):
    made = []

    def clear():
        nc.clear_and_free_semaphores(made)
        nc.all_engine_barrier()

    def sem(name):
        made.append(nc.alloc_semaphore(name=name))
        return made[-1]
    stack.callback(clear)
    return sem


def layer(nc, a, outs):
    with ExitStack() as whole:
        g = Shared()
        g.a = a
        g.y_prompt, g.y_sample, g.k_prompt, g.v_prompt, g.s_prompt, g.k_sample, g.v_sample, g.s_sample = outs
        g.w_sec = a["w_in"].rearrange("l (k p) n -> (l p) k n", p=P)
        g.ks_rows = g.k_sample.rearrange("l b q h d -> (l b q) (h d)")
        g.vs_rows = g.v_sample.rearrange("l b q h d -> (l b q) (h d)")
        g.proj_d = nc.dram_tensor("proj_scratch", [SEQ + ST, D_IN], F32, kind="Internal").ap()
        g.tab_d = nc.dram_tensor("bias_scratch", [H, TCH * 512], F32, kind="Internal").ap()
        g.tabs_d = nc.dram_tensor("sample_bias_scratch", [QS, H, DTAB], F32, kind="Internal").ap()
        g.tabp_d = nc.dram_tensor("prompt_bias_scratch", [P, H, PTAB], F32, kind="Internal").ap()
        g.q_d = nc.dram_tensor("query_scratch", [NB, P, 512], F32, kind="Internal").ap()
        sb, _ = tensors(nc, whole)
        g.cst = sb("cst", [P, C_N])
        g.ident = g.cst[:, C_ID:C_ID + P]
        g.mod = sb("mod", [P, 2, 512])
        g.rT = sb("rT", [P, P])
        g.wqk = sb("wqk", [P, 2, DH])
        g.subw = sb("subw", [P, P])
        g.hgw = sb("hgw", [P, P])
        g.nlam = sb("nlam", [P, 1])
        g.lamc = sb("lamc", [P, 1])
        g.epsc = sb("epsc", [P, 1])
        g.Oall = sb("Oall", [P, NB, P])
        g.dve = Own(whole.enter_context(nc.semaphore("own_dve")))
        g.act = Own(whole.enter_context(nc.semaphore("own_act")))
        with ExitStack() as inputs:
            sb, _ = tensors(nc, inputs)
            g.hTh = sb("hTh", [P, KT_N, SEQ], F32R)
            g.hTl = sb("hTl", [P, KT_N, SEQ], F32R)
            g.hS = sb("hS", [P, KT_N, 2 * ST], F32R)
            g.hSh, g.hSl = g.hS[:, :, 0:ST], g.hS[:, :, ST:2 * ST]
            g.Wraw = sb("Wraw", [P, KT_N, HSEC])
            g.w_early = inputs.enter_context(nc.semaphore("w_early"))
            g.w_low = inputs.enter_context(nc.semaphore("w_low"))
            g.tab_rows = inputs.enter_context(nc.semaphore("tab_rows"))
            setup(nc, g)
            with ExitStack() as both:
                sb, _ = tensors(nc, both)
                g.Wh = sb("Wh", [P, 2, KT_N, HSEC], F32R)
                g.Wl = sb("Wl", [P, 2, KT_N, HSEC], F32R)
                g.stage = sb("stage", [P, 3, HSEC])
                g.bias = sb("bias", [P, 2, SUSE])
                sample_projection(nc, g)
                main_loop(nc, g)
        with ExitStack() as ys:
            sb, _ = tensors(nc, ys)
            g.yT = sb("yT", [P, KT_N, SEQ + ST])
            g.ot = sb("ot", [P, NT + 1, SEC])
            prompt_attention(nc, g)
            g.WO = sb("WO", [P, KT_N // 2, DM])
            g.wo_in = ys.enter_context(nc.semaphore("wo_in"))
            recurrence(nc, g)
            output(nc, g)


def split_product(nc, out, high, low, w_high, w_low):
    for k in range(KT_N):
        nc.tensor.matmul(out, high(k), w_high(k), start=(k == 0), stop=False)
        nc.tensor.matmul(out, high(k), w_low(k), start=False, stop=False)
        ins = nc.tensor.matmul(out, low(k), w_high(k), start=False, stop=(k == KT_N - 1))
    return ins


def setup(nc, g):
    a = g.a
    x_p = a["x_prompt"].rearrange("a (t p) d -> (a t) p d", p=P)
    x_s = a["x_sample"].rearrange("b q d -> (b q) d")
    w_ada = a["w_ada"].rearrange("l (k p) n -> (l k) p n", p=P)
    with ExitStack() as here:
        sb, pb = tensors(nc, here)
        sem = semaphores(nc, here)
        wa = sb("wa", [P, WA_RING, 3 * DM])
        xin = sb("xin", [P, NT + 1, DM])
        rows = sb("rows", [P, P])
        silu_c = sb("silu_c", [P, KT_N, 32])
        sig_c = sb("sig_c", [P, 72])
        hot = sb("hot", [P, DTAB])
        rel = sb("rel", [P, H])
        tab = hot[64:64 + H, :]
        bada = hot[96:P, 0:3 * DM]
        modT = sb("modT", [P, 2, 4, P])
        amp = sb("amp", [P, KT_N, 9])
        shf = sb("shf", [P, KT_N, 9])
        lamv = sb("lamv", [P, 4, DH])
        lamp = sb("lamp", [P, 2, DH])
        lamd = sb("lamd", [P, 2])
        lame = sb("lame", [P, 2])
        ssq = sb("ssq", [P, NT + 1])
        lnx = sb("lnx", [P, NT + 1])
        rsx = sb("rsx", [P, NT + 1])
        tmpS = sb("tmpS", [P, KT_N, ST])
        hx = sb("hx", [P, HX, KT_N, P])
        junk = hx[:, 0, :, :].rearrange("p k n -> p (k n)")
        ada_ps = pb("ada_ps", [P, 2, 512])
        x_ps = pb("x_ps", [P, 2, DM])
        m_ps = pb("m_ps", [P, 2, 512])

        zeroed, bada_in = sem("zeroed"), sem("bada_in")
        cst_in, small_in, lam_in, hot_in = sem("cst_in"), sem("small_in"), sem("lam_in"), sem("hot_in")
        wa_in = [sem(f"wa_in{i}") for i in range(WA_RING)]
        x_in = [sem(f"x_in{t}") for t in range(NT + 1)]
        rows_t, rT_ok, silu_ok, wa_used = sem("rows_t"), sem("rT_ok"), sem("silu_ok"), sem("wa_used")
        tab_t, tab_ok, tab_out = sem("tab_t"), sem("tab_ok"), sem("tab_out")
        ada_t, mod_ok, modT_t, modT_ok, amp_ok = sem("ada_t"), sem("mod_ok"), sem("modT_t"), sem("modT_ok"), sem("amp_ok")
        sq_ok, xn_ok, x_t, hT_dve, hT_act, high_ok, low_ok, lamd_ok, lame_ok = (sem(n) for n in (
            "sq_ok", "xn_ok", "x_t", "hT_dve", "hT_act", "high_ok", "low_ok", "lamd_ok", "lame_ok"))

        block = here.enter_context(nc.Block())

        @block.sync
        def _(sp):
            sp.dma_start(g.cst[:, :], a["constants"]).then_inc(cst_in, 16)
            sp.wait_ge(zeroed, 1)
            sp.dma_start(rows[0:8, :], a["c_prompt"].rearrange("b (k p) -> (b k) p", p=P)).then_inc(small_in, 16)
            sp.dma_start(rows[8:72, :], a["c_sample"].rearrange("b (k p) -> (b k) p", p=P)).then_inc(small_in, 16)
            sp.dma_start(rows[72:80, :], a["norm_w"].rearrange("b (k p) -> (b k) p", p=P)).then_inc(small_in, 16)
            sp.dma_start(rows[80:88, :], a["lb_param"].rearrange("b (k p) -> (b k) p", p=P)).then_inc(small_in, 16)
            sp.wait_ge(zeroed, 3)
            sp.dma_start(hot[96:97, 0:3 * DM], a["b_ada"]).then_inc(bada_in, 16)
            for k in range(KT_N):
                if k >= WA_RING:
                    sp.wait_ge(wa_used, k - WA_RING + 1)
                sp.dma_start(wa[:, k % WA_RING, :], w_ada[k]).then_inc(wa_in[k % WA_RING], 16)
                if k < 4:
                    for t in (2 * k, 2 * k + 1):
                        sp.dma_start(xin[:, t, :], x_p[t]).then_inc(x_in[t], 16)
                if k == 3:
                    sp.dma_start(xin[0:ST, NT, :], x_s).then_inc(x_in[NT], 16)
            sp.dma_start(g.Wraw[:, :, :], g.w_sec[:, :, QB * SEC:QB * SEC + HSEC]).then_inc(g.w_early, 16)
            sp.wait_ge(tab_out, 16)
            sp.dma_start(g.tabs_d, spread(g.tab_d[:, 0:DTAB], 0, QS)).then_inc(g.tab_rows, 16)
            sp.dma_start(g.tabp_d, spread(g.tab_d[:, DTAB - PTAB:DTAB], 0, P)).then_inc(g.tab_rows, 16)

        @block.gpsimd
        def _(pool):
            nc.gpsimd.memset(rows[:, :], 0.0).then_inc(zeroed, 1)
            nc.gpsimd.memset(rel[:, :], 0.0).then_inc(zeroed, 1)
            pool.wait_ge(zeroed, 2)
            nc.gpsimd.memset(bada, 0.0).then_inc(zeroed, 1)
            pool.wait_ge(zeroed, 3)
            nc.gpsimd.memset(hot[0:64, :], 0.0).then_inc(zeroed, 1)
            pool.wait_ge(zeroed, 4)
            nc.gpsimd.memset(silu_c[:, :, :], 0.0).then_inc(zeroed, 1)

        @block.scalar
        def _(act):
            act.wait_ge(zeroed, 2)
            act.dma_start(rel[0:32, :], a["rel_table"]).then_inc(hot_in, 16)
            act.dma_start(rel[32:33, :], a["masked"]).then_inc(hot_in, 16)
            act.wait_ge(zeroed, 4)
            act.dma_start(hot[0:33, :], a["buckets"]).then_inc(hot_in, 16)
            for j, name in enumerate(("lam_q1", "lam_k1", "lam_q2", "lam_k2")):
                act.dma_start(lamv[:, j, :], a[name].partition_broadcast(P)).then_inc(lam_in, 16)
            act.dma_start(g.wqk[:, 0, :], a["q_norm_w"].partition_broadcast(P)).then_inc(lam_in, 16)
            act.dma_start(g.wqk[:, 1, :], a["k_norm_w"].partition_broadcast(P)).then_inc(lam_in, 16)
            act.dma_start(g.subw[:, :], a["sub_norm_w"].partition_broadcast(P)).then_inc(lam_in, 16)
            act.dma_start(g.hgw[:, :], a["hg_norm_w"].partition_broadcast(P)).then_inc(lam_in, 16)
            act.wait_ge(rT_ok, 1)
            nc.scalar.activation(sig_c[:, :], g.rT[:, 0:72], ACT.Sigmoid).then_inc(silu_ok, 1)

            for t in range(NT + 1):
                n = P if t < NT else ST
                act.wait_ge(x_in[t], 16)
                g.act.done(act, nc.scalar.activation(junk[0:n, :], xin[0:n, t, :], ACT.Square,
                                                     accum_out=ssq[0:n, t:t + 1]))
            act.wait_ge(sq_ok, 1)
            g.act.done(act, nc.scalar.activation(lnx[:, :], ssq[:, :], ACT.Ln, bias=g.epsc[:, :], scale=1.0 / DM))
            g.act.done(act, nc.scalar.activation(rsx[:, :], lnx[:, :], ACT.Exp, scale=-0.5))
            for t in range(NT + 1):
                n = P if t < NT else ST
                nc.scalar.activation(xin[0:n, t, :], xin[0:n, t, :], ACT.Copy,
                                     scale=rsx[0:n, t:t + 1]).then_inc(xn_ok, 1)
            act.wait_ge(tab_ok, TCH)
            act.dma_start(g.tab_d[:, 0:DTAB], tab).then_inc(tab_out, 16)
            act.wait_ge(lamd_ok, 1)
            nc.scalar.activation(lame[:, :], lamd[:, :], ACT.Exp).then_inc(lame_ok, 1)
            act.wait_ge(amp_ok, 1)
            def high(t):
                act.wait_ge(hT_act, t + 1)
                act.wait_ge(hT_dve, t + 1)
                nc.scalar.activation(g.hTh[:, :, t * P:(t + 1) * P], hx[:, t % HX, :, :], ACT.Copy).then_inc(high_ok, 1)

            for t in range(NT):
                act.wait_ge(x_t, t + 1)
                if t >= HX:
                    act.wait_ge(low_ok, t - HX + 1)
                for k in range(4, KT_N):
                    ins = nc.scalar.activation(hx[:, t % HX, k, :], x_ps[:, t % 2, k * P:(k + 1) * P],
                                               ACT.Identity, bias=shf[:, k, 0:1], scale=amp[:, k, 0:1])
                ins.then_inc(hT_act, 1)
                if t >= 1:
                    high(t - 1)
            high(NT - 1)
            act.wait_ge(hT_dve, NT + 1)
            nc.scalar.activation(g.hSh[:, :, :], hx[:, NT % HX, :, 0:ST], ACT.Copy).then_inc(high_ok, 1)

        @block.vector
        def _(dve):
            own = g.dve
            nc.vector.memset(ssq[:, NT:NT + 1], 1.0)
            nc.vector.memset(g.epsc[:, :], EPS)
            nc.vector.memset(ada_ps[:, 1, :], 0.0).then_inc(sq_ok, 1)
            dve.wait_ge(rows_t, 1)
            nc.vector.tensor_copy(g.rT[:, :], m_ps[:, 0, 0:P]).then_inc(rT_ok, 1)
            dve.wait_ge(silu_ok, 1)
            dve.wait_ge(rT_ok, 1)
            dve.wait_ge(zeroed, 5)
            nc.vector.tensor_tensor(silu_c[:, :, 0:9], sig_c[:, :].rearrange("p (r k) -> p k r", k=KT_N),
                                    g.rT[:, 0:72].rearrange("p (r k) -> p k r", k=KT_N),
                                    ALU.mult).then_inc(silu_ok, 1)
            dve.wait_ge(lam_in, 16 * 8)
            dve.wait_ge(cst_in, 16)
            for j in range(2):
                own.done(dve, nc.vector.tensor_tensor_reduce(
                    out=lamp[:, j, :], in0=lamv[:, 2 * j, :], in1=lamv[:, 2 * j + 1, :], scale=1.0, scalar=0.0,
                    op0=ALU.mult, op1=ALU.add, accum_out=lamd[:, j:j + 1]))
            nc.vector.tensor_scalar(g.subw[:, :], g.subw[:, :], 1.0 - LAMBDA_INIT, None, ALU.mult).then_inc(lamd_ok, 1)
            for c in range(TCH):
                if c == KT_N:
                    dve.wait_ge(ada_t, 1)
                    nc.vector.tensor_copy(g.mod[:, :, :], ada_ps[:, :, :]).then_inc(mod_ok, 1)
                dve.wait_ge(tab_t, c + 1)
                n = min(512, DTAB - 512 * c)
                nc.vector.tensor_copy(tab[:, 512 * c:512 * c + n], m_ps[0:H, c % 2, 0:n]).then_inc(tab_ok, 1)
            for b in range(2):
                dve.wait_ge(modT_t, b + 1)
                own.done(dve, nc.vector.tensor_copy(modT[:, b, :, :], m_ps[:, b, :].rearrange("p (k c) -> p k c", c=P)))
            nw = g.rT[:, 72:80]
            for j in range(2):
                ks = slice(4 * j, 4 * j + 4)
                own.done(dve, nc.vector.tensor_scalar(amp[:, ks, :], modT[:, 0, :, 64 + 32 * j:73 + 32 * j],
                                                      1.0, None, ALU.add))
                own.done(dve, nc.vector.tensor_tensor(amp[:, ks, :], amp[:, ks, :], spread(nw[:, ks], 2, 9), ALU.mult))
                ins = nc.vector.tensor_copy(shf[:, ks, :], modT[:, 0, :, 32 * j:9 + 32 * j])
                if j == 0:
                    own.done(dve, ins)
            ins.then_inc(amp_ok, 1)
            dve.wait_ge(amp_ok, 1)

            def low(t):
                dve.wait_ge(high_ok, t + 1)
                if t < NT:
                    cols = slice(t * P, (t + 1) * P)
                    out, h, x = g.hTl[:, :, cols], g.hTh[:, :, cols], hx[:, t % HX, :, :]
                else:
                    out, h, x = g.hSl[:, :, :], g.hSh[:, :, :], hx[:, NT % HX, :, 0:ST]
                nc.vector.tensor_tensor(out, x, h.bitcast(F32), ALU.subtract).then_inc(low_ok, 1)

            for t in range(NT):
                dve.wait_ge(x_t, t + 1)
                if t >= HX:
                    dve.wait_ge(low_ok, t - HX + 1)
                for k in range(4):
                    ins = nc.vector.tensor_scalar(hx[:, t % HX, k, :], x_ps[:, t % 2, k * P:(k + 1) * P],
                                                  amp[:, k, 0:1], shf[:, k, 0:1], ALU.mult, ALU.add)
                ins.then_inc(hT_dve, 1)
                if t >= 1:
                    low(t - 1)
            low(NT - 1)
            dve.wait_ge(low_ok, NT)
            dve.wait_ge(x_t, NT + 1)
            own.done(dve, nc.vector.tensor_tensor(
                tmpS[:, :, :].rearrange("p k (b q) -> p k b q", q=QS),
                x_ps[:, 0, 0:512].rearrange("p (k b q) -> p k b q", k=KT_N, q=QS),
                spread(amp[:, :, 1:9], 3, QS), ALU.mult))
            nc.vector.tensor_tensor(
                hx[:, NT % HX, :, 0:ST].rearrange("p k (b q) -> p k b q", q=QS),
                tmpS[:, :, :].rearrange("p k (b q) -> p k b q", q=QS),
                spread(shf[:, :, 1:9], 3, QS), ALU.add).then_inc(hT_dve, 1)
            low(NT)
            dve.wait_ge(lame_ok, 1)
            own.done(dve, nc.vector.tensor_tensor(lamd[:, 0:1], lame[:, 1:2], lame[:, 0:1], ALU.subtract))
            own.done(dve, nc.vector.tensor_scalar(g.nlam[:, :], lamd[:, 0:1], LAMBDA_INIT, None, ALU.subtract))
            own.done(dve, nc.vector.tensor_tensor(g.lamc[:, :], g.nlam[:, :], g.cst[:, C_LC + 1:C_LC + 2], ALU.mult))
            own.done(dve, nc.vector.tensor_tensor(g.lamc[:, :], g.lamc[:, :], g.cst[:, C_LC:C_LC + 1], ALU.add))

        @block.tensor
        def _(pe):
            pe.wait_ge(cst_in, 16)
            pe.wait_ge(small_in, 64)
            nc.tensor.transpose(m_ps[:, 0, 0:P], rows[:, :], g.ident).then_inc(rows_t, 1)

            def table(c):
                if c >= 2:
                    pe.wait_ge(tab_ok, c - 1)
                n = min(512, DTAB - 512 * c)
                nc.tensor.matmul(m_ps[0:H, c % 2, 0:n], rel[0:64, :], hot[0:64, 512 * c:512 * c + n],
                                 start=True, stop=True).then_inc(tab_t, 1)

            pe.wait_ge(rT_ok, 1)
            pe.wait_ge(silu_ok, 2)
            pe.wait_ge(sq_ok, 1)
            for k in range(KT_N):
                pe.wait_ge(wa_in[k % WA_RING], 16 * (k // WA_RING + 1))
                for c in range(6):
                    ins = nc.tensor.matmul(ada_ps[32 * (c % 4):32 * (c % 4) + 32, c // 4, :], silu_c[:, k, :],
                                           wa[:, k % WA_RING, 512 * c:512 * c + 512], start=(k == 0), stop=False)
                ins.then_inc(wa_used, 1)
                if k == 0:
                    pe.wait_ge(hot_in, 48)
                table(k)
            pe.wait_ge(bada_in, 16)
            for c in range(6):
                ins = nc.tensor.matmul(ada_ps[32 * (c % 4):32 * (c % 4) + 32, c // 4, :],
                                       g.cst[96:P, C_ONE:C_ONE + 32], bada[:, 512 * c:512 * c + 512],
                                       start=False, stop=True)
            ins.then_inc(ada_t, 1)
            for c in range(KT_N, TCH):
                table(c)
            pe.wait_ge(mod_ok, 1)
            pe.wait_ge(tab_ok, TCH)
            for b in range(2):
                for k in range(4):
                    ins = nc.tensor.transpose(m_ps[:, b, k * P:(k + 1) * P], g.mod[:, b, k * P:(k + 1) * P], g.ident)
                ins.then_inc(modT_t, 1)
            pe.wait_ge(xn_ok, NT + 1)
            for t in range(NT):
                if t >= 2:
                    pe.wait_ge(hT_dve, t - 1)
                    pe.wait_ge(hT_act, t - 1)
                for k in range(KT_N):
                    ins = nc.tensor.transpose(x_ps[:, t % 2, k * P:(k + 1) * P], xin[:, t, k * P:(k + 1) * P], g.ident)
                ins.then_inc(x_t, 1)
            pe.wait_ge(hT_dve, NT - 1)
            pe.wait_ge(hT_act, NT - 1)
            for k in range(KT_N):
                ins = nc.tensor.transpose(x_ps[:, 0, k * ST:(k + 1) * ST], xin[0:ST, NT, k * P:(k + 1) * P],
                                          g.ident[0:ST, 0:ST])
            ins.then_inc(x_t, 1)


def sample_projection(nc, g):
    halves = [s * SEC + half * HSEC for s in (QB, KB, VB, ZB) for half in range(2)] + [0]
    with ExitStack() as here:
        sb, pb = tensors(nc, here)
        sem = semaphores(nc, here)
        proj = sb("s_proj", [ST, 3 * SEC])
        sq = sb("s_sq", [ST, 2 * SEC])
        qkn = sb("s_qkn", [ST, 2 * SEC])
        ssum, lns, rs = sb("s_ssum", [ST, 16]), sb("s_ln", [ST, 16]), sb("s_rs", [ST, 16])
        qT = sb("s_qT", [ST, SEC])
        qst = sb("s_qst", [P, NB, 16, 32])
        s_ps = pb("s_ps", [P, 2, SEC])
        p_ps = pb("p_ps", [P, 2, SEC])
        raws = [g.Wraw, sb("s_raw1", [P, KT_N, HSEC]), sb("s_raw2", [P, KT_N, HSEC])]
        w_raw = [sem(f"sw_raw{i}") for i in range(3)]
        w_high, w_low, bias_in = sem("sw_high"), sem("sw_low"), sem("bias_in")
        s_done, s_copied = sem("s_done"), sem("s_copied")
        z_done, z_copied, z_out = sem("z_done"), sem("z_copied"), [sem(f"z_out{i}") for i in range(3)]
        NU = 2 * (NT + 1)
        sum_ok, rs_ok, qkn_ok, qst0, qst_ok, stored = (sem(n) for n in (
            "sum_ok", "rs_ok", "qkn_ok", "qst0", "qst_ok", "s_stored"))
        block = here.enter_context(nc.Block())

        @block.sync
        def _(sp):
            for m in range(1, len(halves)):
                if m >= 3:
                    sp.wait_ge(w_low, m - 2)
                sp.dma_start(raws[m % 3][:, :, :], g.w_sec[:, :, halves[m]:halves[m] + HSEC]).then_inc(w_raw[m % 3], 16)
                if m == 7:
                    sp.wait_ge(qkn_ok, 1)
                    sp.dma_start(g.ks_rows, qkn[:, SEC:2 * SEC]).then_inc(stored, 16)
                    sp.wait_ge(s_copied, 6)
                    sp.dma_start(g.vs_rows, proj[:, 2 * SEC:3 * SEC]).then_inc(stored, 16)
                if m == 8:
                    sp.wait_ge(qst_ok, 8)
                    sp.dma_start(g.q_d.rearrange("b p n -> p b n"), qst[:, :, :, :].rearrange("p b j q -> p b (j q)")
                                 ).then_inc(stored, 16)
            sp.wait_ge(stored, 48)
            for i in range(3):
                sp.wait_ge(z_out[i], 16 * (NU // 3))

        @block.gpsimd
        def _(pool):
            nc.gpsimd.memset(qst[:, :, :, :], 0.0).then_inc(qst0, 1)

        @block.scalar
        def _(act):
            def high(m):
                if m == 0:
                    act.wait_ge(g.w_early, 16)
                else:
                    act.wait_ge(w_raw[m % 3], 16 * (m // 3 + (m % 3 > 0)))
                if 2 <= m <= 7:
                    act.wait_ge(s_done, m - 1)
                elif m == 8:
                    act.wait_ge(z_done, NU // 2)
                nc.scalar.activation(g.Wh[:, m % 2, :, :], raws[m % 3][:, :, :], ACT.Copy).then_inc(w_high, 1)

            high(0)
            high(1)
            for s in range(6):
                act.wait_ge(s_done, s + 1)
                nc.scalar.activation(proj[:, s * HSEC:(s + 1) * HSEC], s_ps[0:ST, s % 2, 0:HSEC], ACT.Copy).then_inc(s_copied, 1)
                high(s + 2)
                if s == 4:
                    act.wait_ge(sum_ok, 1)
                    g.act.done(act, nc.scalar.activation(lns[:, :], ssum[:, :], ACT.Ln, bias=g.epsc[0:ST, :], scale=1.0 / DH))
                    nc.scalar.activation(rs[:, :], lns[:, :], ACT.Exp, scale=-0.5).then_inc(rs_ok, 1)
            act.wait_ge(g.tab_rows, 32)
            loads = [(j, i, gr) for j in range(4) for i in range(4) for gr in range(2)]
            for u in range(NU):
                half, t = u // (NT + 1), u % (NT + 1)
                n = P if t < NT else ST
                act.wait_ge(z_done, u + 1)
                if u >= 3:
                    act.wait_ge(z_out[u % 3], 16 * (u // 3))
                nc.scalar.activation(g.stage[0:n, u % 3, :], p_ps[0:n, u % 2, 0:HSEC], ACT.Copy).then_inc(z_copied, 1)
                act.wait_ge(z_copied, u + 1)
                c0 = ZB * SEC + half * HSEC
                act.dma_start(g.proj_d[t * P:t * P + n, c0:c0 + HSEC], g.stage[0:n, u % 3, :]).then_inc(z_out[u % 3], 16)
                if u == NT + 2:
                    high(8)
                for j, i, gr in loads[u * 2:u * 2 + 2]:
                    first = g.tabs_d.offset + (2 * gr + j // 2) * DTAB + DMAX - PAST + 32 * i
                    row = 32 * j + QS * i
                    act.dma_start(g.bias[row:row + QS, gr, :].rearrange("p (n k) -> p n k", k=32),
                                  bass.AP(g.tabs_d.tensor, first, [[H * DTAB - 1, QS], [PAGE, PAGES + 1], [1, 32]])
                                  ).then_inc(bias_in, 16)
            act.wait_ge(bias_in, 16 * 32)

        @block.vector
        def _(dve):
            own = g.dve

            def low(m):
                dve.wait_ge(w_high, m + 1)
                nc.vector.tensor_tensor(g.Wl[:, m % 2, :, :], raws[m % 3][:, :, :], g.Wh[:, m % 2, :, :].bitcast(F32),
                                        ALU.subtract).then_inc(g.w_low if m == 8 else w_low, 1)

            own.done(dve, nc.vector.tensor_scalar(g.wqk[:, 0, :], g.wqk[:, 0, :], DH ** -0.5, None, ALU.mult))
            for m in range(6):
                low(m)
            dve.wait_ge(s_copied, 4)
            qk = proj[:, 0:2 * SEC]
            own.done(dve, nc.vector.tensor_tensor(sq[:, :], qk, qk, ALU.mult))
            nc.vector.tensor_reduce(ssum[:, :], sq[:, :].rearrange("p (n d) -> p n d", d=DH), AX.X,
                                    ALU.add).then_inc(sum_ok, 1)
            low(6)
            dve.wait_ge(rs_ok, 1)
            own.done(dve, nc.vector.tensor_tensor(
                sq[:, :].rearrange("p (n d) -> p n d", d=DH), qk.rearrange("p (n d) -> p n d", d=DH),
                spread(rs[:, :], 2, DH), ALU.mult))
            ins = nc.vector.tensor_tensor(
                qkn[:, :].rearrange("p (w n d) -> p w n d", w=2, d=DH),
                sq[:, :].rearrange("p (w n d) -> p w n d", w=2, d=DH), spread(g.wqk[0:ST, :, :], 2, 8), ALU.mult)
            ins.then_inc(qkn_ok, 1)
            low(7)
            dve.wait_ge(qkn_ok, 1)
            own.done(dve, nc.vector.transpose(qT[:, :].bitcast(U32), qkn[:, 0:SEC].bitcast(U32)))
            dve.wait_ge(qst0, 1)
            for i in range(4):
                for hi in range(2):
                    nc.vector.tensor_copy(
                        qst[32 * i:32 * i + 32, 4 * hi:4 * hi + 4, :, QS * i:QS * i + QS],
                        qT[32 * hi:32 * hi + 32, :].rearrange("p (j b q) -> p b j q", j=16, q=QS)).then_inc(qst_ok, 1)
            low(8)

        @block.tensor
        def _(pe):
            def weights(m):
                pe.wait_ge(w_low, m + 1)
                return (lambda k: g.Wh[:, m % 2, k, :]), (lambda k: g.Wl[:, m % 2, k, :])

            for m in range(6):
                if m >= 2:
                    pe.wait_ge(s_copied, m - 1)
                wh, wl = weights(m)
                split_product(nc, s_ps[0:ST, m % 2, 0:HSEC], lambda k: g.hSh[:, k, :], lambda k: g.hSl[:, k, :],
                              wh, wl).then_inc(s_done, 1)
            for u in range(NU):
                half, t = u // (NT + 1), u % (NT + 1)
                if t == 0:
                    wh, wl = weights(6 + half)
                if u >= 2:
                    pe.wait_ge(z_copied, u - 1)
                if t < NT:
                    split_product(nc, p_ps[:, u % 2, 0:HSEC], lambda k: g.hTh[:, k, t * P:(t + 1) * P],
                                  lambda k: g.hTl[:, k, t * P:(t + 1) * P], wh, wl).then_inc(z_done, 1)
                else:
                    split_product(nc, p_ps[0:ST, u % 2, 0:HSEC], lambda k: g.hSh[:, k, :], lambda k: g.hSl[:, k, :],
                                  wh, wl).then_inc(z_done, 1)


KT0, SC0, SE0, KX0, PT0, PTV0, PV0, PJ0, PE0, OE0, SP0, WL0 = 4, 12, 2, 1, 1, 2, 5, 16, 2, 1, 16, 1
PJR = 2 * (NT + 1)
RING = 4
KTR = 2


def main_loop(nc, g):
    a = g.a
    ck = a["cache_k"].rearrange("l n t h d -> (l n) t (h d)")
    cv = a["cache_v"].rearrange("l n (i k) h d -> (l n) k i (h d)", i=4)
    n_pool = ck.shape[0]
    ks_b = g.k_sample.rearrange("l b q h d -> (l b) q (h d)")
    vs_b = g.v_sample.rearrange("l b q h d -> (l b) q (h d)")
    with ExitStack() as here:
        sb, pb = tensors(nc, here)
        sem = semaphores(nc, here)
        pages = sb("pages", [1, NB * PAGES], I32)
        KV = sb("KV", [P, RING, CH, SEC])
        KT = sb("KT", [P, KTR, CH * SEC])
        kx = sb("kx", [32, SEC])
        kxT = sb("kxT", [P, SEC])
        vx = sb("vx", [P, SEC])
        Q = sb("Q", [P, 2, 512])
        S = sb("S", [P, 2, SROW])
        bias = g.bias
        mx = sb("mx", [P, 2, NCH + 1])
        m32, mT, mr, mE, mB = (sb(n, [P, 32]) for n in ("m32", "mT", "mr", "mE", "mB"))
        den = sb("den", [P, 2])
        PTs = sb("PTs", [P, 2, 2 * P])
        coef = sb("coef", [P, 2])
        lows = sb("lows", [ST, HSEC])
        low_out, summed = sem("low_out"), sem("summed")
        pj_ps = pb("pj_ps", [P, 2, SEC])
        sc_ps = pb("sc_ps", [P, 2, 512])
        pt_ps = pb("pt_ps", [P, 2, 512])
        o_ps = pb("o_ps", [P, 512])
        l_ps = pb("l_ps", [P, 512])

        pages_in, cleared = sem("pages_in"), sem("cleared")
        kv_in, kv_in_sw = [sem(f"kv_in{i}") for i in range(RING)], [sem(f"kv_in_sw{i}") for i in range(RING)]
        SLOT = 2 * NCH // RING
        w_raw, w_high, w_low, q_in = sem("w_raw"), sem("w_high"), g.w_low, [sem("q_in0"), sem("q_in1")]
        kx_in, vx_in = sem("kx_in"), sem("vx_in")
        transposed, kx_done = sem("transposed"), sem("kx_done")
        scored, biased, max_ok, exp_ok = sem("scored"), sem("biased"), sem("max_ok"), sem("exp_ok")
        p_turned, p_copied, pv_done, den_done, o_copied = (sem(n) for n in (
            "p_turned", "p_copied", "pv_done", "den_done", "o_copied"))
        projected, proj_copied = sem("projected"), sem("proj_copied")
        spilled = [sem(f"spilled{i}") for i in range(3)]
        own_loop, passed, issued = sem("own_loop"), sem("passed"), sem("issued")
        OWN = 2 * 6

        def load_keys(eng, came, n, c, part):
            if c < RING:
                eng.wait_ge(pv_done, n * (NCH + 1) + (c - RING + PV0))
            else:
                eng.wait_ge(transposed, n * NCH + (c - RING + 1 + KT0))
            eng.sem_inc(issued, 1)
            for i in part:
                page = eng.value_load(pages[0:1, bass.ds(n * PAGES + (c * CH + i), 1)], min_val=0, max_val=n_pool - 1)
                eng.dma_start(KV[:, c % RING, i, :], ck[bass.ds(page, 1), :, :].rearrange("n t d -> (n t) d")
                              ).then_inc(came[c % RING], 16)

        def load_values(eng, came, n, c, part):
            if c < RING:
                eng.wait_ge(transposed, n * NCH + (NCH - RING + c + 1 + KT0))
            else:
                eng.wait_ge(pv_done, n * (NCH + 1) + (c - RING + 1 + PV0))
            eng.sem_inc(issued, 1)
            for i in part:
                page = eng.value_load(pages[0:1, bass.ds(n * PAGES + (c * CH + i), 1)], min_val=0, max_val=n_pool - 1)
                eng.dma_start(KV[32 * i:32 * i + 32, c % RING, :, :],
                              cv[bass.ds(page, 1), :, :, :].rearrange("n k i d -> (n k) i d")
                              ).then_inc(came[c % RING], 16)

        block = here.enter_context(nc.Block())

        @block.sync
        def _(sp):
            for s, v in ((transposed, KT0), (scored, SC0), (biased, SE0), (kx_done, KX0), (p_turned, PT0),
                         (p_copied, PTV0), (pv_done, PV0), (projected, PJ0), (proj_copied, PE0), (o_copied, OE0)):
                sp.sem_inc(s, v)
            for s in spilled:
                sp.sem_inc(s, SP0)
            sp.dma_start(pages[:, :], a["page_table"].rearrange("b n -> (b n)").rearrange("(o n) -> o n", o=1)).then_inc(pages_in, 16)
            sp.wait_ge(pages_in, 16)
            sp.wait_ge(cleared, 6)
            with sp.Fori(0, NB // 2) as it:
                for par in range(2):
                    n = it * 2 + par
                    sp.wait_ge(scored, n * (NCH + 1) + (SC0 - NCH - 1))
                    sp.dma_start(Q[:, par, :], g.q_d[bass.ds(n, 1), :, :].rearrange("b p n -> (b p) n")).then_inc(q_in[par], 16)
                    for c in range(NCH):
                        if c == 2:
                            sp.wait_ge(w_low, n * 2 + WL0)
                            sp.dma_start(g.Wraw[:, :, :], g.w_sec[:, :, bass.ds(n * SEC + HSEC, HSEC)]).then_inc(w_raw, 16)
                        load_keys(sp, kv_in, n, c, (0, 1))
                    sp.wait_ge(kx_done, n + KX0)
                    sp.dma_start(kx[0:QS, :], ks_b[bass.ds(n, 1), :, :].rearrange("b q d -> (b q) d")).then_inc(kx_in, 16)
                    for c in range(NCH):
                        if c == 2:
                            sp.wait_ge(w_low, n * 2 + (1 + WL0))
                            sp.dma_start(g.Wraw[:, :, :], g.w_sec[:, :, bass.ds(n * SEC + SEC, HSEC)]).then_inc(w_raw, 16)
                        load_values(sp, kv_in, n, c, (0, 1))
            for i in range(3):
                sp.wait_ge(spilled[i], SP0 + 16 * NB * PJR // 3)

        @block.gpsimd
        def _(pool):
            nc.gpsimd.memset(kx[:, :], 0.0).then_inc(cleared, 1)
            nc.gpsimd.memset(vx[:, :], 0.0).then_inc(cleared, 1)
            nc.gpsimd.memset(kxT[:, :], 0.0).then_inc(cleared, 1)
            nc.gpsimd.memset(S[:, :, SUSE:SROW], 0.0).then_inc(cleared, 1)
            pool.wait_ge(pages_in, 16)
            pool.wait_ge(cleared, 6)
            with pool.Fori(0, NB // 2) as it:
                for par in range(2):
                    n = it * 2 + par
                    for c in range(NCH):
                        load_keys(pool, kv_in_sw, n, c, (2, 3))
                    for c in range(RING):
                        load_values(pool, kv_in_sw, n, c, (2, 3))
                    pool.wait_ge(pv_done, n * (NCH + 1) + PV0)
                    pool.dma_start(vx[0:QS, :], vs_b[bass.ds(n, 1), :, :].rearrange("b q d -> (b q) d")).then_inc(vx_in, 16)
                    for c in range(RING, NCH):
                        load_values(pool, kv_in_sw, n, c, (2, 3))

        @block.scalar
        def _(act):
            with act.Fori(0, NB // 2) as it:
                for par in range(2):
                    n = it * 2 + par
                    for u in range(PJR):
                        half, t = u // (NT + 1), u % (NT + 1)
                        rows = P if t < NT else ST
                        if u in (4, 13):
                            act.wait_ge(w_raw, n * 32 + (16 if u == 4 else 32))
                            nc.scalar.activation(g.Wh[:, 1 - half, :, :], g.Wraw[:, :, :], ACT.Copy).then_inc(w_high, 1)
                        if u == NT + 1:
                            act.wait_ge(max_ok, n + 1)
                            for gr in range(2):
                                nc.scalar.activation(S[:, gr, 0:SUSE], S[:, gr, 0:SUSE], ACT.Exp, bias=mB[:, gr:gr + 1],
                                                     accum_out=den[:, gr:gr + 1]).then_inc(exp_ok, 1)
                        act.wait_ge(projected, n * PJR + (u + 1 + PJ0))
                        act.wait_ge(spilled[u % 3], n * (PJR // 3 * 16) + (u // 3 * 16 + SP0))
                        if t < NT:
                            nc.scalar.activation(g.stage[:, u % 3, :], pj_ps[:, u % 2, 0:HSEC], ACT.Copy).then_inc(proj_copied, 1)
                        else:
                            nc.scalar.activation(lows[:, :], pj_ps[ST:P, u % 2, 0:HSEC], ACT.Copy).then_inc(low_out, 1)
                            act.wait_ge(summed, n * 2 + (half + 1))
                            act.sem_inc(proj_copied, 1)
                        act.wait_ge(proj_copied, n * PJR + (u + 1 + PE0))
                        act.dma_start(g.proj_d[t * P:t * P + rows, bass.ds(n * SEC + half * HSEC, HSEC)],
                                      g.stage[0:rows, u % 3, :]).then_inc(spilled[u % 3], 16)

        @block.vector
        def _(dve):
            nc.vector.memset(m32[:, :], 0.0).then_inc(cleared, 1)
            nc.vector.memset(o_ps[:, :], 0.0).then_inc(cleared, 1)
            dve.wait_ge(cleared, 6)

            with dve.Fori(0, NB // 2) as it:
                own = Own(own_loop, it * OWN)

                def turn(n, par, c):
                    e = n * (NCH + 1)
                    if c < NCH:
                        dve.wait_ge(kv_in[c % RING], (n * SLOT + (c // RING + 1)) * 32)
                        dve.wait_ge(kv_in_sw[c % RING], (n * SLOT + (c // RING + 1)) * 32)
                        dve.wait_ge(scored, e + (c - KTR + 1 + SC0 if c >= KTR else c - KTR + SC0))
                        nc.vector.transpose(KT[:, c % KTR, :].bitcast(U32),
                                            KV[:, c % RING, :, :].rearrange("p i d -> p (i d)").bitcast(U32)
                                            ).then_inc(transposed, 1)
                    else:
                        dve.wait_ge(kx_in, (n + 1) * 16)
                        dve.wait_ge(scored, e + (SC0 + c - (NCH + 1) + 1))
                        nc.vector.transpose(kxT[0:32, :].bitcast(U32), kx[:, :].bitcast(U32)).then_inc(kx_done, 1)

                def low(n, half):
                    dve.wait_ge(w_high, n * 2 + (2 - half))
                    nc.vector.tensor_tensor(g.Wl[:, half, :, :], g.Wraw[:, :, :], g.Wh[:, half, :, :].bitcast(F32),
                                            ALU.subtract).then_inc(w_low, 1)

                def samples(n, half):
                    u = half * (NT + 1) + NT
                    dve.wait_ge(low_out, n * 2 + (half + 1))
                    nc.vector.tensor_tensor(g.stage[0:ST, u % 3, :], pj_ps[0:ST, u % 2, 0:HSEC], lows[:, :],
                                            ALU.add).then_inc(summed, 1)

                def add_bias(n, par, c):
                    bank, w = (par * (NCH + 1) + c) % 2, P if c < NCH else 32
                    dve.wait_ge(scored, n * (NCH + 1) + (c + 1 + SC0))
                    if c == 0:
                        dve.wait_ge(p_turned, n * (NCH + 1) + PT0)
                    dve.sem_inc(passed, 1)
                    for gr in range(2):
                        ins = nc.vector.tensor_tensor_reduce(
                            out=S[:, gr, c * P:c * P + w], in0=sc_ps[:, bank, gr * P:gr * P + w],
                            in1=bias[:, gr, c * P:c * P + w], scale=1.0, scalar=-3e38, op0=ALU.add, op1=ALU.max,
                            accum_out=mx[:, gr, c:c + 1])
                    ins.then_inc(biased, 1)

                for par in range(2):
                    n = it * 2 + par
                    turn(n, par, 0)
                    for c in range(1, NCH + 1):
                        turn(n, par, c)
                        if c == NCH:
                            samples(n, 0)
                        add_bias(n, par, c - 1)
                        if c == 5:
                            low(n, 1)
                    add_bias(n, par, NCH)
                    dve.wait_ge(biased, n * (NCH + 1) + (NCH + 1 + SE0))
                    own.done(dve, nc.vector.tensor_reduce(m32[:, 0:2], mx[:, :, :], AX.X, ALU.max))
                    own.done(dve, nc.vector.transpose(mT[:, :].bitcast(U32), m32[:, :].bitcast(U32)))
                    own.done(dve, nc.vector.tensor_reduce(mr[:, 0:QS], mT[:, :].rearrange("p (i q) -> p q i", i=4),
                                                          AX.X, ALU.max, negate=True))
                    own.done(dve, nc.vector.tensor_copy(mE[:, :].rearrange("p (i q) -> p i q", i=4),
                                                        spread(mr[:, 0:QS], 1, 4)))
                    nc.vector.transpose(mB[:, :].bitcast(U32), mE[:, :].bitcast(U32)).then_inc(max_ok, 1)
                    for c in range(NCH + 1):
                        f = n * (NCH + 1)
                        bank = (par * (NCH + 1) + c) % 2
                        dve.wait_ge(p_turned, f + (c + 1 + PT0))
                        dve.wait_ge(pv_done, f + (c - 1 + PV0))
                        nc.vector.tensor_copy(
                            PTs[:, bank, :].rearrange("p (h i c q) -> p h c i q", h=H, i=4, q=QS),
                            pt_ps[:, bank, 0:2 * P].rearrange("p (h c i q) -> p h c i q", h=H, c=2, q=QS)
                        ).then_inc(p_copied, 1)
                        if c == 3:
                            low(n, 0)
                        if c == NCH - 1:
                            samples(n, 1)
                    dve.wait_ge(den_done, n + 1)
                    own.done(dve, nc.vector.reciprocal(coef[:, 0:1], l_ps[:, 0:1]))
                    own.done(dve, nc.vector.tensor_tensor(coef[:, 1:2], coef[:, 0:1], g.lamc[:, :], ALU.mult))
                    dve.wait_ge(pv_done, (n + 1) * (NCH + 1) + PV0)
                    nc.vector.tensor_scalar(g.Oall[:, bass.ds(n, 1), :].rearrange("p b v -> p (b v)"),
                                            o_ps[:, 0:P], coef[:, 1:2], None, ALU.mult).then_inc(o_copied, 1)
                assert own.n == OWN

        @block.tensor
        def _(pe):
            pe.wait_ge(cleared, 6)
            with pe.Fori(0, NB // 2) as it:

                def project(n, half, t):
                    u = half * (NT + 1) + t
                    if t == 0:
                        pe.wait_ge(w_low, n * 2 + (half + WL0))
                    pe.wait_ge(proj_copied, n * PJR + (u + 1 - 2 + PE0))
                    wh, wl = (lambda k: g.Wh[:, half, k, :]), (lambda k: g.Wl[:, half, k, :])
                    if t < NT:
                        ins = split_product(nc, pj_ps[:, u % 2, 0:HSEC], lambda k: g.hTh[:, k, t * P:(t + 1) * P],
                                            lambda k: g.hTl[:, k, t * P:(t + 1) * P], wh, wl)
                    else:
                        for k in range(KT_N):
                            if k:
                                nc.tensor.matmul(pj_ps[0:ST, u % 2, 0:HSEC], g.hSh[:, k - 1, :], wl(k - 1), start=False, stop=False)
                            if k == KT_N - 1:
                                nc.tensor.matmul(pj_ps[0:ST, u % 2, 0:HSEC], g.hSh[:, k, :], wl(k), start=False, stop=False)
                            ins = nc.tensor.matmul(pj_ps[:, u % 2, 0:HSEC], g.hS[:, k, :], wh(k), start=(k == 0),
                                                   stop=(k == KT_N - 1))
                    ins.then_inc(projected, 1)

                def score(n, par, c):
                    bank, e = (par * (NCH + 1) + c) % 2, n * (NCH + 1)
                    if c == 0:
                        pe.wait_ge(q_in[par], (it + 1) * 16)
                    if c < NCH:
                        pe.wait_ge(transposed, n * NCH + (c + 1 + KT0))
                        keys, w = KT[:, c % KTR, :].rearrange("p (n j k) -> p n j k", n=CH, k=32), P
                    else:
                        pe.wait_ge(kx_done, n + (1 + KX0))
                        keys, w = kxT[:, :].rearrange("p (n j k) -> p n j k", n=1, k=32), 32
                    pe.wait_ge(biased, e + (c + 1 - 2 + SE0))
                    for gr in range(2):
                        for db in range(2):
                            for m in range(4):
                                j = (4 * gr + m) * 2 + db
                                ins = nc.tensor.matmul(sc_ps[32 * m:32 * m + 32, bank, gr * P:gr * P + w],
                                                       Q[:, par, j * 32:j * 32 + 32], keys[:, :, j, :],
                                                       start=(db == 0), stop=(db == 1))
                    ins.then_inc(scored, 1)

                def turn(n, par, c):
                    bank = (par * (NCH + 1) + c) % 2
                    if c == 0:
                        pe.wait_ge(exp_ok, n * 2 + 2)
                    pe.wait_ge(p_copied, n * (NCH + 1) + (c + 1 - 2 + PTV0))
                    for gr in range(2):
                        ins = nc.tensor.transpose(pt_ps[:, bank, gr * P:(gr + 1) * P], S[:, gr, c * P:(c + 1) * P], g.ident)
                    ins.then_inc(p_turned, 1)

                def values(n, par, c):
                    bank, f = (par * (NCH + 1) + c) % 2, n * (NCH + 1)
                    pe.wait_ge(p_copied, f + (c + 1 + PTV0))
                    if c < NCH:
                        pe.wait_ge(kv_in[c % RING], (n * SLOT + (SLOT // 2 + c // RING + 1)) * 32)
                        pe.wait_ge(kv_in_sw[c % RING], (n * SLOT + (SLOT // 2 + c // RING + 1)) * 32)
                    else:
                        pe.wait_ge(vx_in, (n + 1) * 16)
                    for i in range(4 if c < NCH else 1):
                        for h in range(H):
                            part = PTs[:, bank, h * DH + 16 * i:h * DH + 16 * i + 16]
                            v = KV[:, c % RING, i, h * P:(h + 1) * P] if c < NCH else vx[:, h * P:(h + 1) * P]
                            ins = nc.tensor.matmul(o_ps[32 * h:32 * h + 16, 0:P], part, v,
                                                   start=(c == 0 and i == 0), stop=(c == NCH))
                    ins.then_inc(pv_done, 1)

                for par in range(2):
                    n = it * 2 + par
                    project(n, 0, 0)
                    for t in range(NT + 1):
                        if t < NT:
                            project(n, 0, t + 1)
                        score(n, par, t)
                    project(n, 1, 0)
                    project(n, 1, 1)
                    turn(n, par, 0)
                    pe.wait_ge(o_copied, n + OE0)
                    for gr in range(2):
                        ins = nc.tensor.matmul(l_ps[:, 0:1], g.cst[:, C_SL + gr * P:C_SL + (gr + 1) * P],
                                               den[:, gr:gr + 1], start=(gr == 0), stop=(gr == 1))
                    ins.then_inc(den_done, 1)
                    for c in range(NCH + 1):
                        if c < NCH:
                            turn(n, par, c + 1)
                        values(n, par, c)
                        if c + 2 <= NT:
                            project(n, 1, c + 2)


def prompt_attention(nc, g):
    a = g.a
    kp_rows = g.k_prompt.rearrange("l b (t p) h d -> (l b t) p (h d)", p=P)
    vp_rows = g.v_prompt.rearrange("l b (t p) h d -> (l b t) p (h d)", p=P)
    STEPS = NT * H
    groups = [[(k, min(k + 4, v // H + 1)) for k in range(0, v // H + 1, 4)] for v in range(STEPS)]
    first_group = [sum(len(x) for x in groups[:v]) for v in range(STEPS + 1)]
    with ExitStack() as here:
        sb, pb = tensors(nc, here)
        sem = semaphores(nc, here)
        KTh = sb("a_KT", [P, H, SEQ])
        Vp = sb("a_V", [P, NT, SEC])
        Z = sb("a_Z", [P, NT + 1, SEC])
        sig = sb("a_sig", [P, NT + 1, SEC])
        bias = sb("a_bias", [P, H, SEQ])
        E = sb("a_E", [P, 2, 2, SEQ])
        AT = sb("a_AT", [P, 2, SEQ])
        qk = sb("a_qk", [P, 2, 2 * SEC])
        sq = sb("a_sq", [P, 2 * SEC])
        junk = sb("a_junk", [P, H, P])
        QZ = sb("a_QZ", [P, 2, 2, H, P])
        o = sb("a_o", [P, 2, SEC])
        os_sq = sb("a_ossq", [ST, SEC])
        ssum, lns, rs = sb("a_ssum", [P, 16]), sb("a_lns", [P, 16]), sb("a_rs", [P, 16])
        mx, nm, den, rec = sb("a_mx", [P, 4]), sb("a_nm", [P, 4]), sb("a_den", [P, 4]), sb("a_rec", [P, 8])
        coef = sb("a_coef", [P, 1])
        oss, oln, ors = sb("a_oss", [P, 8]), sb("a_oln", [P, 4]), sb("a_ors", [P, 8])
        qk_ps = pb("a_qk_ps", [P, 512])
        s_ps = pb("a_s_ps", [P, 2, SEQ])
        at_ps = pb("a_at_ps", [P, 2, 512])
        o_ps = pb("a_o_ps", [P, 512])

        z_in, v_in, bias_in = sem("az_in"), sem("av_in"), sem("abias_in")
        qk_in, k_out = [sem("aqk_in0"), sem("aqk_in1")], [sem("ak_out0"), sem("ak_out1")]
        v_out, qz0 = sem("av_out"), sem("aqz0")
        names = ("sig_ok z_ok so_t so_ok so_sum so_rs so_y so_turned so_copied sq_ok sum_ok rs_ok qkn_ok q_turned "
                 "k_turned q_copied k_copied s_done biased max_ok exp_ok a_ok at_turned at_copied pv_group "
                 "o_ok oss_ok ors_ok y_ok y_turned y_copied")
        (sig_ok, z_ok, so_t, so_ok, so_sum, so_rs, so_y, so_turned, so_copied, sq_ok, sum_ok, rs_ok, qkn_ok,
         q_turned, k_turned, q_copied, k_copied, s_done, biased, max_ok, exp_ok, a_ok, at_turned, at_copied,
         pv_done, o_ok, oss_ok, ors_ok, y_ok, y_turned, y_copied) = (sem("a_" + n) for n in names.split())
        block = here.enter_context(nc.Block())

        @block.sync
        def _(sp):
            for i in range(NT):
                if i >= 2:
                    sp.wait_ge(qkn_ok, i - 1)
                    sp.dma_start(kp_rows[i - 2], qk[:, i % 2, SEC:2 * SEC]).then_inc(k_out[i % 2], 16)
                    sp.wait_ge(k_turned, i - 1)
                    sp.wait_ge(k_out[i % 2], 16 * (i // 2))
                sp.dma_start(qk[:, i % 2, :], g.proj_d[i * P:(i + 1) * P, QB * SEC:(KB + 1) * SEC]).then_inc(qk_in[i % 2], 16)
                if i == 0:
                    for j in range(NT):
                        sp.dma_start(Vp[:, j, :], g.proj_d[j * P:(j + 1) * P, VB * SEC:(VB + 1) * SEC]).then_inc(v_in, 16)
                if i == 1:
                    for t in range(NT + 1):
                        n = P if t < NT else ST
                        sp.dma_start(Z[0:n, t, :], g.proj_d[t * P:t * P + n, ZB * SEC:(ZB + 1) * SEC]).then_inc(z_in, 16)
            sp.wait_ge(v_in, 16 * NT)
            sp.dma_start(vp_rows.rearrange("t p d -> p t d"), Vp[:, :, :]).then_inc(v_out, 16)
            for i in (NT - 2, NT - 1):
                sp.wait_ge(qkn_ok, i + 1)
                sp.dma_start(kp_rows[i], qk[:, i % 2, SEC:2 * SEC]).then_inc(k_out[i % 2], 16)
            sp.wait_ge(v_out, 16)
            for b in range(2):
                sp.wait_ge(k_out[b], 16 * NT // 2)

        @block.gpsimd
        def _(pool):
            nc.gpsimd.memset(QZ[:, :, :, :, :], 0.0).then_inc(qz0, 1)
            pool.dma_start(bias[:, :, :], bass.AP(g.tabp_d.tensor, g.tabp_d.offset + P - 1,
                                                  [[H * PTAB - 1, P], [PTAB, H], [1, SEQ]])).then_inc(bias_in, 16)
            pool.wait_ge(sig_ok, 2)
            nc.gpsimd.tensor_tensor(Z[:, 0:NT, :], Z[:, 0:NT, :], sig[:, 0:NT, :], ALU.mult).then_inc(z_ok, 1)
            pool.wait_ge(z_ok, 1)
            nc.gpsimd.tensor_tensor(
                Z[:, 0:NT, :].rearrange("p t (h d) -> p (t h) d", h=H), Z[:, 0:NT, :].rearrange("p t (h d) -> p (t h) d", h=H),
                spread(g.subw[:, :], 1, NT * H), ALU.mult).then_inc(z_ok, 1)

        @block.scalar
        def _(act):
            def square(i):
                act.wait_ge(qk_in[i % 2], 16 * (i // 2 + 1))
                if i:
                    act.wait_ge(sum_ok, i)
                nc.scalar.activation(sq[:, :], qk[:, i % 2, :], ACT.Square).then_inc(sq_ok, 1)

            def scales(i, u):
                if i < NT:
                    act.wait_ge(sum_ok, i + 1)
                    ins = nc.scalar.activation(lns[:, :], ssum[:, :], ACT.Ln, bias=g.epsc[:, :], scale=1.0 / DH)
                if u >= 0:
                    if i < NT:
                        g.act.done(act, ins)
                    s0 = (u % 2) * H
                    act.wait_ge(oss_ok, H * (u + 1))
                    ins = nc.scalar.activation(oln[:, :], oss[:, s0:s0 + H], ACT.Ln, bias=g.epsc[:, :], scale=1.0 / P)
                if i == 1:
                    act.wait_ge(so_sum, 1)
                    g.act.done(act, ins)
                    ins = nc.scalar.activation(oln[0:ST, 0:H], oss[0:ST, H:2 * H], ACT.Ln, bias=g.epsc[0:ST, :], scale=1.0 / P)
                g.act.done(act, ins)
                if i == 1:
                    nc.scalar.activation(ors[0:ST, H:2 * H], oln[0:ST, 0:H], ACT.Exp, scale=-0.5).then_inc(so_rs, 1)
                if i < NT:
                    nc.scalar.activation(rs[:, :], lns[:, :], ACT.Exp, scale=-0.5).then_inc(rs_ok, 1)
                if u >= 0:
                    nc.scalar.activation(ors[:, s0:s0 + H], oln[:, :], ACT.Exp, scale=-0.5).then_inc(ors_ok, 1)

            def queries(i):
                act.wait_ge(q_turned, i + 1)
                if i == 0:
                    act.wait_ge(qz0, 1)
                if i >= 2:
                    act.wait_ge(s_done, 2 * H * (i - 1))
                for c in range(2):
                    rows = slice(DH * c, DH * c + DH)
                    ins = nc.scalar.activation(QZ[rows, i % 2, c, :, :],
                                               qk_ps[rows, :].rearrange("p (h t) -> p h t", h=H), ACT.Copy)
                ins.then_inc(q_copied, 1)

            def numerators(v):
                for c in range(2):
                    act.wait_ge(max_ok, 2 * v + c + 1)
                    w = (v // H + 1) * P
                    nc.scalar.activation(E[:, v % 2, c, 0:w], E[:, v % 2, c, 0:w], ACT.Exp,
                                         bias=nm[:, 2 * (v % 2) + c:2 * (v % 2) + c + 1],
                                         accum_out=den[:, 2 * (v % 2) + c:2 * (v % 2) + c + 1]).then_inc(exp_ok, 1)

            square(0)
            scales(0, -1)
            queries(0)
            numerators(0)
            for v in range(STEPS + 4):
                i, h = divmod(v, H)
                if v == 2:
                    act.wait_ge(z_in, 16 * (NT + 1))
                    nc.scalar.activation(sig[0:ST, NT, :], Z[0:ST, NT, :], ACT.Sigmoid).then_inc(sig_ok, 1)
                    nc.scalar.activation(sig[:, 0:NT, :], Z[:, 0:NT, :], ACT.Sigmoid).then_inc(sig_ok, 1)
                    act.wait_ge(so_turned, 1)
                    nc.scalar.activation(g.yT[:, 4:8, SEQ:SEQ + ST], qk_ps[:, 0:H * ST].rearrange("p (h t) -> p h t", h=H),
                                         ACT.Copy).then_inc(so_copied, 1)
                if h == 1:
                    scales(i + 1, i - 1)
                if i + 1 < NT:
                    if h == 0:
                        square(i + 1)
                    if h == 2:
                        queries(i + 1)
                if v + 1 < STEPS:
                    numerators(v + 1)
                if v < STEPS:
                    for n, (k0, k1) in enumerate(groups[v]):
                        e = first_group[v] + n
                        act.wait_ge(at_turned, e + 1)
                        nc.scalar.activation(AT[:, v % 2, k0 * P:k1 * P], at_ps[:, e % 2, 0:(k1 - k0) * P],
                                             ACT.Copy).then_inc(at_copied, 1)
                if 1 <= v <= STEPS:
                    u = v - 1
                    act.wait_ge(o_ok, u + 1)
                    slot = (u // H % 2) * H + u % H
                    nc.scalar.activation(junk[:, u % H, :], o[:, u // H % 2, (u % H) * P:(u % H + 1) * P], ACT.Square,
                                         accum_out=oss[:, slot:slot + 1]).then_inc(oss_ok, 1)
                if h == 3 and i >= 1:
                    act.wait_ge(y_turned, i)
                    nc.scalar.activation(g.yT[:, 4:8, (i - 1) * P:i * P],
                                         qk_ps[:, :].rearrange("p (h t) -> p h t", h=H), ACT.Copy).then_inc(y_copied, 1)

        @block.vector
        def _(dve):
            own = g.dve

            def sums(i):
                dve.wait_ge(sq_ok, i + 1)
                nc.vector.tensor_reduce(ssum[:, :], sq[:, :].rearrange("p (n d) -> p n d", d=DH), AX.X,
                                        ALU.add).then_inc(sum_ok, 1)

            def normalise(i):
                dve.wait_ge(rs_ok, i + 1)
                x = qk[:, i % 2, :]
                own.done(dve, nc.vector.tensor_tensor(x.rearrange("p (n d) -> p n d", d=DH), x.rearrange("p (n d) -> p n d", d=DH),
                                                      spread(rs[:, :], 2, DH), ALU.mult))
                nc.vector.tensor_tensor(x.rearrange("p (w n d) -> p w n d", w=2, d=DH),
                                        x.rearrange("p (w n d) -> p w n d", w=2, d=DH),
                                        spread(g.wqk[:, :, :], 2, 8), ALU.mult).then_inc(qkn_ok, 1)

            def keys(i):
                dve.wait_ge(k_turned, i + 1)
                nc.vector.tensor_copy(KTh[:, :, i * P:(i + 1) * P],
                                      qk_ps[:, :].rearrange("p (h t) -> p h t", h=H)).then_inc(k_copied, 1)

            def maxima(v):
                w = (v // H + 1) * P
                if v >= 2:
                    dve.wait_ge(at_turned, first_group[v - 1])
                for c in range(2):
                    slot = 2 * (v % 2) + c
                    dve.wait_ge(s_done, 2 * v + c + 1)
                    if v == 0 and c == 0:
                        dve.wait_ge(bias_in, 16)
                    nc.vector.tensor_tensor_reduce(
                        out=E[:, v % 2, c, 0:w], in0=s_ps[:, c, 0:w], in1=bias[:, v % H, SEQ - w:SEQ], scale=1.0,
                        scalar=-3e38, op0=ALU.add, op1=ALU.max, accum_out=mx[:, slot:slot + 1]).then_inc(biased, 1)
                    dve.wait_ge(biased, 2 * v + c + 1)
                    nc.vector.tensor_scalar(nm[:, slot:slot + 1], mx[:, slot:slot + 1], -1.0, None, ALU.mult).then_inc(max_ok, 1)

            def sample_rows():
                dve.wait_ge(sig_ok, 1)
                own.done(dve, nc.vector.tensor_tensor(Z[0:ST, NT, :], Z[0:ST, NT, :], sig[0:ST, NT, :], ALU.mult))
                own.done(dve, nc.vector.tensor_tensor(
                    Z[0:ST, NT, :].rearrange("p (h d) -> p h d", h=H), Z[0:ST, NT, :].rearrange("p (h d) -> p h d", h=H),
                    spread(g.subw[0:ST, :], 1, H), ALU.mult))
                dve.wait_ge(so_rs, 1)
                own.done(dve, nc.vector.tensor_tensor(so_h, so_h, spread(ors[0:ST, H:2 * H], 2, P), ALU.mult))
                nc.vector.tensor_tensor(o[0:ST, 1, :], o[0:ST, 1, :], Z[0:ST, NT, :], ALU.mult).then_inc(so_y, 1)

            sums(0)
            dve.wait_ge(so_t, 1)
            own.done(dve, nc.vector.tensor_copy(o[0:ST, 1, :], o_ps[0:ST, :]))
            so_h = o[0:ST, 1, :].rearrange("p (h d) -> p h d", h=H)
            own.done(dve, nc.vector.tensor_tensor(os_sq[:, :], o[0:ST, 1, :], o[0:ST, 1, :], ALU.mult))
            nc.vector.tensor_reduce(oss[0:ST, H:2 * H], os_sq[:, :].rearrange("p (h d) -> p h d", h=H), AX.X,
                                    ALU.add).then_inc(so_sum, 1)
            normalise(0)
            keys(0)
            maxima(0)
            for v in range(STEPS + 4):
                i, h = divmod(v, H)
                if v == 2:
                    sample_rows()
                if h == 3 and i + 1 < NT:
                    keys(i + 1)
                if v < STEPS:
                    s0, r0 = 2 * (v % 2), 2 * (v % 4)
                    w = (i + 1) * P
                    dve.wait_ge(exp_ok, 2 * v + 2)
                    own.done(dve, nc.vector.reciprocal(rec[:, r0:r0 + 2], den[:, s0:s0 + 2]))
                    own.done(dve, nc.vector.scalar_tensor_tensor(coef[:, :], rec[:, r0 + 1:r0 + 2], g.nlam[:, :],
                                                                 den[:, s0:s0 + 1], ALU.mult, ALU.mult))
                    nc.vector.scalar_tensor_tensor(E[:, v % 2, 0, 0:w], E[:, v % 2, 1, 0:w], coef[:, :],
                                                   E[:, v % 2, 0, 0:w], ALU.mult, ALU.add).then_inc(a_ok, 1)
                if v + 1 < STEPS:
                    maxima(v + 1)
                if 1 <= v <= STEPS:
                    u = v - 1
                    dve.wait_ge(pv_done, u + 1)
                    if u == H:
                        dve.wait_ge(so_turned, 1)
                    if u % H == 0 and u // H >= 2:
                        dve.wait_ge(y_turned, u // H - 1)
                    nc.vector.tensor_scalar(o[:, u // H % 2, (u % H) * P:(u % H + 1) * P], o_ps[:, (u % H) * P:(u % H + 1) * P],
                                            rec[:, 2 * (u % 4):2 * (u % 4) + 1], None, ALU.mult).then_inc(o_ok, 1)
                if h == 0 and i + 1 < NT:
                    sums(i + 1)
                if h == 1:
                    if i + 1 < NT:
                        normalise(i + 1)
                    if i >= 1:
                        b = (i - 1) % 2
                        if i == 1:
                            dve.wait_ge(z_ok, 2)
                        dve.wait_ge(ors_ok, i)
                        dve.wait_ge(o_ok, H * i)
                        x = o[:, b, :]
                        own.done(dve, nc.vector.tensor_tensor(x.rearrange("p (h d) -> p h d", h=H), x.rearrange("p (h d) -> p h d", h=H),
                                                              spread(ors[:, b * H:b * H + H], 2, P), ALU.mult))
                        nc.vector.tensor_tensor(x, x, Z[:, i - 1, :], ALU.mult).then_inc(y_ok, 1)

        @block.tensor
        def _(pe):
            for h in range(H):
                for b in range(NB):
                    ins = nc.tensor.matmul(o_ps[0:ST, h * P:(h + 1) * P],
                                           g.cst[:, C_SZ + h * 120 + 56 - QS * b:C_SZ + h * 120 + 120 - QS * b],
                                           g.Oall[:, b, :], start=(b == 0), stop=(b == NB - 1))
            ins.then_inc(so_t, 1)

            def turn_q(i):
                pe.wait_ge(qkn_ok, i + 1)
                if i == 1:
                    pe.wait_ge(so_copied, 1)
                if i:
                    pe.wait_ge(k_copied, i)
                    if i >= 3:
                        pe.wait_ge(y_copied, i - 2)
                for h in range(H):
                    ins = nc.tensor.transpose(qk_ps[:, h * P:(h + 1) * P], qk[:, i % 2, h * P:(h + 1) * P], g.ident)
                ins.then_inc(q_turned, 1)

            def turn_k(i):
                pe.wait_ge(q_copied, i + 1)
                for h in range(H):
                    ins = nc.tensor.transpose(qk_ps[:, h * P:(h + 1) * P], qk[:, i % 2, SEC + h * P:SEC + (h + 1) * P], g.ident)
                ins.then_inc(k_turned, 1)

            def turn_y(i):
                pe.wait_ge(y_ok, i + 1)
                if i + 2 < NT:
                    pe.wait_ge(k_copied, i + 3)
                elif i >= 1:
                    pe.wait_ge(y_copied, i)
                for j in range(H):
                    ins = nc.tensor.transpose(qk_ps[:, j * P:(j + 1) * P], o[:, i % 2, j * P:(j + 1) * P], g.ident)
                ins.then_inc(y_turned, 1)

            def scores(v):
                i, h = divmod(v, H)
                if h == 0:
                    pe.wait_ge(k_copied, i + 1)
                    pe.wait_ge(q_copied, i + 1)
                for c in range(2):
                    if v >= 1:
                        pe.wait_ge(biased, 2 * v + c - 1)
                    w = (i + 1) * P
                    for n0 in range(0, w, 512):
                        n1 = min(n0 + 512, w)
                        ins = nc.tensor.matmul(s_ps[:, c, n0:n1], QZ[:, i % 2, c, h, :], KTh[:, h, n0:n1], start=True, stop=True)
                    ins.then_inc(s_done, 1)

            def turn(v):
                pe.wait_ge(a_ok, v + 1)
                for n, (k0, k1) in enumerate(groups[v]):
                    e = first_group[v] + n
                    if e >= 2:
                        pe.wait_ge(at_copied, e - 1)
                    for k in range(k0, k1):
                        ins = nc.tensor.transpose(at_ps[:, e % 2, (k - k0) * P:(k - k0 + 1) * P],
                                                  E[:, v % 2, 0, k * P:(k + 1) * P], g.ident)
                    ins.then_inc(at_turned, 1)

            def values(v):
                i, h = divmod(v, H)
                pe.wait_ge(at_copied, first_group[v + 1])
                if v == 0:
                    pe.wait_ge(so_sum, 1)
                else:
                    pe.wait_ge(o_ok, v)
                for k in range(i + 1):
                    ins = nc.tensor.matmul(o_ps[:, h * P:(h + 1) * P], AT[:, v % 2, k * P:(k + 1) * P],
                                           Vp[:, k, h * P:(h + 1) * P], start=(k == 0), stop=(k == i))
                ins.then_inc(pv_done, 1)

            turn_q(0)
            turn_k(0)
            scores(0)
            pe.wait_ge(v_in, 16 * NT)
            for v in range(STEPS + 4):
                i, h = divmod(v, H)
                if v == 2:
                    pe.wait_ge(k_copied, 1)
                    pe.wait_ge(so_y, 1)
                    for j in range(H):
                        ins = nc.tensor.transpose(qk_ps[:, j * ST:(j + 1) * ST], o[0:ST, 1, j * P:(j + 1) * P], g.ident[0:ST, 0:ST])
                    ins.then_inc(so_turned, 1)
                if h == 2 and i + 1 < NT:
                    turn_q(i + 1)
                if v + 1 < STEPS:
                    scores(v + 1)
                if 1 <= v <= STEPS:
                    values(v - 1)
                if v < STEPS:
                    turn(v)
                if h == 2 and i + 1 < NT:
                    turn_k(i + 1)
                if h == 3 and i >= 1:
                    turn_y(i - 1)


def recurrence(nc, g):
    a = g.a
    NL = len(LEVELS) + 1
    PL = [64, 32] + list(LEVELS)
    SL = [4, 2, 1]
    with ExitStack() as here:
        sb, pb = tensors(nc, here)
        sem = semaphores(nc, here)
        q, kin, B = (sb("r_" + n, [P, H, SEQ]) for n in ("q", "k", "b"))
        qs, ks, Bs = (sb("r_" + n, [P, H, ST]) for n in ("qs", "ks", "bs"))
        reset = sb("r_reset", [P, SEQ + ST])
        v = sb("r_v", [P, 2, NT, P])
        x = sb("r_x", [P, 2, 2 * SEC])
        M = sb("r_M", [P, 3, SEQ])
        qe = sb("r_qe", [P, SEQ])
        kd = sb("r_kd", [P, SEQ])
        kdT = sb("r_kdT", [P, SEQ])
        At = sb("r_At", [P, SEQ])
        wm = sb("r_wm", [P, NT, NL * 32])
        ws = sb("r_ws", [P, NT, 32])
        S = sb("r_S", [P, NT + 1, P])
        eb = sb("r_eb", [P, NT])
        lb = sb("r_lb", [P, 2, H])
        lm, lsum, oml = sb("r_lm", [P, H]), sb("r_lsum", [P, H]), sb("r_oml", [P, H])
        win_ps = pb("r_win", [P, NT, 256])
        dir_ps = pb("r_dir", [P, SEQ])
        k_ps = pb("r_kps", [P, 512])
        o_ps = pb("r_ops", [P, 512])

        xs = [x[:, 0, :], x[:, 1, :], qe[:, :], kd[:, :], kdT[:, :], At[:, :]] + [M[:, i, :] for i in range(3)]
        x_in, v_in = [sem(f"rx_in{t}") for t in range(NT + 1)], [sem("rv_in0"), sem("rv_in1")]
        reset_in, st_out = sem("r_reset_in"), sem("r_st_out")
        names = ("lb_e lb_ok x_turned q_copied f_copied log_ok scan_ok zero_ok d_ok e_ok mk_ok mq_ok lev_done win_ok at_ok "
                 "dir_ok ebe_ok kd_ok qe_ok kd_turned kd_copied ds_done s_ok o_done o_copied")
        (lb_e, lb_ok, x_turned, q_copied, f_copied, log_ok, scan_ok, zero_ok, d_ok, e_ok, mk_ok, mq_ok, lev_done,
         win_ok, at_ok, dir_ok, ebe_ok, kd_ok, qe_ok, kd_turned, kd_copied, ds_done, s_ok, o_done,
         o_copied) = (sem("r_" + n) for n in names.split())
        NLEV = len(PL)
        stage = ExitStack()
        block = stage.enter_context(nc.Block())

        @block.sync
        def _(sp):
            for t in range(NT + 1):
                n = P if t < NT else ST
                sp.dma_start(xs[t][0:n, :], g.proj_d[t * P:t * P + n, 0:2 * SEC]).then_inc(x_in[t], 16)
            sp.dma_start(reset[:, :], bass.AP(a["resets"].tensor, a["resets"].offset,
                                              [[0, P], [1, SEQ + ST]])).then_inc(reset_in, 16)

            def values(h):
                sp.dma_start(v[:, h % 2, :, :], g.proj_d[0:SEQ, IA * SEC + h * P:IA * SEC + (h + 1) * P].rearrange(
                    "(t p) d -> p t d", p=P)).then_inc(v_in[h % 2], 16)

            values(0)
            values(1)
            sp.dma_start(g.WO[:, :, :], a["w_out"].rearrange("l (k p) n -> (l p) k n", p=P)[:, KT_N // 2:, :]).then_inc(g.wo_in, 16)
            for h in range(H):
                sp.wait_ge(s_ok, (h + 1) * NT)
                sp.dma_start(g.s_prompt[0, 0, h, :, :], S[:, NT, :]).then_inc(st_out, 16)
                if h + 2 < H:
                    sp.wait_ge(o_done, (h + 1) * NT)
                    values(h + 2)
            sp.wait_ge(st_out, 16 * H)

        @block.scalar
        def _(act):
            act.wait_ge(lb_e, 1)
            nc.scalar.activation(lb[:, :, :], lb[:, :, :], ACT.Exp).then_inc(lb_e, 1)
            for t in range(NT + 1):
                n = P if t < NT else ST
                act.wait_ge(x_turned, t + 1)
                src = (win_ps[:, 4 * (t % 2) + 2:4 * (t % 2) + 4, :].rearrange("p a c -> p (a c)")[:, 0:H * n]
                       .rearrange("p (h n) -> p h n", h=H))
                fo, ko = (B[:, :, t * P:(t + 1) * P], kin[:, :, t * P:(t + 1) * P]) if t < NT else (Bs[:, :, :], ks[:, :, :])
                nc.scalar.activation(fo, src, ACT.Sigmoid)
                nc.scalar.activation(ko, src, ACT.Sigmoid, scale=-1.0).then_inc(f_copied, 1)
            act.wait_ge(lb_ok, 1)
            act.wait_ge(f_copied, NT + 1)
            for h in range(H):
                for m in (B, Bs):
                    ins = nc.scalar.activation(m[:, h, :], m[:, h, :], ACT.Ln, bias=lb[:, 0, h:h + 1],
                                               scale=oml[:, h:h + 1])
                ins.then_inc(log_ok, 1)

            def level(h, n):
                e, s = h * (NLEV + 1) + n, PL[n]
                act.wait_ge(d_ok, e + 1)
                m = M[:, e % 3, :].rearrange("p (b s) -> p b s", s=2 * s)
                nc.scalar.activation(m[:, :, 0:s], m[:, :, 0:s], ACT.Exp, scale=-1.0)
                nc.scalar.activation(m[:, :, s:2 * s], m[:, :, s:2 * s], ACT.Exp).then_inc(e_ok, 1)

            def ends(h):
                e = h * (NLEV + 1) + NLEV
                act.wait_ge(d_ok, e + 1)
                nc.scalar.activation(M[:, e % 3, :], M[:, e % 3, :], ACT.Exp).then_inc(e_ok, 1)
                if h >= 1:
                    act.wait_ge(o_done, h * NT)
                    act.wait_ge(s_ok, h * NT)
                nc.scalar.activation(qe[:, :], B[:, h, :], ACT.Exp)
                nc.scalar.activation(eb[:, :], B[:, h, :].rearrange("p (t n) -> p t n", n=P)[:, :, P - 1], ACT.Exp).then_inc(ebe_ok, 1)

            for h in range(H):
                for n in range(2 if h else 0, NLEV):
                    level(h, n)
                ends(h)
                if h + 1 < H:
                    level(h + 1, 0)
                act.wait_ge(lev_done, (h + 1) * (NLEV + 1))
                nc.scalar.activation(At[:, :], dir_ps[:, :], ACT.Copy).then_inc(dir_ok, 1)
                for half in range(2):
                    act.wait_ge(kd_turned, 2 * h + half + 1)
                    nc.scalar.activation(kdT[:, half * 512:(half + 1) * 512], k_ps[:, :], ACT.Copy).then_inc(kd_copied, 1)
                if h + 1 < H:
                    level(h + 1, 1)
                for half in range(2):
                    act.wait_ge(o_done, h * NT + 4 * (half + 1))
                    nc.scalar.activation(g.ot[:, 4 * half:4 * half + 4, h * P:(h + 1) * P],
                                         o_ps[:, :].rearrange("p (t d) -> p t d", t=4), ACT.Copy).then_inc(o_copied, 1)

        @block.gpsimd
        def _(pool):
            for h in range(H):
                for n, s in enumerate(PL):
                    e = h * (NLEV + 1) + n
                    pool.wait_ge(e_ok, e + 1)
                    if n == 0:
                        pool.wait_ge(scan_ok, 3 * (h + 1))
                    m = M[:, e % 3, :].rearrange("p (b s) -> p b s", s=2 * s)
                    k = kin[:, h, :].rearrange("p (b s) -> p b s", s=2 * s)
                    nc.gpsimd.tensor_tensor(m[:, :, 0:s], m[:, :, 0:s], k[:, :, 0:s], ALU.mult).then_inc(mk_ok, 1)

        @block.vector
        def _(dve):
            own = g.dve
            raw = g.rT[:, 80:88].rearrange("p (l h) -> p l h", h=H)
            own.done(dve, nc.vector.tensor_tensor(lm[:, :], raw[:, 0, :], raw[:, 1, :], ALU.max))
            nc.vector.tensor_tensor(lb[:, :, :], raw, spread(lm[:, :], 1, 2), ALU.subtract).then_inc(lb_e, 1)
            nc.vector.memset(dir_ps[:, :], 0.0).then_inc(zero_ok, 1)
            nc.vector.memset(S[:, 0, :], 0.0).then_inc(zero_ok, 1)
            dve.wait_ge(lb_e, 2)
            own.done(dve, nc.vector.tensor_tensor(lsum[:, :], lb[:, 0, :], lb[:, 1, :], ALU.add))
            own.done(dve, nc.vector.reciprocal(lsum[:, :], lsum[:, :]))
            own.done(dve, nc.vector.tensor_tensor(lb[:, 0, :], lb[:, 0, :], lsum[:, :], ALU.mult))
            nc.vector.tensor_scalar(oml[:, :], lb[:, 0, :], -1.0, 1.0, ALU.mult, ALU.add).then_inc(lb_ok, 1)
            for t in range(NT + 1):
                n = P if t < NT else ST
                dve.wait_ge(x_turned, t + 1)
                src = (win_ps[:, 4 * (t % 2):4 * (t % 2) + 2, :].rearrange("p a c -> p (a c)")[:, 0:H * n]
                       .rearrange("p (h n) -> p h n", h=H))
                dst = q[:, :, t * P:(t + 1) * P] if t < NT else qs[:, :, :]
                nc.vector.tensor_scalar(dst, src, P ** -0.5, None, ALU.mult).then_inc(q_copied, 1)
            dve.wait_ge(f_copied, NT + 1)
            dve.wait_ge(lb_ok, 1)
            dve.wait_ge(reset_in, 16)

            def prepare(h):
                for m in (kin, ks):
                    ins = nc.vector.tensor_scalar(m[:, h, :], m[:, h, :], oml[:, h:h + 1], None, ALU.mult)
                ins.then_inc(scan_ok, 1)
                dve.wait_ge(log_ok, h + 1)
                for m, r0, r1 in ((B, 0, SEQ), (Bs, SEQ, SEQ + ST)):
                    nc.vector.tensor_tensor_scan(m[:, h, :], reset[:, r0:r1], m[:, h, :], 0.0, ALU.mult, ALU.add).then_inc(scan_ok, 1)
                dve.wait_ge(scan_ok, 3 * (h + 1))

            def differences(h, n):
                e = h * (NLEV + 1) + n
                if e >= 3:
                    dve.wait_ge(lev_done, (e - 3) + 1)
                if n < NLEV:
                    s = PL[n]
                    b = B[:, h, :].rearrange("p (b s) -> p b s", s=2 * s)
                    nc.vector.tensor_tensor(M[:, e % 3, :].rearrange("p (b s) -> p b s", s=2 * s), b,
                                            spread(b[:, :, s - 1], 2, 2 * s), ALU.subtract).then_inc(d_ok, 1)
                else:
                    b = B[:, h, :].rearrange("p (t n) -> p t n", n=P)
                    nc.vector.tensor_tensor(M[:, e % 3, :].rearrange("p (t n) -> p t n", n=P),
                                            spread(b[:, :, P - 1], 2, P), b, ALU.subtract).then_inc(d_ok, 1)

            def queries(h, n):
                e = h * (NLEV + 1) + n
                dve.wait_ge(e_ok, e + 1)
                if n < NLEV:
                    s = PL[n]
                    m = M[:, e % 3, :].rearrange("p (b s) -> p b s", s=2 * s)
                    qq = q[:, h, :].rearrange("p (b s) -> p b s", s=2 * s)
                    nc.vector.tensor_tensor(m[:, :, s:2 * s], m[:, :, s:2 * s], qq[:, :, s:2 * s], ALU.mult).then_inc(mq_ok, 1)
                else:
                    if h >= 1:
                        dve.wait_ge(kd_turned, 2 * h)
                    nc.vector.tensor_tensor(kd[:, :], M[:, e % 3, :], kin[:, h, :], ALU.mult).then_inc(kd_ok, 1)
                    dve.wait_ge(ebe_ok, h + 1)
                    nc.vector.tensor_tensor(qe[:, :], qe[:, :], q[:, h, :], ALU.mult).then_inc(qe_ok, 1)

            prepare(0)
            differences(0, 0)
            differences(0, 1)
            queries(0, 0)
            for h in range(H):
                for n in range(1, NLEV + 1):
                    if n < NLEV:
                        differences(h, n + 1)
                    queries(h, n)
                if h + 1 < H:
                    prepare(h + 1)
                    differences(h + 1, 0)
                dve.wait_ge(lev_done, (h + 1) * (NLEV + 1))
                own.done(dve, nc.vector.tensor_tensor(wm[:, :, :], win_ps[:, :, 0:NL * 32],
                                                      spread(g.cst[:, C_WM:C_WM + NL * 32], 1, NT), ALU.mult))
                nc.vector.tensor_reduce(ws[:, :, :], wm[:, :, :].rearrange("p t (l c) -> p t c l", l=NL), AX.X,
                                        ALU.add).then_inc(win_ok, 1)
                dve.wait_ge(win_ok, h + 1)
                dve.wait_ge(dir_ok, h + 1)
                for w in range(4):
                    rows = slice(32 * w, 32 * w + 32)
                    ins = nc.vector.tensor_copy(At[rows, :].rearrange("p (t n) -> p t n", n=P)[:, :, 32 * w:32 * w + 32],
                                                ws[rows, :, :])
                ins.then_inc(at_ok, 1)
                if h + 1 < H:
                    differences(h + 1, 1)
                    queries(h + 1, 0)
                for t in range(NT):
                    dve.wait_ge(ds_done, h + 1)
                    if t >= 1:
                        dve.wait_ge(s_ok, h * NT + t)
                    if h >= 1:
                        if t == 0:
                            dve.wait_ge(o_done, h * NT)
                            dve.wait_ge(st_out, 16 * h)
                    nc.vector.scalar_tensor_tensor(S[:, t + 1, :], S[:, t, :], eb[:, t:t + 1],
                                                   win_ps[:, t, 0:P], ALU.mult, ALU.add).then_inc(s_ok, 1)

        @block.tensor
        def _(pe):
            pe.wait_ge(zero_ok, 2)
            for t in range(NT + 1):
                n = P if t < NT else ST
                pe.wait_ge(x_in[t], 16)
                if t >= 2:
                    pe.wait_ge(q_copied, t - 1)
                    pe.wait_ge(f_copied, t - 1)
                for part in range(2):
                    bank = win_ps[:, 4 * (t % 2) + 2 * part:4 * (t % 2) + 2 * part + 2, :].rearrange("p a c -> p (a c)")
                    for h in range(H):
                        ins = nc.tensor.transpose(bank[:, h * n:(h + 1) * n], xs[t][0:n, part * SEC + h * P:part * SEC + (h + 1) * P],
                                                  g.ident[0:n, 0:n])
                ins.then_inc(x_turned, 1)
            pe.wait_ge(q_copied, NT + 1)
            pe.wait_ge(f_copied, NT + 1)
            for h in range(H):
                pe.wait_ge(scan_ok, 3 * (h + 1))
                if h >= 1:
                    pe.wait_ge(s_ok, h * NT)
                    pe.wait_ge(dir_ok, h)
                for n, s in enumerate(PL):
                    e = h * (NLEV + 1) + n
                    pe.wait_ge(mk_ok, h * NLEV + n + 1)
                    pe.wait_ge(mq_ok, h * NLEV + n + 1)
                    for t in range(NT):
                        m = M[:, e % 3, t * P:(t + 1) * P]
                        if s >= 32:
                            for b in range(P // (2 * s)):
                                j0 = 2 * s * b
                                ins = nc.tensor.matmul(dir_ps[j0:j0 + s, t * P + j0 + s:t * P + j0 + 2 * s], m[:, j0:j0 + s],
                                                       m[:, j0 + s:j0 + 2 * s], start=True, stop=True)
                        else:
                            for w in range(4):
                                ins = nc.tensor.matmul(win_ps[32 * w:32 * w + 32, t, (n - 2) * 32:(n - 1) * 32],
                                                       m[:, 32 * w:32 * w + 32], m[:, 32 * w:32 * w + 32], start=True, stop=True)
                    ins.then_inc(lev_done, 1)
                for t in range(NT):
                    for w in range(4):
                        c0 = t * P + 32 * w
                        ins = nc.tensor.matmul(win_ps[32 * w:32 * w + 32, t, (NL - 1) * 32:NL * 32], kin[:, h, c0:c0 + 32],
                                               q[:, h, c0:c0 + 32], start=True, stop=True)
                ins.then_inc(lev_done, 1)
                pe.wait_ge(kd_ok, h + 1)
                for half in range(2):
                    if half:
                        pe.wait_ge(kd_copied, 2 * h + 1)
                    for t in range(4):
                        c0 = (4 * half + t) * P
                        last = nc.tensor.transpose(k_ps[:, t * P:(t + 1) * P], kd[:, c0:c0 + P], g.ident)
                    last.then_inc(kd_turned, 1)
                pe.wait_ge(at_ok, h + 1)
                pe.wait_ge(qe_ok, h + 1)
                pe.wait_ge(kd_copied, 2 * h + 2)
                pe.wait_ge(v_in[h % 2], 16 * (h // 2 + 1))
                for t in range(NT):
                    ins = nc.tensor.matmul(win_ps[:, t, 0:P], kdT[:, t * P:(t + 1) * P], v[:, h % 2, t, :],
                                           start=True, stop=True)
                ins.then_inc(ds_done, 1)
                for t in range(NT):
                    if t == 0 and h >= 1:
                        pe.wait_ge(o_copied, 2 * h)
                    if t == 4:
                        pe.wait_ge(o_copied, 2 * h + 1)
                    col = (t % 4) * P
                    nc.tensor.matmul(o_ps[:, col:col + P], At[:, t * P:(t + 1) * P], v[:, h % 2, t, :], start=True, stop=False)
                    if t >= 1:
                        pe.wait_ge(s_ok, h * NT + t)
                    nc.tensor.matmul(o_ps[:, col:col + P], qe[:, t * P:(t + 1) * P], S[:, t, :], start=False, stop=True).then_inc(o_done, 1)
        stage.close()

        s_in, v_s_in, st_s_out = sem("rs_st_in"), sem("rs_v_in"), sem("rs_st_out")
        names = "zero d_ok e_ok m_ok lev_done win_ok at_ok kd_turned kd_copied kdm_ok ds_done s_ok o_done o_copied"
        (zero, d_ok, e_ok, m_ok, lev_done, win_ok, at_ok, kd_turned, kd_copied, kdm_ok, ds_done, s_ok, o_done,
         o_copied) = (sem("rs_" + n) for n in names.split())
        n_sl = len(SL) + 1
        W = H * ST
        wide = q[:, 0:2, :].rearrange("p h n -> p (h n)")
        st = kin[:, :, :].rearrange("p h n -> p (h n)").rearrange("p (b h d) -> p b h d", b=NB, h=H)
        kdm = B[:, :, :].rearrange("p h n -> p (h n)").rearrange("p (b n) -> p b n", b=NB)
        vs = x[:, 0, 0:SEC]
        kdt = x[:, 1, 0:SEC]
        qflat, kflat, bflat = (m[:, :, :].rearrange("p h n -> p (h n)") for m in (qs, ks, Bs))
        kend, qdec, ends = M[:, 0, W:2 * W], M[:, 1, W:2 * W], M[:, 2, W:W + H * NB]
        masks = g.cst[0:ST, C_WM + 32 * LEVELS.index(SL[0]):C_WM + 32 * LEVELS.index(SL[0]) + 32 * n_sl]
        stage = ExitStack()
        block = stage.enter_context(nc.Block())

        @block.sync
        def _(sp):
            sp.wait_ge(zero, 1)
            sp.dma_start(vs[0:ST, :], g.proj_d[SEQ:SEQ + ST, IA * SEC:(IA + 1) * SEC]).then_inc(v_s_in, 16)
            for b in range(NB):
                sp.dma_start(st[:, b, :, :], a["state_hgrn"].rearrange("l b h k v -> (l b) k h v")[b]).then_inc(s_in, 16)
            for b in range(NB):
                sp.wait_ge(s_ok, H * (b + 1))
                sp.dma_start(g.s_sample.rearrange("l b h k v -> (l b) k h v")[b], st[:, b, :, :]).then_inc(st_s_out, 16)
            sp.wait_ge(st_s_out, 16 * NB)

        @block.gpsimd
        def _(pool):
            nc.gpsimd.memset(vs, 0.0).then_inc(zero, 1)
            nc.gpsimd.memset(At[:, 0:W], 0.0).then_inc(zero, 1)
            nc.gpsimd.memset(wide, 0.0).then_inc(zero, 1)
            pool.wait_ge(zero, 3)
            nc.gpsimd.memset(kdm[ST:P, :, :], 0.0).then_inc(zero, 1)

        @block.scalar
        def _(act):
            for n, s in enumerate(SL):
                act.wait_ge(d_ok, n + 1)
                m = M[:, n, 0:W].rearrange("p (b s) -> p b s", s=2 * s)
                nc.scalar.activation(m[:, :, 0:s], m[:, :, 0:s], ACT.Exp, scale=-1.0)
                nc.scalar.activation(m[:, :, s:2 * s], m[:, :, s:2 * s], ACT.Exp).then_inc(e_ok, 1)
            act.wait_ge(d_ok, len(SL) + 1)
            nc.scalar.activation(kend, kend, ACT.Exp).then_inc(e_ok, 1)
            nc.scalar.activation(qdec, bflat, ACT.Exp).then_inc(e_ok, 1)
            nc.scalar.activation(ends, bflat.rearrange("p (b q) -> p b q", q=QS)[:, :, QS - 1], ACT.Exp).then_inc(e_ok, 1)
            act.wait_ge(kd_turned, 1)
            nc.scalar.activation(kdt[0:ST, :], k_ps[0:ST, :], ACT.Copy).then_inc(kd_copied, 1)
            act.wait_ge(o_done, 1)
            nc.scalar.activation(g.ot[0:ST, NT, :], o_ps[0:ST, :], ACT.Copy).then_inc(o_copied, 1)

        @block.vector
        def _(dve):
            own = g.dve
            for n, s in enumerate(SL):
                b = bflat.rearrange("p (b s) -> p b s", s=2 * s)
                nc.vector.tensor_tensor(M[:, n, 0:W].rearrange("p (b s) -> p b s", s=2 * s), b,
                                        spread(b[:, :, s - 1], 2, 2 * s), ALU.subtract).then_inc(d_ok, 1)
            b = bflat.rearrange("p (b q) -> p b q", q=QS)
            nc.vector.tensor_tensor(kend.rearrange("p (b q) -> p b q", q=QS), spread(b[:, :, QS - 1], 2, QS), b,
                                    ALU.subtract).then_inc(d_ok, 1)
            for n, s in enumerate(SL):
                dve.wait_ge(e_ok, n + 1)
                m, kk, qq = (z.rearrange("p (b s) -> p b s", s=2 * s) for z in (M[:, n, 0:W], kflat, qflat))
                nc.vector.tensor_tensor(m[:, :, 0:s], m[:, :, 0:s], kk[:, :, 0:s], ALU.mult)
                nc.vector.tensor_tensor(m[:, :, s:2 * s], m[:, :, s:2 * s], qq[:, :, s:2 * s], ALU.mult).then_inc(m_ok, 1)
            dve.wait_ge(e_ok, len(SL) + 3)
            nc.vector.tensor_tensor(kend, kend, kflat, ALU.mult).then_inc(m_ok, 1)
            dve.wait_ge(zero, 4)
            diagonal = bass.AP(wide.tensor, wide.offset, [list(wide.ap[0]), [NB * ST, H], [ST + QS, NB], [1, QS]])
            nc.vector.tensor_tensor(diagonal, qdec.rearrange("p (h b q) -> p h b q", h=H, q=QS),
                                    qflat.rearrange("p (h b q) -> p h b q", h=H, q=QS), ALU.mult).then_inc(m_ok, 1)
            dve.wait_ge(lev_done, 1)
            own.done(dve, nc.vector.tensor_tensor(wm[0:ST, 0:H, 0:32 * n_sl], win_ps[0:ST, 0:H, 0:32 * n_sl],
                                                  spread(masks, 1, H), ALU.mult))
            own.done(dve, nc.vector.tensor_reduce(
                ws[0:ST, 0:H, :], wm[0:ST, 0:H, 0:32 * n_sl].rearrange("p h (l c) -> p h c l", l=n_sl), AX.X, ALU.add))
            for w in range(2):
                rows = slice(32 * w, 32 * w + 32)
                ins = nc.vector.tensor_copy(At[rows, 0:W].rearrange("p (h n) -> p h n", h=H)[:, :, 32 * w:32 * w + 32],
                                            ws[rows, 0:H, :])
            ins.then_inc(at_ok, 1)
            dve.wait_ge(kd_copied, 1)
            nc.vector.tensor_tensor(kdm[0:ST, :, :], spread(kdt[0:ST, :], 1, NB),
                                    spread(g.cst[0:ST, C_BM:C_BM + NB], 2, SEC), ALU.mult).then_inc(kdm_ok, 1)
            dve.wait_ge(o_done, 1)
            for b in range(NB):
                dve.wait_ge(ds_done, b + 1)
                for h in range(H):
                    nc.vector.scalar_tensor_tensor(st[:, b, h, :], st[:, b, h, :], ends[:, h * NB + b:h * NB + b + 1],
                                                   dir_ps[:, (b % 2) * 512 + h * P:(b % 2) * 512 + (h + 1) * P],
                                                   ALU.mult, ALU.add).then_inc(s_ok, 1)

        @block.tensor
        def _(pe):
            for n in range(n_sl):
                if n < len(SL):
                    pe.wait_ge(m_ok, n + 1)
                for h in range(H):
                    for w in range(2):
                        c0 = h * ST + 32 * w
                        left, right = (M[:, n, c0:c0 + 32],) * 2 if n < len(SL) else (kflat[:, c0:c0 + 32], qflat[:, c0:c0 + 32])
                        ins = nc.tensor.matmul(win_ps[32 * w:32 * w + 32, h, 32 * n:32 * n + 32], left, right, start=True, stop=True)
            ins.then_inc(lev_done, 1)
            pe.wait_ge(m_ok, len(SL) + 1)
            for h in range(H):
                ins = nc.tensor.transpose(k_ps[0:ST, h * P:(h + 1) * P], kend[:, h * ST:(h + 1) * ST], g.ident)
            ins.then_inc(kd_turned, 1)
            pe.wait_ge(v_s_in, 16)
            pe.wait_ge(s_in, 16 * NB)
            pe.wait_ge(at_ok, 1)
            pe.wait_ge(m_ok, len(SL) + 2)
            for h in range(H):
                nc.tensor.matmul(o_ps[0:ST, h * P:(h + 1) * P], At[:, h * ST:(h + 1) * ST], vs[:, h * P:(h + 1) * P],
                                 start=True, stop=False)
                for b in range(NB):
                    c0 = (h * NB + b) * ST
                    ins = nc.tensor.matmul(o_ps[0:ST, h * P:(h + 1) * P], wide[:, c0:c0 + ST], st[:, b, h, :],
                                           start=False, stop=(b == NB - 1))
            ins.then_inc(o_done, 1)
            pe.wait_ge(kdm_ok, 1)
            for b in range(NB):
                if b >= 2:
                    pe.wait_ge(s_ok, H * (b - 1))
                for h in range(H):
                    ins = nc.tensor.matmul(dir_ps[:, (b % 2) * 512 + h * P:(b % 2) * 512 + (h + 1) * P],
                                           kdm[:, b, h * P:(h + 1) * P], vs[:, h * P:(h + 1) * P], start=True, stop=True)
                ins.then_inc(ds_done, 1)
        stage.close()


def output(nc, g):
    a = g.a
    x_p = a["x_prompt"].rearrange("a (t p) d -> (a t) p d", p=P)
    x_s = a["x_sample"].rearrange("b q d -> (b q) d")
    y_p = g.y_prompt.rearrange("a (t p) d -> (a t) p d", p=P)
    y_s = g.y_sample.rearrange("b q d -> (b q) d")
    w_out = a["w_out"].rearrange("l (k p) n -> (l p) k n", p=P)
    with ExitStack() as here:
        sb, pb = tensors(nc, here)
        sem = semaphores(nc, here)
        WH = sb("f_W", [P, KT_N // 2, DM])
        gz = sb("f_gz", [P, NT + 1, 2, SEC])
        sg = sb("f_sg", [P, NT + 1, 2, SEC])
        xr = sb("f_x", [P, 2, DM])
        y = sb("f_y", [P, 2, DM])
        junk = sb("f_junk", [P, H, P])
        ssq, lns, rs = sb("f_ssq", [P, (NT + 1) * H]), sb("f_ln", [P, H]), sb("f_rs", [P, (NT + 1) * H])
        gate = sb("f_gate", [P, 2, DM])
        p_ps = pb("f_ps", [P, 2, DM])
        t_ps = pb("f_tps", [P, 2, SEC])
        g_ps = pb("f_gps", [P, 2, SEC])
        z_in, w_in = [sem(f"oz_in{t}") for t in range(NT + 1)], sem("ow_in")
        x_in, y_out = [sem("ox_in0"), sem("ox_in1")], [sem("oy_out0"), sem("oy_out1")]
        names = "sg_ok gp_t gp_ok gated ss_ok rs_ok y_ok turned yT_ok done added"
        (sg_ok, gp_t, gp_ok, gated, ss_ok, rs_ok, y_ok, turned, yT_ok, done, added) = (sem("f_" + n) for n in names.split())
        block = here.enter_context(nc.Block())
        rows = [P] * NT + [ST]

        @block.sync
        def _(sp):
            for t, n in enumerate(rows):
                sp.dma_start(gz[0:n, t, :, :].rearrange("p a d -> p (a d)"),
                             g.proj_d[t * P:t * P + n, GA * SEC:(ZA + 1) * SEC]).then_inc(z_in[t], 16)
                if t == 2:
                    sp.dma_start(WH[:, :, :], w_out[:, 0:KT_N // 2, :]).then_inc(w_in, 16)
            for t, n in enumerate(rows):
                if t >= 2:
                    sp.wait_ge(added, t - 1)
                sp.dma_start(xr[0:n, t % 2, :], x_p[t] if t < NT else x_s).then_inc(x_in[t % 2], 16)
            for b in range(2):
                sp.wait_ge(y_out[b], 16 * ((NT + 2 - b) // 2))

        @block.gpsimd
        def _(pool):
            for t, n in enumerate(rows):
                pool.wait_ge(added, t + 1)
                pool.dma_start(y_p[t] if t < NT else y_s, y[0:n, t % 2, :]).then_inc(y_out[t % 2], 16)

        @block.scalar
        def _(act):
            for j in range(2):
                act.wait_ge(gp_t, j + 1)
                n = (P, ST)[j]
                nc.scalar.activation(gate[0:n, j, :], g_ps[0:n, :, :].rearrange("p a d -> p (a d)"), ACT.Copy).then_inc(gp_ok, 1)
            for t, n in enumerate(rows):
                act.wait_ge(z_in[t], 16)
                nc.scalar.activation(sg[0:n, t, :, :], gz[0:n, t, :, :], ACT.Sigmoid).then_inc(sg_ok, 1)
            for t, n in enumerate(rows):
                act.wait_ge(gated, t + 1)
                for h in range(H):
                    ins = nc.scalar.activation(junk[0:n, h, :], g.ot[0:n, t, h * P:(h + 1) * P], ACT.Square,
                                               accum_out=ssq[0:n, t * H + h:t * H + h + 1])
                ins.then_inc(ss_ok, 1)
                act.wait_ge(ss_ok, t + 1)
                g.act.done(act, nc.scalar.activation(lns[0:n, :], ssq[0:n, t * H:(t + 1) * H], ACT.Ln,
                                                     bias=g.epsc[0:n, :], scale=1.0 / P))
                nc.scalar.activation(rs[0:n, t * H:(t + 1) * H], lns[0:n, :], ACT.Exp, scale=-0.5).then_inc(rs_ok, 1)
                act.wait_ge(turned, t + 1)
                nc.scalar.activation(g.yT[:, 0:4, t * P:t * P + n],
                                     t_ps[:, t % 2, 0:H * n].rearrange("p (h t) -> p h t", h=H), ACT.Copy).then_inc(yT_ok, 1)

        @block.vector
        def _(dve):
            own = g.dve

            def gates(t, n):
                dve.wait_ge(sg_ok, t + 1)
                nc.vector.tensor_tensor(g.ot[0:n, t, :], g.ot[0:n, t, :], sg[0:n, t, 0, :], ALU.mult).then_inc(gated, 1)

            def branch(t, n):
                z, s = gz[0:n, t, 1, :], sg[0:n, t, 1, :]
                o = g.ot[0:n, t, :]
                own.done(dve, nc.vector.tensor_tensor(z, z, s, ALU.mult))
                own.done(dve, nc.vector.tensor_tensor(z.rearrange("p (h d) -> p h d", h=H), z.rearrange("p (h d) -> p h d", h=H),
                                                      spread(g.hgw[0:n, :], 1, H), ALU.mult))
                dve.wait_ge(rs_ok, t + 1)
                own.done(dve, nc.vector.tensor_tensor(o.rearrange("p (h d) -> p h d", h=H), o.rearrange("p (h d) -> p h d", h=H),
                                                      spread(rs[0:n, t * H:(t + 1) * H], 2, P), ALU.mult))
                nc.vector.tensor_tensor(o, o, z, ALU.mult).then_inc(y_ok, 1)

            def residual(t, n):
                if t == 0:
                    dve.wait_ge(gp_ok, 2)
                dve.wait_ge(done, t + 1)
                dve.wait_ge(x_in[t % 2], 16 * (t // 2 + 1))
                if t >= 2:
                    dve.wait_ge(y_out[t % 2], 16 * (t // 2))
                own.done(dve, nc.vector.tensor_tensor(y[0:n, t % 2, :], p_ps[0:n, t % 2, :], gate[0:n, t // NT, :], ALU.mult))
                nc.vector.tensor_tensor(y[0:n, t % 2, :], y[0:n, t % 2, :], xr[0:n, t % 2, :], ALU.add).then_inc(added, 1)

            gates(0, P)
            for t in range(NT + 2):
                if t + 1 <= NT:
                    gates(t + 1, rows[t + 1])
                if t <= NT:
                    branch(t, rows[t])
                if t >= 1:
                    residual(t - 1, rows[t - 1])

        @block.tensor
        def _(pe):
            for j, (c0, n) in enumerate(((C_GP, P), (C_GS, ST))):
                if j:
                    pe.wait_ge(gp_ok, 1)
                for half in range(2):
                    ins = nc.tensor.matmul(g_ps[0:n, half, :], g.cst[:, c0 + half * n:c0 + (half + 1) * n], g.mod[:, 1, :],
                                           start=True, stop=True)
                ins.then_inc(gp_t, 1)

            def turn(t, n):
                pe.wait_ge(y_ok, t + 1)
                if t >= 2:
                    pe.wait_ge(yT_ok, t - 1)
                for h in range(H):
                    ins = nc.tensor.transpose(t_ps[:, t % 2, h * n:(h + 1) * n], g.ot[0:n, t, h * P:(h + 1) * P], g.ident[0:n, 0:n])
                ins.then_inc(turned, 1)

            def attention_half(t, n):
                if t >= 2:
                    pe.wait_ge(added, t - 1)
                for n0 in range(2):
                    for k in range(4):
                        nc.tensor.matmul(p_ps[0:n, t % 2, n0 * 512:(n0 + 1) * 512], g.yT[:, 4 + k, t * P:t * P + n],
                                         g.WO[:, k, n0 * 512:(n0 + 1) * 512], start=(k == 0), stop=False)

            def hgrn_half(t, n):
                pe.wait_ge(yT_ok, t + 1)
                for n0 in range(2):
                    for k in range(4):
                        ins = nc.tensor.matmul(p_ps[0:n, t % 2, n0 * 512:(n0 + 1) * 512], g.yT[:, k, t * P:t * P + n],
                                               WH[:, k, n0 * 512:(n0 + 1) * 512], start=False, stop=(k == 3))
                ins.then_inc(done, 1)

            pe.wait_ge(g.wo_in, 16)
            attention_half(0, P)
            attention_half(1, P)
            turn(0, P)
            pe.wait_ge(w_in, 16)
            for t, n in enumerate(rows):
                hgrn_half(t, n)
                if t < NT:
                    turn(t + 1, rows[t + 1])
                    if t >= 1:
                        attention_half(t + 1, rows[t + 1])


def constants():
    c = np.zeros((P, C_N), np.float32)
    p = np.arange(P)
    c[p, C_ID + p] = 1
    j, i, q = p // 32, p % 32 // QS, p % QS
    for gr in range(2):
        for z in range(2):
            c[p, C_SL + gr * P + 32 * (2 * gr + j // 2) + 16 * z + 8 * (j % 2) + q] = 1
    used = p % 32 < 16
    for h in range(H):
        rows = p[used & (p // 32 == h)]
        c[rows, C_SZ + h * 120 + 56 + rows % QS] = 1
    t = np.arange(32)
    jj = (p % 32)[:, None]
    for n, s in enumerate(LEVELS):
        c[:, C_WM + 32 * n:C_WM + 32 * n + 32] = ((jj // (2 * s) == t // (2 * s)) & (jj % (2 * s) < s)
                                                  & (t % (2 * s) >= s))
    c[:, C_WM + 160:C_WM + 192] = jj == t
    for half in range(2):
        c[32 * half, C_GP + half * P:C_GP + half * P + P] = 1
        for b in range(NB):
            c[32 * half + 1 + b, C_GS + half * ST + QS * b:C_GS + half * ST + QS * b + QS] = 1
    for b in range(NB):
        c[QS * b:QS * b + QS, C_BM + b] = 1
    c[96, C_ONE:C_ONE + 9] = 1
    c[:, C_LC] = p % 16 < 8
    c[:, C_LC + 1] = p % 16 >= 8
    return c


def buckets():
    d = DMAX - np.arange(DTAB)
    pos = np.maximum(d, 1).astype(np.float32)
    large = 16 + (np.log(pos / np.float32(16)) / np.float32(np.log(64.0)) * np.float32(16)).astype(np.int32)
    b = np.where(d < 16, d, np.minimum(large, 31))
    b = np.where(d < 0, 32, b)
    return (np.arange(33)[:, None] == b).astype(np.float32)


def resets():
    n = np.arange(SEQ + ST)
    return np.where(n < SEQ, n % P, n % QS).astype(bool).astype(np.float32)[None, :]


OUTS = [(1, SEQ, DM), (NB, QS, DM), (1, 1, SEQ, H, P), (1, 1, SEQ, H, P), (1, 1, H, P, P),
        (1, NB, QS, H, P), (1, NB, QS, H, P), (1, NB, H, P, P)]


def build(nc, arrays):
    a = {n: nc.dram_tensor(n, x.shape, mybir.dt.from_np(x.dtype), kind="ExternalInput").ap()
         for n, x in arrays.items()}
    outs = [nc.dram_tensor(f"out_{i}", s, F32, kind="ExternalOutput").ap() for i, s in enumerate(OUTS)]
    layer(nc, a, outs)


def host_arrays(inputs):
    arrays = {n: np.ascontiguousarray(x) for n, x in inputs.items()}
    arrays["constants"] = constants()
    arrays["buckets"] = buckets()
    arrays["resets"] = resets()
    arrays["masked"] = np.full((1, H), NEG, np.float32)
    return arrays


def kernel(**inputs):
    import concourse.bacc as bacc
    from concourse.bass_utils import run_bass_kernel_spmd

    nc = bacc.Bacc("TRN2", target_bir_lowering=False, num_devices=1)
    arrays = host_arrays(inputs)
    build(nc, arrays)
    r = run_bass_kernel_spmd(nc, [arrays], core_ids=[0])
    return tuple(r.results[0][f"out_{i}"] for i in range(len(OUTS)))
```
